# Optimizing a Trainium2 kernel written in Bass

```python
import jax, jax.numpy as jnp
from jax import lax
import numpy as np

D_MODEL = 1024
BATCH = 1
SEQ = 512
DEPTH = 1
DEC_BATCH = 8
DEC_SEQ = 1
PAST_LEN = 4096
PAGE_SIZE = 128

CHUNK = 128
A_HEADS = 8
A_HEAD_DIM = D_MODEL // A_HEADS
A_WIDTH = A_HEADS * A_HEAD_DIM
B_HEAD_DIM = 64
B_HEADS = D_MODEL // B_HEAD_DIM
B_WIDTH = B_HEADS * B_HEAD_DIM
W_LORA = 64
A_LORA = 64
G_LORA = 128
SHIFT_WIDTH = 3 * B_WIDTH + W_LORA + A_LORA + G_LORA
OFF_U = 0
OFF_V = A_WIDTH
OFF_SHIFT = 2 * A_WIDTH
OFF_GATE_A = OFF_SHIFT + SHIFT_WIDTH
OFF_GATE_B = OFF_GATE_A + D_MODEL
IN_COLS = OFF_GATE_B + D_MODEL
N_GROUPS = 4
EXPERTS_PER_GROUP = 8
N_EXPERTS = N_GROUPS * EXPERTS_PER_GROUP
TOP_K = 2
D_EXPERT = 256
RMS_EPS = 1e-6
LN_EPS = 1e-5
GN_EPS = 64e-5

kernel_name = 'hybrid_sgu_rwkv7_hmoe_step'

def rms_norm(x, g):
    xf = x.astype(jnp.float32)
    y = xf * lax.rsqrt(jnp.mean(xf * xf, axis=-1, keepdims=True) + RMS_EPS)
    return (y * g.astype(jnp.float32)).astype(x.dtype)

def head_norm(x, w, b, eps):
    xf = x.astype(jnp.float32)
    mu = jnp.mean(xf, axis=-1, keepdims=True)
    xc = xf - mu
    var = jnp.mean(xc * xc, axis=-1, keepdims=True)
    y = xc * lax.rsqrt(var + eps) * w.astype(jnp.float32) + b.astype(jnp.float32)
    return y.astype(x.dtype)

def spatial_gating(v, w_s, b_s):
    bsz, t_len = v.shape[0], v.shape[1]
    n_chunks = -(-t_len // CHUNK)
    pad = n_chunks * CHUNK - t_len
    vp = jnp.pad(v, ((0, 0), (0, pad), (0, 0), (0, 0))).reshape(bsz, n_chunks, CHUNK, A_HEADS, A_HEAD_DIM)
    causal = jnp.tril(jnp.ones((CHUNK, CHUNK), dtype=bool))
    w_c = jnp.where(causal[None], w_s, 0.0)
    s = jnp.einsum('hts,bcshn->bcthn', w_c, vp) + jnp.transpose(b_s)[None, None, :, :, None]
    return s.reshape(bsz, n_chunks * CHUNK, A_HEADS, A_HEAD_DIM)[:, :t_len]

def wkv7_scan(s0, r, w, k, v, a, b):
    def step(s, inp):
        r_t, w_t, k_t, v_t, a_t, b_t = inp
        sa = jnp.einsum('bhij,bhj->bhi', s, a_t)
        s = s * w_t[:, :, None, :] + sa[..., :, None] * b_t[..., None, :] + v_t[..., :, None] * k_t[..., None, :]
        y = jnp.einsum('bhij,bhj->bhi', s, r_t)
        return s, y
    xs = (jnp.moveaxis(r, 1, 0), jnp.moveaxis(w, 1, 0), jnp.moveaxis(k, 1, 0),
          jnp.moveaxis(v, 1, 0), jnp.moveaxis(a, 1, 0), jnp.moveaxis(b, 1, 0))
    s_last, ys = lax.scan(step, s0, xs)
    return jnp.moveaxis(ys, 0, 1), s_last

def token_mixers(xn, wkv0, shift0, w_in, sgu_ln_w, sgu_ln_b, sgu_w_s, sgu_b, rwkv_mu,
                 w_lora_up, w_bias, a_lora_up, a_bias, g_lora_up, k_k, k_a, r_k,
                 lnx_w, lnx_b, proj_a, proj_b, w_out):
    bsz, t_len = xn.shape[0], xn.shape[1]
    f32 = jnp.float32
    proj = jnp.einsum('btd,dc->btc', xn, w_in)
    u = jax.nn.gelu(proj[..., OFF_U:OFF_V])
    v = jax.nn.gelu(proj[..., OFF_V:OFF_SHIFT]).reshape(bsz, t_len, A_HEADS, A_HEAD_DIM)
    cols = proj[..., OFF_SHIFT:OFF_GATE_A]
    gate_a = jax.nn.sigmoid(proj[..., OFF_GATE_A:OFF_GATE_B])
    gate_b = jax.nn.sigmoid(proj[..., OFF_GATE_B:IN_COLS])

    v_n = head_norm(v, sgu_ln_w, sgu_ln_b, LN_EPS)
    y_a = u * spatial_gating(v_n, sgu_w_s, sgu_b).reshape(bsz, t_len, A_WIDTH)

    prev = jnp.concatenate([shift0[:, None, :].astype(cols.dtype), cols[:, :-1]], axis=1)
    xs = cols + (prev - cols) * rwkv_mu
    o = 3 * B_WIDTH
    r = xs[..., 0:B_WIDTH]
    k = xs[..., B_WIDTH:2 * B_WIDTH]
    vb = xs[..., 2 * B_WIDTH:o]
    w_d = xs[..., o:o + W_LORA]
    a_d = xs[..., o + W_LORA:o + W_LORA + A_LORA]
    g_d = xs[..., o + W_LORA + A_LORA:SHIFT_WIDTH]
    w_log = -jax.nn.softplus(-(w_bias + jnp.tanh(w_d) @ w_lora_up)) - 0.5
    decay = jnp.exp(-jnp.exp(w_log.astype(f32)))
    a = jax.nn.sigmoid(a_bias + a_d @ a_lora_up)
    g = jax.nn.sigmoid(g_d) @ g_lora_up
    hs = (bsz, t_len, B_HEADS, B_HEAD_DIM)
    kk = (k * k_k).astype(f32).reshape(hs)
    kk = kk / jnp.maximum(jnp.sqrt(jnp.sum(kk * kk, axis=-1, keepdims=True)), 1e-12)
    k = k * (1.0 + (a - 1.0) * k_a)
    r_h = r.astype(f32).reshape(hs)
    k_h = k.astype(f32).reshape(hs)
    v_h = vb.astype(f32).reshape(hs)
    a_h = a.astype(f32).reshape(hs)
    y, wkv_new = wkv7_scan(wkv0.astype(f32), r_h, decay.reshape(hs), k_h, v_h, -kk, kk * a_h)
    y = head_norm(y, lnx_w, lnx_b, GN_EPS)
    bonus = jnp.sum(r_h * k_h * r_k.astype(f32), axis=-1, keepdims=True) * v_h
    y_b = (y + bonus).astype(xn.dtype).reshape(bsz, t_len, B_WIDTH) * g

    merged = gate_a * (y_a @ proj_a) + gate_b * (y_b @ proj_b)
    out = merged @ w_out
    return out, wkv_new.astype(wkv0.dtype), cols[:, -1], v_n

def hier_moe(x2d, router_group, router_group_bias, router_expert, router_expert_bias,
             moe_w_gate, moe_w_up, moe_w_down):
    f32 = jnp.float32
    lg = (x2d @ router_group + router_group_bias).astype(f32)
    grp = jnp.argmax(lg, axis=-1)
    p_grp = jnp.max(jax.nn.softmax(lg, axis=-1), axis=-1, keepdims=True)
    le = (x2d @ router_expert + router_expert_bias).astype(f32).reshape(-1, N_GROUPS, EXPERTS_PER_GROUP)
    le_g = jnp.einsum('tg,tge->te', jax.nn.one_hot(grp, N_GROUPS, dtype=f32), le)
    top_v, top_i = lax.top_k(le_g, TOP_K)
    weights = p_grp * jax.nn.softmax(top_v, axis=-1)
    eid = grp[:, None] * EXPERTS_PER_GROUP + top_i
    combine = jnp.sum(jax.nn.one_hot(eid, N_EXPERTS, dtype=f32) * weights[..., None], axis=1).astype(x2d.dtype)
    y = jnp.zeros_like(x2d)
    for e in range(N_EXPERTS):
        h = jax.nn.silu(x2d @ moe_w_gate[e]) * (x2d @ moe_w_up[e])
        y = y + combine[:, e:e + 1] * (h @ moe_w_down[e])
    return y

def setup_inputs(seed: int = 0) -> dict:
    key = jax.random.key(seed)
    ks = iter(jax.random.split(key, 40))
    nrm = lambda shape, scale: scale * jax.random.normal(next(ks), shape, jnp.float32)
    L = DEPTH
    decay_speed = jnp.tile(jnp.linspace(-6.5, -1.5, B_WIDTH, dtype=jnp.float32)[None], (L, 1))
    return {
        'x_prompt': nrm((BATCH, SEQ, D_MODEL), 1.0),
        'x_sample': nrm((DEC_BATCH, DEC_SEQ, D_MODEL), 1.0),
        'state_wkv': nrm((L, DEC_BATCH, B_HEADS, B_HEAD_DIM, B_HEAD_DIM), 0.5),
        'state_shift': nrm((L, DEC_BATCH, SHIFT_WIDTH), 1.0),
        'norm_mix_w': 1.0 + nrm((L, D_MODEL), 0.05),
        'w_in': nrm((L, D_MODEL, IN_COLS), D_MODEL ** -0.5),
        'sgu_ln_w': 1.0 + nrm((L, A_HEADS, A_HEAD_DIM), 0.05),
        'sgu_ln_b': nrm((L, A_HEADS, A_HEAD_DIM), 0.01),
        'sgu_w_s': nrm((L, A_HEADS, CHUNK, CHUNK), 0.5 * CHUNK ** -0.5),
        'sgu_b': 1.0 + nrm((L, A_HEADS, CHUNK), 0.05),
        'rwkv_mu': jax.random.uniform(next(ks), (L, SHIFT_WIDTH), jnp.float32),
        'w_lora_up': nrm((L, W_LORA, B_WIDTH), 0.5 * W_LORA ** -0.5),
        'w_bias': decay_speed + nrm((L, B_WIDTH), 0.1),
        'a_lora_up': nrm((L, A_LORA, B_WIDTH), 0.5 * A_LORA ** -0.5),
        'a_bias': nrm((L, B_WIDTH), 0.1),
        'g_lora_up': nrm((L, G_LORA, B_WIDTH), G_LORA ** -0.5),
        'k_k': 0.85 + nrm((L, B_WIDTH), 0.05),
        'k_a': 1.0 + nrm((L, B_WIDTH), 0.05),
        'r_k': nrm((L, B_HEADS, B_HEAD_DIM), 0.1),
        'lnx_w': 1.0 + nrm((L, B_HEADS, B_HEAD_DIM), 0.05),
        'lnx_b': nrm((L, B_HEADS, B_HEAD_DIM), 0.01),
        'proj_a': nrm((L, A_WIDTH, D_MODEL), A_WIDTH ** -0.5),
        'proj_b': nrm((L, B_WIDTH, D_MODEL), B_WIDTH ** -0.5),
        'w_out': nrm((L, D_MODEL, D_MODEL), D_MODEL ** -0.5),
        'norm_ffn_w': 1.0 + nrm((L, D_MODEL), 0.05),
        'router_group': nrm((L, D_MODEL, N_GROUPS), D_MODEL ** -0.5),
        'router_group_bias': nrm((L, N_GROUPS), 0.01),
        'router_expert': nrm((L, D_MODEL, N_EXPERTS), D_MODEL ** -0.5),
        'router_expert_bias': nrm((L, N_EXPERTS), 0.01),
        'moe_w_gate': nrm((L, N_EXPERTS, D_MODEL, D_EXPERT), D_MODEL ** -0.5),
        'moe_w_up': nrm((L, N_EXPERTS, D_MODEL, D_EXPERT), D_MODEL ** -0.5),
        'moe_w_down': nrm((L, N_EXPERTS, D_EXPERT, D_MODEL), D_EXPERT ** -0.5),
        'norm_final_w': 1.0 + nrm((D_MODEL,), 0.05),
    }

def reference(x_prompt, x_sample, state_wkv, state_shift, norm_mix_w, w_in, sgu_ln_w, sgu_ln_b,
              sgu_w_s, sgu_b, rwkv_mu, w_lora_up, w_bias, a_lora_up, a_bias, g_lora_up, k_k, k_a,
              r_k, lnx_w, lnx_b, proj_a, proj_b, w_out, norm_ffn_w, router_group, router_group_bias,
              router_expert, router_expert_bias, moe_w_gate, moe_w_up, moe_w_down, norm_final_w):
    xp, xs = x_prompt, x_sample
    bp, tp = xp.shape[0], xp.shape[1]
    n_prompt_tokens = bp * tp
    wkv_p_list, shift_p_list, wkv_s_list, shift_s_list, v_s_list = [], [], [], [], []
    for l in range(DEPTH):
        mix_w = (w_in[l], sgu_ln_w[l], sgu_ln_b[l], sgu_w_s[l], sgu_b[l], rwkv_mu[l], w_lora_up[l],
                 w_bias[l], a_lora_up[l], a_bias[l], g_lora_up[l], k_k[l], k_a[l], r_k[l],
                 lnx_w[l], lnx_b[l], proj_a[l], proj_b[l], w_out[l])
        wkv0_p = jnp.zeros((bp, B_HEADS, B_HEAD_DIM, B_HEAD_DIM), xp.dtype)
        shift0_p = jnp.zeros((bp, SHIFT_WIDTH), xp.dtype)
        out_p, wkv_p, shift_p, _ = token_mixers(rms_norm(xp, norm_mix_w[l]), wkv0_p, shift0_p, *mix_w)
        out_s, wkv_s, shift_s, v_s = token_mixers(rms_norm(xs, norm_mix_w[l]), state_wkv[l], state_shift[l], *mix_w)
        xp = xp + out_p
        xs = xs + out_s
        tokens = jnp.concatenate([rms_norm(xp, norm_ffn_w[l]).reshape(-1, D_MODEL),
                                  rms_norm(xs, norm_ffn_w[l]).reshape(-1, D_MODEL)], axis=0)
        f = hier_moe(tokens, router_group[l], router_group_bias[l], router_expert[l],
                     router_expert_bias[l], moe_w_gate[l], moe_w_up[l], moe_w_down[l])
        xp = xp + f[:n_prompt_tokens].reshape(xp.shape)
        xs = xs + f[n_prompt_tokens:].reshape(xs.shape)
        wkv_p_list.append(wkv_p)
        shift_p_list.append(shift_p)
        wkv_s_list.append(wkv_s)
        shift_s_list.append(shift_s)
        v_s_list.append(v_s)
    y_prompt = rms_norm(xp, norm_final_w)
    y_sample = rms_norm(xs, norm_final_w)
    return (y_prompt, y_sample, jnp.stack(wkv_p_list), jnp.stack(shift_p_list),
            jnp.stack(wkv_s_list), jnp.stack(shift_s_list), jnp.stack(v_s_list))


_drawn_inputs = setup_inputs


def setup_inputs(seed=0):
    import zlib

    import numpy as np

    out = dict(_drawn_inputs(seed))
    spreads = {}
    factors = {'sgu_ln_b': 5.736,
     'w_lora_up': 3.339,
     'lnx_w': 2.685,
     'lnx_b': 6.945,
     'router_group_bias': 13.921,
     'router_expert_bias': 3.963}
    for name, (base, spread) in spreads.items():
        noise = np.random.default_rng([zlib.crc32(name.encode()), seed]).standard_normal(out[name].shape)
        drawn = base * np.exp(spread * noise) if base else spread * noise
        out[name] = __import__('jax').numpy.asarray(drawn.astype(out[name].dtype))
    for name, factor in factors.items():
        out[name] = (out[name] * factor).astype(out[name].dtype)
    return out
```

```python
import math
from contextlib import ExitStack

import concourse.bass as bass
from concourse import mybir

F32 = mybir.dt.float32
I32 = mybir.dt.int32
ALU = mybir.AluOpType
ACT = mybir.ActivationFunctionType
AX = mybir.AxisListType

P = 128
D = 1024
NK = D // P
TP = 512
TS = 8
T = TP + TS
TH = T // 2
NT = TP // P
HD = 64
NP = D // P
CH = 64
NC = TP // CH
G = 2
GP = NP // G
LEVELS = (2, 4, 8, 16, 32)
OFF_V = D
OFF_SHIFT = 2 * D
SHIFT = 3 * D + 256
NSH = SHIFT // P
OFF_GA = OFF_SHIFT + SHIFT
OFF_GB = OFF_GA + D
NE = 32
NG = 4
EG = NE // NG
DE = 256
CAP = P
ROUNDS = -(-T // CAP)
DECAY = -math.exp(-0.5)
RMS_EPS, LN_EPS, GN_EPS = 1e-6, 1e-5, 64e-5

VEC_NAMES = ("norm_mix_w", "w_bias", "a_bias", "k_k", "k_a", "r_k", "lnx_w", "lnx_b", "norm_ffn_w", "rwkv_mu")
VEC = {name: (n * NP, NSH if name == "rwkv_mu" else NP) for n, name in enumerate(VEC_NAMES)}
NVEC = (len(VEC_NAMES) - 1) * NP + NSH


class Steps:

    def __init__(self, eng, sem, base=0):
        self.eng, self.sem, self.n, self.base = eng, sem, 0, base

    def did(self, ins):
        ins.then_inc(self.sem, 1)
        self.n += 1

    def wait(self):
        self.eng.wait_ge(self.sem, self.base + self.n)


def halves(ap):
    return ap[:, :, 0:TH]


def split(ap):
    return ap.rearrange("p (a t) -> p a t", a=2)


def vec(m, name):
    start, rows = VEC[name]
    return m.vecs[:, start:start + rows]


def open_phase(nc):
    ctx, sems = ExitStack(), []

    def sem(name):
        sems.append(nc.alloc_semaphore(name))
        return sems[-1]

    def close():
        nc.clear_and_free_semaphores(sems)
        nc.all_engine_barrier()

    ctx.callback(close)
    return ctx, (lambda n, s, d=F32: ctx.enter_context(nc.sbuf_tensor(n, s, d))), \
        (lambda n, s, d=F32: ctx.enter_context(nc.psum_tensor(n, s, d))), sem


def phase_constants(nc, m):
    ctx, sb, ps, sem = open_phase(nc)
    with ctx:
        s_set = sem("c_set")
        s_zero = sem("c_zero")
        block = ctx.enter_context(nc.Block())

        @block.gpsimd
        def _(eng):
            step = Steps(eng, s_set)

            def select(view, op, base, pattern, cm, fill):
                step.wait()
                step.did(eng.affine_select(out=view, in_=view, compare_op=op, fill=fill, base=base,
                                           pattern=pattern, channel_multiplier=cm))

            step.did(eng.memset(m.ident[:, :], 0.0))
            step.did(eng.memset(m.levels[:, :, :], 0.0))
            step.did(eng.memset(m.level1t[:, :], 0.0))
            step.did(eng.memset(m.headones[:, :], 0.0))
            step.did(eng.memset(m.below[:, :], 1.0))
            step.did(eng.memset(m.ones[:, :], 1.0))
            step.did(eng.memset(m.causal[:, :], 1.0))
            select(m.ident[:, :], ALU.not_equal, 0, [[-1, P]], 1, 1.0)
            step.wait()
            step.did(eng.memset(m.headones[0:HD, 0:HD], 1.0))
            step.did(eng.memset(m.headones[HD:P, HD:P], 1.0))
            select(m.below[:, :], ALU.is_gt, 0, [[1, P]], -1, 0.0)
            for half in range(2):
                rows = m.causal[HD * half:HD * (half + 1), :]
                select(rows[:, 0:CH], ALU.is_gt, 0, [[1, CH]], -1, 0.0)
                select(rows[:, CH:P], ALU.is_ge, 0, [[1, CH]], -1, 0.0)
            for n, b in enumerate((1,) + LEVELS):
                odd = m.levels[:, n, :].rearrange("p (a two b) -> p a two b", two=2, b=b)[:, :, 1, :]
                step.wait()
                step.did(eng.memset(odd, 1.0))
                select(odd, ALU.is_ge, 0, [[-2 * b, P // (2 * b)], [0, b]], 1, 0.0)
                select(odd, ALU.is_ge, b - 1, [[2 * b, P // (2 * b)], [0, b]], -1, 0.0)
                select(m.levels[:, n, :], ALU.not_equal, 0, [[-1, P]], 1, 1.0)
            even = m.level1t[:, :].rearrange("p (a two) -> p a two", two=2)[:, :, 0]
            select(even, ALU.not_equal, -1, [[-2, P // 2]], 1, 1.0)
            select(m.level1t[:, :], ALU.not_equal, 0, [[-1, P]], 1, 1.0)
            step.wait()


def phase_tokens(nc, m, a):
    ctx, sb, ps, sem = open_phase(nc)
    with ctx:
        x = sb("x_tok", [P, NT + 1, D])
        sq = sb("x_sq", [P, D])
        rows = sb("vec_rows", [P, P])
        shift_rows = sb("shift_rows", [TS, SHIFT])
        ms = sb("x_ms", [P, NT + 1])
        psx = ps("ps_x", [P, 4, 512])
        psv = ps("ps_v", [P, 512])
        pss = ps("ps_s", [P, 512])
        s_x = [sem(f"t_x{j}") for j in range(NT + 1)]
        s_vec, s_shift, s_sq, s_ms, s_rstd, s_ln, s_scaled, s_xt, s_xe, s_zero = \
            (sem("t_" + n) for n in ("vec", "shift", "sq", "ms", "rstd", "ln", "scaled", "xt", "xe", "zero"))
        s_vt, s_ve, s_st, s_se = (sem("t_" + n) for n in ("vt", "ve", "st", "se"))
        block = ctx.enter_context(nc.Block())

        @block.sync
        def _(eng):
            for j in range(NT):
                eng.dma_start(x[:, j, :], a["x_prompt"][0, j * P:(j + 1) * P, :]).then_inc(s_x[j], 16)
            eng.dma_start(x[0:TS, NT, :], a["x_sample"][:, 0, :]).then_inc(s_x[NT], 16)

        @block.scalar
        def _(eng):
            for name, (start, n) in VEC.items():
                ap = m.flat[name]
                eng.dma_start(rows[start:start + n, :], ap.rearrange("(r c) -> r c", c=P)).then_inc(s_vec, 16)
            eng.dma_start(shift_rows[:, :], a["state_shift"][0]).then_inc(s_shift, 16)
            eng.wait_ge(s_zero, 1)
            for j in range(NT + 1):
                n = P if j < NT else TS
                eng.wait_ge(s_x[j], 16)
                if j:
                    eng.wait_ge(s_sq, j)
                eng.activation(sq[0:n, :], x[0:n, j, :], ACT.Square, accum_out=ms[0:n, j:j + 1]).then_inc(s_sq, 1)
            eng.wait_ge(s_ms, 1)
            eng.activation(ms[:, :], ms[:, :], ACT.Ln).then_inc(s_ln, 1)
            eng.wait_ge(s_ln, 1)
            eng.activation(ms[:, :], ms[:, :], ACT.Exp, scale=-0.5).then_inc(s_rstd, 1)

        @block.vector
        def _(eng):
            eng.memset(ms[:, :], 1.0).then_inc(s_zero, 1)
            eng.wait_ge(s_vt, 1)
            eng.tensor_copy(m.vecs[:, :], psv[:, 0:NVEC]).then_inc(s_ve, 1)
            eng.wait_ge(s_st, 1)
            eng.tensor_copy(m.shift_prev[:, :, :], pss[:, 0:NSH * TS].rearrange("p (c t) -> p c t", t=TS)).then_inc(s_se, 1)
            eng.wait_ge(s_sq, NT + 1)
            eng.tensor_scalar(ms[:, :], ms[:, :], 1.0 / D, RMS_EPS, ALU.mult, ALU.add).then_inc(s_ms, 1)
            eng.wait_ge(s_rstd, 1)
            for j in range(NT + 1):
                n = P if j < NT else TS
                eng.tensor_scalar(x[0:n, j, :], x[0:n, j, :], ms[0:n, j:j + 1], None, ALU.mult).then_inc(s_scaled, 1)
            eng.wait_ge(s_ve, 1)
            for j in range(NT + 1):
                n = P if j < NT else TS
                for h in range(2):
                    eng.wait_ge(s_xt, 2 * j + h + 1)
                    w = vec(m, "norm_mix_w")[:, 4 * h:4 * h + 4].unsqueeze(2).to_broadcast([P, 4, n])
                    src = psx[:, 2 * (j % 2) + h, 0:4 * n].rearrange("p (k t) -> p k t", t=n)
                    eng.tensor_tensor(m.xT[:, 4 * h:4 * h + 4, j * P:j * P + n], src, w, ALU.mult).then_inc(s_xe, 1)

        @block.tensor
        def _(eng):
            eng.wait_ge(s_vec, 16 * len(VEC))
            eng.transpose(psv[:, 0:NVEC], rows[0:NVEC, :], m.ident[0:NVEC, 0:NVEC]).then_inc(s_vt, 1)
            eng.wait_ge(s_shift, 16)
            for c in range(NSH):
                last = eng.transpose(pss[:, c * TS:(c + 1) * TS], shift_rows[:, c * P:(c + 1) * P], m.ident[0:TS, 0:TS])
            last.then_inc(s_st, 1)
            for j in range(NT + 1):
                n = P if j < NT else TS
                eng.wait_ge(s_scaled, j + 1)
                for h in range(2):
                    if j >= 2:
                        eng.wait_ge(s_xe, 2 * (j - 2) + h + 1)
                    for k in range(4):
                        kk = 4 * h + k
                        last = eng.transpose(psx[:, 2 * (j % 2) + h, k * n:(k + 1) * n], x[0:n, j, kk * P:(kk + 1) * P],
                                             m.ident[0:n, 0:n])
                    last.then_inc(s_xt, 1)


def shift_mix(eng, step, m, cols, diff, out, mu, prev):
    step.did(eng.tensor_tensor(diff[:, 0:TP], cols[:, 0:TP], cols[:, 1:TP + 1], ALU.subtract))
    step.did(eng.tensor_tensor(diff[:, TP:T], prev, cols[:, TP + 1:T + 1], ALU.subtract))
    step.wait()
    step.did(eng.scalar_tensor_tensor(out=out, in0=diff[:, :], scalar=mu, in1=cols[:, 1:T + 1],
                                      op0=ALU.mult, op1=ALU.add))
    step.wait()


def project(eng, out, weights, xT):
    for h in range(2):
        for k in range(NK):
            last = eng.matmul(out[:, h, 0:TH], weights[:, k, :], xT[:, k, h * TH:(h + 1) * TH],
                              start=(k == 0), stop=(k == NK - 1))
    return last


def w_cols(w_in, at):
    return w_in[0, :, at].rearrange("(k p) c -> p k c", p=P)


def phase_lora_inputs(nc, m, a):
    ctx, sb, ps, sem = open_phase(nc)
    with ctx:
        w = sb("lw_w", [P, 2, NK, P])
        diff = sb("lw_diff", [P, T])
        xs = sb("lw_xs", [P, 2, T])
        cols = sb("lw_cols", [P, 2, T + 1])
        psp = ps("lw_ps", [P, 2, 2, 512])
        s_w = [sem("l_w0"), sem("l_w1")]
        s_p, s_e, s_zero, s_step, s_xs, s_t = (sem("l_" + n) for n in ("p", "e", "zero", "step", "xs", "t"))
        block = ctx.enter_context(nc.Block())

        @block.sync
        def _(eng):
            for n in range(2):
                at = OFF_SHIFT + 3 * D + n * P
                eng.dma_start(w[:, n], w_cols(a["w_in"], slice(at, at + P))).then_inc(s_w[n], 16)

        @block.tensor
        def _(eng):
            for n in range(2):
                eng.wait_ge(s_w[n], 16)
                project(eng, psp[:, n], w[:, n], m.xT).then_inc(s_p, 1)

        @block.scalar
        def _(eng):
            for n in range(2):
                eng.wait_ge(s_p, n + 1)
                eng.activation(split(cols[:, n, 1:T + 1]), halves(psp[:, n]), ACT.Copy).then_inc(s_e, 1)
            eng.wait_ge(s_xs, 1)
            eng.activation(m.lora_in[0:HD, :], xs[0:HD, 0, :], ACT.Tanh)
            eng.activation(m.lora_in[HD:P, :], xs[HD:P, 0, :], ACT.Copy)
            eng.wait_ge(s_xs, 2)
            eng.activation(m.gate_in[:, :], xs[:, 1, :], ACT.Tanh, scale=0.5).then_inc(s_t, 1)

        @block.vector
        def _(eng):
            step = Steps(eng, s_step)
            step.did(eng.memset(cols[:, :, 0:1], 0.0))
            step.did(eng.tensor_scalar(m.half_bias[:, 0, :], vec(m, "w_bias"), 0.5, None, ALU.mult))
            step.did(eng.tensor_scalar(m.half_bias[:, 1, :], vec(m, "a_bias"), 0.5, None, ALU.mult))
            step.wait()
            for n in range(2):
                eng.wait_ge(s_e, n + 1)
                c = 3 * NP + n
                shift_mix(eng, step, m, cols[:, n], diff, xs[:, n, :], vec(m, "rwkv_mu")[:, c:c + 1], m.shift_prev[:, c, :])
                step.did(eng.tensor_copy(m.shift_last[:, :, c], cols[:, n, TP:T + 1]))
                step.wait()
                eng.sem_inc(s_xs, 1)
            eng.wait_ge(s_t, 1)
            step.did(eng.tensor_scalar(m.gate_in[:, :], m.gate_in[:, :], 0.5, 0.5, ALU.mult, ALU.add))


def phase_rkv(nc, m, a):
    ctx, sb, ps, sem = open_phase(nc)
    with ctx:
        w = sb("rk_w", [P, 2, 3, NK, P])
        lw = sb("rk_lw", [P, 2, P])
        cols = [sb(f"rk_cols{j}", [P, T + 1]) for j in range(3)]
        diff = sb("rk_diff", [P, T])
        rate = sb("rk_rate", [P, T])
        tw = sb("rk_tw", [P, T])
        ta = sb("rk_ta", [P, T])
        kk2 = sb("rk_kk2", [P, T])
        rkk = sb("rk_rkk", [P, T])
        carry = sb("rk_carry", [P, NC, CH + 1])
        psp = [ps(f"rk_ps{n}", [P, 2, 512]) for n in range(2)]
        psz = ps("rk_psz", [P, 2, 512])
        pss = ps("rk_pss", [P, 2, 512])
        s_w = [sem("r_w0"), sem("r_w1")]
        names = ("step", "proj", "cols", "zw", "za", "tw", "ta", "ss", "bo", "ss_read", "bo_read",
                 "kk", "kk2", "rkk", "r_used", "k_used", "v_used", "lw_used", "rate_used", "init", "norm", "ln", "rn")
        (s_step, s_proj, s_cols, s_zw, s_za, s_tw, s_ta, s_ss, s_bo, s_ss_read, s_bo_read, s_kk, s_kk2,
         s_rkk, s_r_used, s_k_used, s_v_used, s_lw_used, s_rate_used, s_init, s_norm, s_ln, s_rn) = \
            (sem("r_" + n) for n in names)
        used = [s_r_used, s_k_used, s_v_used]
        block = ctx.enter_context(nc.Block())
        @block.sync
        def _(eng):
            def load(slot, pair):
                for j in range(3):
                    eng.dma_start(w[:, slot, j], w_cols(a["w_in"], bass.ds(pair * P + (OFF_SHIFT + j * D), P)))\
                       .then_inc(s_w[slot], 16)
                eng.dma_start(lw[0:HD, slot, :], a["w_lora_up"][0, :, bass.ds(pair * P, P)]).then_inc(s_w[slot], 16)
                eng.dma_start(lw[HD:P, slot, :], a["a_lora_up"][0, :, bass.ds(pair * P, P)]).then_inc(s_w[slot], 16)

            for slot in range(2):
                load(slot, slot)
            with eng.Fori(1, NP // 2) as i:
                for slot in range(2):
                    eng.wait_ge(s_proj, i * 6 + (3 * slot - 3))
                    load(slot, i * 2 + slot)

        @block.tensor
        def _(eng):
            with eng.Fori(0, NP // 2) as i:
                for h in range(2):
                    def proj(j):
                        n = 3 * h + j
                        eng.wait_ge(s_cols, i * 6 + (n + 1))
                        project(eng, psp[n % 2], w[:, h, j], m.xT).then_inc(s_proj, 1)

                    def z(rows, s_out, s_free, v):
                        eng.wait_ge(s_free, i * 2 + v)
                        for half in range(2):
                            last = eng.matmul(psz[:, half, 0:TH], lw[rows, h, :], m.lora_in[rows, half * TH:(half + 1) * TH],
                                              start=True, stop=True)
                        last.then_inc(s_out, 1)

                    eng.wait_ge(s_w[h], i * 80 + 80)
                    proj(0)
                    z(slice(0, HD), s_zw, s_bo_read, h + 1)
                    proj(1)
                    z(slice(HD, P), s_za, s_tw, h + 1)
                    proj(2)
                    eng.wait_ge(s_kk2, i * 2 + h + 1)
                    eng.wait_ge(s_ss_read, i * 2 + h + 1)
                    for half in range(2):
                        last = eng.matmul(pss[:, half, 0:TH], m.headones[:, :], kk2[:, half * TH:(half + 1) * TH],
                                          start=True, stop=True)
                    last.then_inc(s_ss, 1)
                    eng.wait_ge(s_rkk, i * 2 + h + 1)
                    eng.wait_ge(s_ta, i * 2 + h + 1)
                    for half in range(2):
                        last = eng.matmul(psz[:, half, 0:TH], m.headones[:, :], rkk[:, half * TH:(half + 1) * TH],
                                          start=True, stop=True)
                    last.then_inc(s_bo, 1)

        @block.scalar
        def _(eng):
            eng.sem_inc(s_cols, 2)
            with eng.Fori(0, NP // 2) as i:
                for h in range(2):
                    def copy_cols(j):
                        eng.wait_ge(s_proj, i * 6 + (3 * h + j + 1))
                        eng.wait_ge(used[j], i * 2 + h + 1)
                        eng.activation(split(cols[j][:, 1:T + 1]), halves(psp[(3 * h + j) % 2]), ACT.Copy).then_inc(s_cols, 1)

                    def half_tanh(out, sem_in, free, bias, sem_out):
                        eng.wait_ge(sem_in, i * 2 + h + 1)
                        eng.wait_ge(free, i * 2 + h + 1)
                        eng.activation(split(out[:, :]), halves(psz), ACT.Tanh, scale=0.5,
                                       bias=m.half_bias[:, bias, bass.ds(i * 2 + h, 1)]).then_inc(sem_out, 1)

                    copy_cols(0)
                    half_tanh(tw, s_zw, s_lw_used, 0, s_tw)
                    copy_cols(1)
                    half_tanh(ta, s_za, s_rate_used, 1, s_ta)
                    eng.wait_ge(s_kk, i * 2 + h + 1)
                    eng.activation(kk2[:, :], m.kk[:, bass.ds(i * 2 + h, 1), :].rearrange("p a t -> p (a t)"),
                                   ACT.Square).then_inc(s_kk2, 1)
                    copy_cols(2)
            eng.wait_ge(s_norm, 1)
            eng.activation(m.kk_norm[:, :, :], m.kk_norm[:, :, :], ACT.Ln).then_inc(s_ln, 1)
            eng.wait_ge(s_ln, 1)
            eng.activation(m.kk_norm[:, :, :], m.kk_norm[:, :, :], ACT.Exp, scale=-0.5).then_inc(s_rn, 1)

        @block.vector
        def _(eng):
            step = Steps(eng, s_step)
            for c in cols:
                step.did(eng.memset(c[:, 0:1], 0.0))
            step.did(eng.memset(m.cum[:, :, :].rearrange("p n (c t) -> p n c t", t=CH + 1)[:, :, :, 0:1], 0.0))
            step.did(eng.memset(carry[:, :, :], 1.0))
            step.wait()
            step.did(eng.memset(carry[:, :, 0:1], 0.0))
            step.wait()
            first = step.n
            for s in used + [s_lw_used, s_rate_used, s_ss_read, s_bo_read]:
                eng.sem_inc(s, 1)
            with eng.Fori(0, NP // 2) as i:
                body = Steps(eng, s_step, i * PER + first)
                for h in range(2):
                    pair = i * 2 + h

                    def at(t):
                        return t[:, bass.ds(pair, 1), :].rearrange("p a t -> p (a t)")

                    def col(name, add=0):
                        return m.vecs[:, bass.ds(pair + (VEC[name][0] + add), 1)]

                    def shifted(j, out):
                        eng.wait_ge(s_cols, i * 6 + (3 * h + j + 3))
                        prev = m.shift_prev[:, bass.ds(pair + j * NP, 1), :].rearrange("p a t -> p (a t)")
                        shift_mix(eng, body, m, cols[j], diff, out, col("rwkv_mu", j * NP), prev)
                        last = m.shift_last[:, :, bass.ds(pair + j * NP, 1)].rearrange("p t a -> p (t a)")
                        eng.tensor_copy(last, cols[j][:, TP:T + 1]).then_inc(used[j], 1)

                    shifted(0, at(m.r))
                    eng.wait_ge(s_tw, pair + 1)
                    body.did(eng.tensor_scalar(at(m.cum).rearrange("p (c t) -> p c t", t=CH + 1)[:, :, 1:CH + 1], tw[:, 0:TP].rearrange("p (c t) -> p c t", t=CH),
                                               DECAY / 2, DECAY / 2, ALU.mult, ALU.add))
                    eng.tensor_scalar(m.lw_sample[:, bass.ds(pair, 1), :].rearrange("p a t -> p (a t)"), tw[:, TP:T],
                                      DECAY / 2, DECAY / 2, ALU.mult, ALU.add).then_inc(s_lw_used, 1)
                    body.wait()
                    body.did(eng.tensor_tensor_scan(at(m.cum), carry[:, :, :].rearrange("p c t -> p (c t)"),
                                                    at(m.cum), 0.0, ALU.mult, ALU.add))
                    kx = at(m.kk_norm)
                    shifted(1, kx)
                    eng.tensor_scalar(at(m.kk), kx, col("k_k"), None, ALU.mult).then_inc(s_kk, 1)
                    eng.wait_ge(s_ta, pair + 1)
                    eng.tensor_scalar(rate[:, :], ta[:, :], 0.5, 0.5, ALU.mult, ALU.add).then_inc(s_rate_used, 1)
                    eng.wait_ge(s_kk, pair + 1)
                    eng.wait_ge(s_rate_used, pair + 2)
                    body.did(eng.tensor_tensor(at(m.br), at(m.kk), rate[:, :], ALU.mult))
                    body.wait()
                    body.did(eng.tensor_scalar(rate[:, :], rate[:, :], -1.0, col("k_a"), ALU.add, ALU.mult))
                    body.wait()
                    body.did(eng.scalar_tensor_tensor(out=at(m.k), in0=rate[:, :], scalar=1.0, in1=kx,
                                                      op0=ALU.add, op1=ALU.mult))
                    body.wait()
                    eng.scalar_tensor_tensor(out=rkk[:, :], in0=at(m.r), scalar=col("r_k"), in1=at(m.k),
                                             op0=ALU.mult, op1=ALU.mult).then_inc(s_rkk, 1)
                    shifted(2, at(m.v))
                    eng.wait_ge(s_ss, pair + 1)
                    eng.tensor_scalar(split(at(m.kk_norm)), halves(pss), 1e-24, None, ALU.max).then_inc(s_ss_read, 1)
                    eng.wait_ge(s_bo, pair + 1)
                    eng.tensor_tensor(split(at(m.bonus)), halves(psz), split(at(m.v)), ALU.mult).then_inc(s_bo_read, 1)
                assert body.n == PER, body.n
            eng.wait_ge(s_step, first + NP // 2 * PER)
            eng.wait_ge(s_ss_read, NP + 1)
            eng.sem_inc(s_norm, 1)
            eng.wait_ge(s_rn, 1)
            eng.scalar_tensor_tensor(out=m.kk[:, :, :], in0=m.kk[:, :, :], scalar=-1.0, in1=m.kk_norm[:, :, :],
                                     op0=ALU.mult, op1=ALU.mult)

        @block.gpsimd
        def _(eng):
            eng.wait_ge(s_rn, 1)
            eng.tensor_tensor(m.br[:, :, :], m.br[:, :, :], m.kk_norm[:, :, :], ALU.mult)


PER = 2 * (3 * 3 + 2 + 3)


def phase_chunks(nc, m, a):
    ctx, sb, ps, sem = open_phase(nc)
    with ctx:
        px = sb("ck_px", [P, NP, CH + 1])
        pi = sb("ck_pi", [P, NP, CH])
        L = sb("ck_L", [P, NP, 2, P])
        bk = sb("ck_bk", [P, NP, P])
        bkt = sb("ck_bkt", [P, NP, P])
        v2 = sb("ck_v2", [P, NP, 2, CH])
        wv = sb("ck_wv", [P, NP, 2, HD])
        mb = sb("ck_mb", [P, NP, P])
        nb = sb("ck_nb", [P, NP, P])
        a1 = sb("ck_a1", [P, NP, P])
        X = sb("ck_X", [P, NP, P])
        Z = sb("ck_Z", [P, NP, P])
        W = sb("ck_W", [P, NP, P])
        rh = sb("ck_rh", [P, NP, HD])
        st = sb("ck_st", [P, NP, HD])
        sto = sb("ck_sto", [HD, NP, P])
        bank = [[ps(f"ck_b{g}{n}", [P, 512]) for n in range(4)] for g in range(G)]
        (s_step, s_init, s_px, s_pi, s_ar, s_bk, s_v2, s_fin, s_sto, s_out, s_pstep, s_i2) = \
            (sem("k_" + n) for n in ("step", "init", "px", "pi", "ar", "bk", "v2", "fin", "sto", "out", "pstep", "i2"))

        def pair_sems(name):
            return [sem(f"k_{name}{g}") for g in range(G)]

        s_eo, s_tb, s_nt, s_w, s_xz, s_rhs, s_u, s_y, s_s = \
            (pair_sems(n) for n in ("eo", "tb", "nt", "w", "xz", "rhs", "u", "y", "s"))
        s_eo_e, s_nb, s_tb_e, s_a1, s_x1, s_w_e, s_xz_e, s_rh_e, s_u_e, s_y_e, s_st, s_s0 = \
            (pair_sems(n) for n in ("eo_e", "nb", "tb_e", "a1", "x1", "w_e", "xz_e", "rh_e", "u_e", "y_e", "st", "s0"))
        NL = len(LEVELS)
        block = ctx.enter_context(nc.Block())

        def grp(g):
            return slice(g * GP, (g + 1) * GP)

        def b4(ap):
            return ap[:, 0:GP * P].rearrange("p (n c) -> p n c", c=P)

        def b64(ap):
            return ap[:, 0:GP * HD].rearrange("p (n c) -> p n c", c=HD)

        lo, hi = slice(0, HD), slice(HD, P)

        @block.tensor
        def _(eng):
            with eng.Fori(0, NC) as c:
                for g in range(G):
                    b = bank[g]
                    if g == 0:
                        eng.wait_ge(s_ar, c * 4 + 4)
                        eng.wait_ge(s_bk, c * 4 + 4)
                    eng.wait_ge(s_st[g], c + 1)
                    eng.wait_ge(s_u_e[g], c * 2 + 2)
                    for n in range(GP):
                        p = g * GP + n
                        eng.matmul(b4(b[0])[:, n, :], bk[lo, p, :], L[lo, p, 0, :], start=True, stop=True)
                    for n in range(GP):
                        p = g * GP + n
                        last = eng.matmul(b4(b[1])[:, n, :], bk[hi, p, :], L[hi, p, 1, :], start=True, stop=True)
                    last.then_inc(s_eo[g], 1)
                for g in range(G):
                    b = bank[g]
                    if g == 0:
                        eng.wait_ge(s_v2, c + 1)
                    eng.wait_ge(s_y_e[g], c * 2 + 2)
                    for n in range(GP):
                        p = g * GP + n
                        eng.transpose(b4(b[2])[:, n, :], bk[:, p, :], m.ident[:, :])
                    for n in range(GP):
                        p = g * GP + n
                        last = eng.transpose(b4(b[3])[:, n, :], v2[:, p].rearrange("p a t -> p (a t)"), m.ident[:, :])
                    last.then_inc(s_tb[g], 1)
                for g in range(G):
                    b = bank[g]
                    eng.wait_ge(s_nb[g], c * 2 + 2)
                    eng.wait_ge(s_eo_e[g], c * 4 + 4)
                    for n in range(GP):
                        last = eng.transpose(b4(b[0])[:, n, :], nb[:, g * GP + n, :], m.ident[:, :])
                    last.then_inc(s_nt[g], 1)
                for lv in range(NL):
                    for g in range(G):
                        b = bank[g]
                        if lv == 0:
                            eng.wait_ge(s_a1[g], c + 1)
                            eng.wait_ge(s_x1[g], c * 2 + 2)
                            eng.wait_ge(s_tb_e[g], c * 3 + 3)
                        else:
                            eng.wait_ge(s_xz_e[g], c * (2 * NL - 1) + 2 * lv)
                        for n in range(GP):
                            p = g * GP + n
                            last = eng.matmul(b4(b[1])[:, n, :], a1[:, p, :], X[:, p, :], start=True, stop=True)
                        last.then_inc(s_w[g], 1)
                    for g in range(G):
                        b = bank[g]
                        eng.wait_ge(s_w_e[g], c * NL + lv + 1)
                        for n in range(GP):
                            p = g * GP + n
                            last = eng.matmul(b4(b[2])[:, n, :], Z[:, p, :], W[:, p, :], start=True, stop=True)
                        last.then_inc(s_xz[g], 1)
                        if lv < NL - 1:
                            for n in range(GP):
                                p = g * GP + n
                                last = eng.matmul(b4(b[3])[:, n, :], W[:, p, :], Z[:, p, :], start=True, stop=True)
                            last.then_inc(s_xz[g], 1)
                for g in range(G):
                    b = bank[g]
                    eng.wait_ge(s_s0[g], c * 2 + 2)
                    eng.wait_ge(s_xz_e[g], c * (2 * NL - 1) + (2 * NL - 1))
                    for n in range(GP):
                        p = g * GP + n
                        eng.matmul(b64(b[0])[lo, n, :], L[:, p, 0, 0:CH], wv[:, p, 0, :], start=True, stop=True)
                        last = eng.matmul(b64(b[0])[hi, n, :], L[:, p, 1, 0:CH], wv[:, p, 1, :], start=True, stop=True)
                    last.then_inc(s_rhs[g], 1)
                    for n in range(GP):
                        p = g * GP + n
                        eng.matmul(b64(b[2])[lo, n, :], wv[:, p, 0, :], L[:, p, 0, CH:P], start=(n == 0), stop=False,
                                   skip_group_check=True)
                        eng.matmul(b64(b[3])[hi, n, :], wv[:, p, 1, :], L[:, p, 1, CH:P], start=(n == 0), stop=False,
                                   skip_group_check=True)
                for g in range(G):
                    b = bank[g]
                    eng.wait_ge(s_rh_e[g], c + 1)
                    for n in range(GP):
                        p = g * GP + n
                        last = eng.matmul(b64(b[1])[:, n, :], X[:, p, :], rh[:, p, :], start=True, stop=True)
                    last.then_inc(s_u[g], 1)
                for g in range(G):
                    b = bank[g]
                    eng.wait_ge(s_u_e[g], c * 2 + 4)
                    for n in range(GP):
                        p = g * GP + n
                        eng.matmul(b64(b[0])[lo, n, :], bkt[:, p, 0:HD], wv[:, p, 0, :], start=True, stop=True)
                        last = eng.matmul(b64(b[0])[hi, n, :], bkt[:, p, HD:P], wv[:, p, 1, :], start=True, stop=True)
                    last.then_inc(s_s[g], 1)
                    for n in range(GP):
                        p = g * GP + n
                        eng.matmul(b64(b[2])[lo, n, :], wv[lo, p, 0, :], mb[lo, p, CH:P], start=False, stop=True,
                                   skip_group_check=True)
                        last = eng.matmul(b64(b[3])[hi, n, :], wv[hi, p, 1, :], mb[hi, p, CH:P], start=False, stop=True,
                                          skip_group_check=True)
                    last.then_inc(s_y[g], 1)
            for g in range(G):
                eng.wait_ge(s_s0[g], NC * 2 + 2)
                eng.wait_ge(s_y_e[g], NC * 2 + 2)
                for n in range(GP):
                    last = eng.transpose(b4(bank[g][2])[0:HD, n, :], st[:, g * GP + n, :], m.ident[:, :])
                last.then_inc(s_fin, 1)

        @block.scalar
        def _(eng):
            for g in range(G):
                eng.sem_inc(s_y_e[g], 2)
            eng.sem_inc(s_u_e[0], 1)
            eng.sem_inc(s_u_e[1], 1)
            with eng.Fori(0, NC) as c:
                def cumulative(first):
                    return m.cum[:, :, :].rearrange("p n (c t) -> p n c t", t=CH + 1)[:, :, bass.ds(c, 1), first:CH + 1]\
                        .rearrange("p n a t -> p n (a t)")

                eng.wait_ge(s_st[1], c + 1)
                eng.activation(px[:, :, :], cumulative(0), ACT.Exp).then_inc(s_px, 1)
                eng.activation(pi[:, :, :], cumulative(1), ACT.Exp, scale=-1.0).then_inc(s_pi, 1)
                for half in range(2):
                    ins = eng.activation(v2[:, :, half, :], m.v[:, :, bass.ds(c * CH, CH)], ACT.Copy)
                ins.then_inc(s_v2, 1)
                for g in range(G):
                    b = bank[g]
                    eng.wait_ge(s_tb[g], c + 1)
                    eng.activation(bkt[:, grp(g), :], b4(b[2]), ACT.Copy).then_inc(s_tb_e[g], 1)
                    eng.activation(wv[hi, grp(g), 0, :], b4(b[3])[hi, :, 0:HD], ACT.Copy).then_inc(s_tb_e[g], 1)
                    eng.activation(wv[lo, grp(g), 1, :], b4(b[3])[lo, :, HD:P], ACT.Copy).then_inc(s_tb_e[g], 1)
                for g in range(G):
                    eng.wait_ge(s_nt[g], c + 1)
                    eng.activation(a1[:, grp(g), :], b4(bank[g][0]), ACT.Copy).then_inc(s_a1[g], 1)
                for lv in range(NL):
                    for g in range(G):
                        eng.wait_ge(s_xz[g], c * (2 * NL - 1) + 2 * lv + 1)
                        eng.activation(X[:, grp(g), :], b4(bank[g][2]), ACT.Copy).then_inc(s_xz_e[g], 1)
                        if lv < NL - 1:
                            eng.wait_ge(s_xz[g], c * (2 * NL - 1) + 2 * lv + 2)
                            eng.activation(Z[:, grp(g), :], b4(bank[g][3]), ACT.Copy).then_inc(s_xz_e[g], 1)
                for g in range(G):
                    eng.wait_ge(s_rhs[g], c + 1)
                    eng.activation(rh[:, grp(g), :], b64(bank[g][0]), ACT.Copy).then_inc(s_rh_e[g], 1)
                for g in range(G):
                    eng.wait_ge(s_u[g], c + 1)
                    eng.activation(wv[lo, grp(g), 0, :], b64(bank[g][1])[lo], ACT.Copy).then_inc(s_u_e[g], 1)
                for g in range(G):
                    eng.wait_ge(s_y[g], c + 1)
                    y = m.r[:, grp(g), bass.ds(c * CH, CH)]
                    eng.activation(y[lo], b64(bank[g][2])[lo], ACT.Copy).then_inc(s_y_e[g], 1)
                    eng.activation(y[hi], b64(bank[g][3])[hi], ACT.Copy).then_inc(s_y_e[g], 1)
                    eng.wait_ge(s_st[g], c + 2)
                    eng.activation(wv[lo, grp(g), 0, :], st[lo, grp(g), :], ACT.Copy).then_inc(s_s0[g], 1)
            for g in range(G):
                eng.wait_ge(s_fin, g + 1)
                eng.activation(sto[:, grp(g), :], b4(bank[g][2])[0:HD], ACT.Copy).then_inc(s_sto, 1)

        @block.vector
        def _(eng):
            step = Steps(eng, s_step)
            step.did(eng.memset(st[:, :, :], 0.0))
            step.did(eng.memset(wv[:, :, :, :], 0.0))
            step.did(eng.memset(nb[:, :, :], 0.0))
            step.wait()
            first = step.n
            for g in range(G):
                eng.sem_inc(s_st[g], 1)
                eng.sem_inc(s_u_e[g], 1)
                eng.sem_inc(s_s0[g], 2)
            eng.sem_inc(s_init, 1)
            with eng.Fori(0, NC) as c:
                body = Steps(eng, s_step, c * G + first)
                eng.wait_ge(s_px, c + 1)
                cc = bass.ds(c * CH, CH)
                for _ in range(1):
                    eng.tensor_tensor(L[lo, :, 0, 0:CH], m.kk[lo, :, cc], px[lo, :, 0:CH], ALU.mult).then_inc(s_ar, 1)
                    eng.tensor_tensor(L[lo, :, 0, CH:P], m.r[lo, :, cc], px[lo, :, 1:CH + 1], ALU.mult).then_inc(s_ar, 1)
                    eng.tensor_tensor(L[hi, :, 1, 0:CH], m.kk[hi, :, cc], px[hi, :, 0:CH], ALU.mult).then_inc(s_ar, 1)
                    eng.tensor_tensor(L[hi, :, 1, CH:P], m.r[hi, :, cc], px[hi, :, 1:CH + 1], ALU.mult).then_inc(s_ar, 1)
                for g in range(G):
                    b = bank[g]
                    mask = m.causal[:, :].unsqueeze(1).to_broadcast([P, GP, P])
                    eng.wait_ge(s_eo[g], c + 1)
                    eng.tensor_tensor(mb[lo, grp(g), :], b4(b[0])[lo], mask[lo], ALU.mult).then_inc(s_eo_e[g], 1)
                    eng.tensor_tensor(mb[hi, grp(g), :], b4(b[1])[hi], mask[hi], ALU.mult).then_inc(s_eo_e[g], 1)
                    eng.tensor_tensor(L[hi, grp(g), 0, :], b4(b[0])[hi], mask[hi], ALU.mult).then_inc(s_eo_e[g], 1)
                    eng.tensor_tensor(L[lo, grp(g), 1, :], b4(b[1])[lo], mask[lo], ALU.mult).then_inc(s_eo_e[g], 1)
                for g in range(G):
                    eng.wait_ge(s_nb[g], c * 2 + 2)
                    eng.tensor_tensor(X[:, grp(g), :], nb[:, grp(g), :],
                                      m.levels[:, 0, :].unsqueeze(1).to_broadcast([P, GP, P]), ALU.mult).then_inc(s_x1[g], 1)
                for g in range(G):
                    eng.wait_ge(s_a1[g], c + 1)
                    eng.tensor_tensor(Z[:, grp(g), :], a1[:, grp(g), :],
                                      m.level1t[:, :].unsqueeze(1).to_broadcast([P, GP, P]), ALU.mult).then_inc(s_x1[g], 1)
                for lv in range(NL):
                    for g in range(G):
                        eng.wait_ge(s_w[g], c * NL + lv + 1)
                        eng.tensor_tensor(W[:, grp(g), :], b4(bank[g][1]),
                                          m.levels[:, lv + 1, :].unsqueeze(1).to_broadcast([P, GP, P]), ALU.mult)\
                           .then_inc(s_w_e[g], 1)
                for g in range(G):
                    eng.wait_ge(s_u[g], c + 1)
                    eng.tensor_copy(wv[hi, grp(g), 1, :], b64(bank[g][1])[hi]).then_inc(s_u_e[g], 1)
                for g in range(G):
                    eng.wait_ge(s_s[g], c + 1)
                    eng.wait_ge(s_s0[g], c * 2 + 2)
                    body.did(eng.tensor_tensor(st[:, grp(g), :], b64(bank[g][0]), st[:, grp(g), :], ALU.add))
                    body.wait()
                    eng.tensor_tensor(st[:, grp(g), :], st[:, grp(g), :],
                                      px[:, grp(g), CH:CH + 1].to_broadcast([P, GP, HD]), ALU.mult).then_inc(s_st[g], 1)
                    eng.wait_ge(s_st[g], c + 2)
                    eng.wait_ge(s_y[g], c + 1)
                    eng.tensor_copy(wv[hi, grp(g), 1, :], st[hi, grp(g), :]).then_inc(s_s0[g], 1)

        @block.gpsimd
        def _(eng):
            eng.wait_ge(s_init, 1)
            with eng.Fori(0, NC) as c:
                cc = bass.ds(c * CH, CH)
                eng.wait_ge(s_pi, c + 1)
                eng.tensor_tensor(bk[lo, :, 0:CH], m.br[lo, :, cc], pi[lo, :, :], ALU.mult).then_inc(s_bk, 1)
                eng.tensor_tensor(bk[lo, :, CH:P], m.k[lo, :, cc], pi[lo, :, :], ALU.mult).then_inc(s_bk, 1)
                eng.tensor_tensor(bk[hi, :, CH:P], m.br[hi, :, cc], pi[hi, :, :], ALU.mult).then_inc(s_bk, 1)
                eng.tensor_tensor(bk[hi, :, 0:CH], m.k[hi, :, cc], pi[hi, :, :], ALU.mult).then_inc(s_bk, 1)
                for g in range(G):
                    eng.wait_ge(s_eo_e[g], c * 4 + 2)
                    eng.tensor_tensor(nb[lo, grp(g), 0:CH], mb[lo, grp(g), 0:CH],
                                      m.ident[lo, 0:CH].unsqueeze(1).to_broadcast([HD, GP, CH]), ALU.add).then_inc(s_nb[g], 1)
                    eng.tensor_tensor(nb[hi, grp(g), CH:P], mb[hi, grp(g), 0:CH],
                                      m.ident[hi, CH:P].unsqueeze(1).to_broadcast([HD, GP, CH]), ALU.add).then_inc(s_nb[g], 1)

        @block.sync
        def _(eng):
            eng.wait_ge(s_sto, G)
            eng.dma_start(a["new_wkv_prompt"][0, 0].rearrange("(n e) i j -> i n e j", e=2),
                          sto[:, :, :].rearrange("i n (e j) -> i n e j", e=2)).then_inc(s_out, 16)
            eng.wait_ge(s_out, 16)


def phase_sample_vectors(nc, m, a):
    ctx, sb, ps, sem = open_phase(nc)
    with ctx:
        tok = sb("sv_tok", [TS, 6, D])
        sh = sb("sv_sh", [3 * NSH, 3, P])
        pst = ps("sv_ps", [P, 6, 512])
        psh = ps("sv_psh", [P, 512])
        s_w, s_t, s_e, s_h, s_he, s_out, s_q = (sem("v_" + n) for n in ("w", "t", "e", "h", "he", "out", "q"))
        block = ctx.enter_context(nc.Block())

        @block.scalar
        def _(eng):
            eng.activation(m.lw_sample[:, :, :], m.lw_sample[:, :, :], ACT.Exp).then_inc(s_w, 1)
            for n in range(6):
                eng.wait_ge(s_t, n + 1)
                eng.activation(tok[:, n, :].rearrange("b (h c) -> b h c", h=2), pst[0:TS, 2 * (n % 3):2 * (n % 3) + 2, :],
                               ACT.Copy).then_inc(s_e, 1)

        @block.tensor
        def _(eng):
            eng.wait_ge(s_w, 1)
            for n, t in enumerate((m.r, m.lw_sample, m.k, m.v, m.kk, m.br)):
                if n >= 3:
                    eng.wait_ge(s_e, n - 2)
                for p in range(NP):
                    src = t[:, p, :] if n == 1 else t[:, p, TP:T]
                    last = eng.transpose(pst[0:TS, 2 * (n % 3) + p // 4, (p % 4) * P:(p % 4 + 1) * P], src, m.ident[:, :])
                last.then_inc(s_t, 1)
            for n in range(3):
                last = eng.transpose(psh[0:3 * NSH, n * P:(n + 1) * P],
                                     m.shift_last[:, 3 * n:3 * n + 3, :].rearrange("p t c -> p (t c)"), m.ident[:, :])
            last.then_inc(s_h, 1)

        @block.vector
        def _(eng):
            eng.wait_ge(s_h, 1)
            eng.tensor_copy(sh[:, :, :], psh[0:3 * NSH, 0:3 * P].rearrange("r (n c) -> r n c", n=3)).then_inc(s_he, 1)

        @block.sync
        def _(eng):
            eng.wait_ge(s_e, 6)
            eng.dma_start(m.d_sample.rearrange("n b c -> b n c"), tok[:, :, :]).then_inc(s_q, 16)
            eng.wait_ge(s_q, 16)
            eng.dma_start(m.sv[:, :, :], m.d_sample.rearrange("n b (h j) -> (b h) n j", j=HD)).then_inc(m.s_sv, 16)
            eng.wait_ge(s_he, 1)
            eng.dma_start(a["new_shift_prompt"][0, 0].rearrange("(c p) -> c p", p=P), sh[0:NSH, 0, :]).then_inc(s_out, 16)
            eng.dma_start(a["new_shift_sample"][0, 0:2].rearrange("t (c p) -> (t c) p", p=P), sh[NSH:3 * NSH, 0, :]).then_inc(s_out, 16)
            for n in range(1, 3):
                eng.dma_start(a["new_shift_sample"][0, 3 * n - 1:3 * n + 2].rearrange("t (c p) -> (t c) p", p=P), sh[:, n, :])\
                   .then_inc(s_out, 16)
            eng.wait_ge(s_out, 64)


def phase_gating(nc, m, a):
    ctx, sb, ps, sem = open_phase(nc)
    with ctx:
        w = sb("uv_w", [P, 2, 2, NK, P])
        lnw = sb("uv_lnw", [P, D])
        lnb = sb("uv_lnb", [P, D])
        sbias = sb("uv_sb", [P, D])
        gv = sb("uv_gv", [P, T])
        gu = sb("uv_gu", [P, T])
        vn = sb("uv_vn", [P, NT + 1, P])
        vns = sb("uv_vns", [TS, D])
        st = sb("uv_st", [P, NT + 1, 6])
        mv = sb("uv_mv", [P, NT + 1, 2])
        rstd = sb("uv_rstd", [P, NT + 1])
        pause = sb("uv_pause", [P, 1])
        gate = sb("uv_gate", [P, T])
        T1 = sb("sw_t", [P, HD, HD])
        sa = sb("sw_sa", [P, HD])
        ys = sb("sw_y", [P, HD])
        yt = sb("sw_yt", [TS, D])
        psv = ps("uv_psv", [P, 2, 512])
        psu = ps("uv_psu", [P, 2, 512])
        pst = ps("uv_pst", [P, 512])
        psx = ps("uv_psx", [P, 512])
        psw = ps("uv_psw", [P, 512])
        pss = ps("uv_pss", [P, 512])
        s_w = [sem("u_w0"), sem("u_w1")]
        s_S = sem("u_S")
        (s_row, s_pv, s_pu, s_gv, s_gu, s_t, s_mv, s_ve, s_ln, s_rs, s_vn, s_sp,
         s_ya, s_step, s_zero, s_vns, s_cv, s_pool, s_sdone, s_y, s_yd, s_yl, s_yt, s_rstep) = \
            (sem("u_" + n) for n in ("row", "pv", "pu", "gv", "gu", "t", "mv", "ve", "ln", "rs",
                                     "vn", "sp", "ya", "step", "zero", "vns", "cv", "pool", "sdone", "y", "yd",
                                     "yl", "yt", "rstep"))
        block = ctx.enter_context(nc.Block())
        row = lambda ap: ap.rearrange("l h d -> l (h d)").partition_broadcast(P).rearrange("p l d -> p (l d)")

        @block.sync
        def _(eng):
            def load(slot, h):
                for n, off in enumerate((OFF_V, 0)):
                    eng.dma_start(w[:, slot, n], w_cols(a["w_in"], bass.ds(h * P + off, P))).then_inc(s_w[slot], 16)

            load(0, 0)
            eng.dma_start(m.S[:, :, :], a["state_wkv"][0].rearrange("b h i j -> (b h) i j")).then_inc(s_S, 16)
            load(1, 1)
            for t, src in ((lnw, a["sgu_ln_w"]), (lnb, a["sgu_ln_b"]), (sbias, a["sgu_b"])):
                eng.dma_start(t[:, :], row(src)).then_inc(s_row, 16)
            with eng.Fori(1, NP // 2) as i:
                for slot in range(2):
                    eng.wait_ge(s_pu, i * 2 + (slot - 1))
                    load(slot, i * 2 + slot)
            eng.wait_ge(s_vns, NP)
            eng.dma_start(a["new_chunk_v_sample"].rearrange("l b t h d -> (l b t) (h d)"), vns[:, :]).then_inc(s_cv, 16)
            eng.wait_ge(s_sdone, 1)
            eng.dma_start(a["new_wkv_sample"][0].rearrange("b h i j -> (b h) i j"), m.S[:, :, :]).then_inc(s_cv, 16)
            eng.wait_ge(s_y, 1)
            eng.dma_start(m.d_y.rearrange("b (h j) -> (b h) j", j=HD), ys[:, :]).then_inc(s_yd, 16)
            eng.wait_ge(s_yd, 16)
            eng.dma_start(yt[:, :], m.d_y).then_inc(s_yl, 16)
            eng.wait_ge(s_cv, 32)

        @block.tensor
        def _(eng):
            with eng.Fori(0, NP // 2) as i:
                for x in range(2):
                    h = i * 2 + x
                    eng.wait_ge(s_w[x], i * 32 + 32)
                    eng.wait_ge(s_gv, h + 1)
                    project(eng, psv, w[:, x, 0], m.xT).then_inc(s_pv, 1)
                    eng.wait_ge(s_gv, h + 2)
                    eng.wait_ge(s_ve, h + 1)
                    for c in range(NT):
                        eng.transpose(pst[:, c * P:(c + 1) * P], gv[:, c * P:(c + 1) * P], m.ident[:, :])
                    eng.transpose(psx[0:TS, 0:P], gv[:, TP:T], m.ident[:, :]).then_inc(s_t, 1)
                    eng.wait_ge(s_gu, h + 1)
                    project(eng, psu, w[:, x, 1], m.xT).then_inc(s_pu, 1)
                    eng.wait_ge(s_vn, h + 1)
                    eng.wait_ge(s_ya, h + 1)
                    for c in range(NT):
                        last = eng.matmul(pss[:, c * P:(c + 1) * P], vn[:, c, :],
                                          m.wst[:, bass.ds(h, 1), :].rearrange("p a t -> p (a t)"),
                                          start=True, stop=True)
                    eng.transpose(psw[:, 0:TS], vn[0:TS, NT, :], m.ident[0:TS, 0:TS]).then_inc(s_sp, 1)
            eng.wait_ge(s_yl, 16)
            eng.wait_ge(s_ya, NP + 1)
            for p in range(NP):
                last = eng.transpose(psw[:, p * TS:(p + 1) * TS], yt[:, p * P:(p + 1) * P], m.ident[0:TS, 0:TS])
            last.then_inc(s_yt, 1)

        @block.scalar
        def _(eng):
            eng.sem_inc(s_gv, 1)
            eng.sem_inc(s_gu, 1)
            with eng.Fori(0, NP // 2) as i:
                for x in range(2):
                    h = i * 2 + x
                    eng.wait_ge(s_pv, h + 1)
                    eng.activation(split(gv[:, :]), halves(psv), ACT.Gelu_apprx_tanh).then_inc(s_gv, 1)
                    eng.wait_ge(s_mv, h + 1)
                    eng.activation(rstd[:, :], mv[:, :, 1], ACT.Ln).then_inc(s_ln, 1)
                    eng.wait_ge(s_ln, h + 1)
                    eng.activation(rstd[:, :], rstd[:, :], ACT.Exp, scale=-0.5).then_inc(s_rs, 1)
                    eng.wait_ge(s_pu, h + 1)
                    eng.wait_ge(s_ya, h + 1)
                    eng.activation(split(gu[:, :]), halves(psu), ACT.Gelu_apprx_tanh).then_inc(s_gu, 1)

        @block.vector
        def _(eng):
            eng.memset(mv[:, :, :], 1.0).then_inc(s_zero, 1)
            eng.wait_ge(s_zero, 1)
            eng.sem_inc(s_ve, 1)
            eng.sem_inc(s_ya, 1)
            eng.wait_ge(s_row, 48)
            with eng.Fori(0, NP // 2) as i:
                body = Steps(eng, s_step, i * UV_PER)
                for x in range(2):
                    h = i * 2 + x
                    hs = bass.ds(h * P, P)
                    eng.wait_ge(s_t, h + 1)
                    for c in range(NT + 1):
                        n = P if c < NT else TS
                        src = pst[:, c * P:(c + 1) * P] if c < NT else psx[0:TS, 0:P]
                        body.did(eng.bn_stats(st[0:n, c, :], src))
                    body.wait()
                    eng.memset(pause[:, :], 0.0)
                    for c in range(NT + 1):
                        n = P if c < NT else TS
                        body.did(eng.bn_aggr(mv[0:n, c, :], st[0:n, c, :]))
                    body.wait()
                    eng.tensor_scalar(mv[:, :, 1], mv[:, :, 1], LN_EPS, None, ALU.add).then_inc(s_mv, 1)
                    eng.wait_ge(s_rs, h + 1)
                    for c in range(NT + 1):
                        n = P if c < NT else TS
                        src = pst[:, c * P:(c + 1) * P] if c < NT else psx[0:TS, 0:P]
                        ins = eng.tensor_scalar(vn[0:n, c, :], src, mv[0:n, c, 0:1], rstd[0:n, c:c + 1],
                                                ALU.subtract, ALU.mult)
                        if c < NT:
                            body.did(ins)
                    ins.then_inc(s_ve, 1)
                    eng.wait_ge(s_ve, h + 2)
                    body.wait()
                    body.did(eng.tensor_tensor(vn[:, 0:NT, :], vn[:, 0:NT, :],
                                               lnw[:, hs].unsqueeze(1).to_broadcast([P, NT, P]), ALU.mult))
                    body.did(eng.tensor_tensor(vn[0:TS, NT, :], vn[0:TS, NT, :], lnw[0:TS, hs], ALU.mult))
                    body.wait()
                    body.did(eng.tensor_tensor(vn[0:TS, NT, :], vn[0:TS, NT, :], lnb[0:TS, hs], ALU.add))
                    eng.tensor_tensor(vn[:, 0:NT, :], vn[:, 0:NT, :],
                                      lnb[:, hs].unsqueeze(1).to_broadcast([P, NT, P]), ALU.add).then_inc(s_vn, 1)
                    body.wait()
                    eng.tensor_copy(vns[:, hs], vn[0:TS, NT, :]).then_inc(s_vns, 1)
                    eng.wait_ge(s_sp, h + 1)
                    body.did(eng.tensor_tensor(gate[:, 0:TP].rearrange("p (c t) -> p c t", t=P),
                                               pss[:, :].rearrange("p (c t) -> p c t", t=P),
                                               sbias[:, hs].unsqueeze(1).to_broadcast([P, NT, P]), ALU.add))
                    body.did(eng.tensor_scalar(gate[:, TP:T], psw[:, 0:TS], m.w00[:, bass.ds(h, 1)],
                                               sbias[:, bass.ds(h * P, 1)], ALU.mult, ALU.add))
                    body.wait()
                    eng.wait_ge(s_gu, h + 2)
                    eng.tensor_tensor(m.ya[:, bass.ds(h, 1), :].rearrange("p a t -> p (a t)"), gate[:, :], gu[:, :],
                                      ALU.mult).then_inc(s_ya, 1)
                assert body.n == UV_PER, body.n
            eng.wait_ge(s_yt, 1)
            eng.tensor_copy(m.r[:, :, TP:T], psw[:, 0:NP * TS].rearrange("p (n t) -> p n t", t=TS)).then_inc(s_rstep, 1)

        @block.gpsimd
        def _(eng):
            eng.wait_ge(m.s_sv, 16)
            eng.wait_ge(s_S, 16)
            step = Steps(eng, s_pool)
            full = [P, HD, HD]
            r, wd, k, v, aa, b = (m.sv[:, n, :] for n in range(6))
            over_i = lambda t: t.unsqueeze(1).to_broadcast(full)
            over_j = lambda t: t.unsqueeze(2).to_broadcast(full)

            def reduce_j(out):
                n = HD // 2
                while n:
                    dst = T1[:, :, 0:n] if n > 1 else out.unsqueeze(2)
                    step.did(eng.tensor_tensor(dst, T1[:, :, 0:n], T1[:, :, n:2 * n], ALU.add))
                    step.wait()
                    n //= 2

            step.did(eng.tensor_tensor(T1[:, :, :], m.S[:, :, :], over_i(aa), ALU.mult))
            step.wait()
            step.did(eng.tensor_tensor(m.S[:, :, :], m.S[:, :, :], over_i(wd), ALU.mult))
            reduce_j(sa[:, :])
            step.did(eng.tensor_tensor(T1[:, :, :], over_j(sa[:, :]), over_i(b), ALU.mult))
            step.wait()
            step.did(eng.tensor_tensor(m.S[:, :, :], m.S[:, :, :], T1[:, :, :], ALU.add))
            step.wait()
            step.did(eng.tensor_tensor(T1[:, :, :], over_j(v), over_i(k), ALU.mult))
            step.wait()
            step.did(eng.tensor_tensor(m.S[:, :, :], m.S[:, :, :], T1[:, :, :], ALU.add))
            step.wait()
            eng.sem_inc(s_sdone, 1)
            step.did(eng.tensor_tensor(T1[:, :, :], m.S[:, :, :], over_i(r), ALU.mult))
            step.wait()
            reduce_j(ys[:, :])
            eng.sem_inc(s_y, 1)


UV_PER = 2 * (5 + 5 + 4 + 3 + 2)


def phase_spatial_weights(nc, m, a):
    ctx, sb, ps, sem = open_phase(nc)
    with ctx:
        ws = sb("sw_ws", [P, NP, P])
        psw = ps("sw_ps", [P, 2, 512])
        ps0 = ps("sw_ps0", [P, 512])
        s_ws, s_wm, s_t, s_e = (sem("w_" + n) for n in ("ws", "wm", "t", "e"))
        block = ctx.enter_context(nc.Block())

        @block.sync
        def _(eng):
            eng.dma_start(ws[:, :, :], a["sgu_w_s"][0].rearrange("h t s -> t h s")).then_inc(s_ws, 16)

        @block.gpsimd
        def _(eng):
            eng.wait_ge(s_ws, 16)
            eng.affine_select(out=ws[:, :, :], in_=ws[:, :, :], compare_op=ALU.is_ge, fill=0.0, base=0,
                              pattern=[[0, NP], [-1, P]], channel_multiplier=1).then_inc(s_wm, 1)

        @block.tensor
        def _(eng):
            eng.wait_ge(s_wm, 1)
            for h in range(NP):
                last = eng.transpose(psw[:, h // 4, (h % 4) * P:(h % 4 + 1) * P], ws[:, h, :], m.ident[:, :])
            last.then_inc(s_t, 1)
            eng.wait_ge(s_e, 1)
            eng.matmul(ps0[:, 0:NP], m.ones[0:1, :], m.wst[0:1, :, 0], start=True, stop=True).then_inc(s_t, 1)

        @block.vector
        def _(eng):
            eng.wait_ge(s_t, 1)
            eng.tensor_copy(m.wst[:, :, :].rearrange("p (a h) t -> p a h t", a=2),
                            psw[:, :, :].rearrange("p a (h t) -> p a h t", t=P)).then_inc(s_e, 1)
            eng.wait_ge(s_t, 2)
            eng.tensor_copy(m.w00[:, :], ps0[:, 0:NP])


def phase_head_norm(nc, m, a):
    ctx, sb, ps, sem = open_phase(nc)
    with ctx:
        gl = sb("hn_gl", [P, 2, P])
        yc = sb("hn_yc", [P, 2, T])
        sq = sb("hn_sq", [P, 2, T])
        psm = ps("hn_psm", [P, 2, 512])
        psq = ps("hn_psq", [P, 2, 512])
        psg = ps("hn_psg", [P, 2, 512])
        s_w = [sem("h_w0"), sem("h_w1")]
        (s_m, s_g, s_v, s_yc, s_sq, s_var, s_ln, s_rs, s_yb, s_step) = \
            (sem("h_" + n) for n in ("m", "g", "v", "yc", "sq", "var", "ln", "rs", "yb", "step"))
        block = ctx.enter_context(nc.Block())

        @block.sync
        def _(eng):
            def load(slot, p):
                eng.dma_start(gl[:, slot, :], a["g_lora_up"][0, :, bass.ds(p * P, P)]).then_inc(s_w[slot], 16)

            for slot in range(2):
                load(slot, slot)
            with eng.Fori(1, NP // 2) as i:
                for slot in range(2):
                    eng.wait_ge(s_g, i * 2 + (slot - 1))
                    load(slot, i * 2 + slot)

        @block.tensor
        def _(eng):
            with eng.Fori(0, NP // 2) as i:
                for x in range(2):
                    p = i * 2 + x
                    y = m.r[:, bass.ds(p, 1), :].rearrange("p a t -> p (a t)")
                    eng.wait_ge(s_yc, p + 1)
                    for half in range(2):
                        last = eng.matmul(psm[:, half, 0:TH], m.headones[:, :], split(y)[:, half, :], start=True, stop=True)
                    last.then_inc(s_m, 1)
                    eng.wait_ge(s_w[x], i * 16 + 16)
                    eng.wait_ge(s_yb, p + 1)
                    for half in range(2):
                        last = eng.matmul(psg[:, half, 0:TH], gl[:, x, :], m.gate_in[:, half * TH:(half + 1) * TH],
                                          start=True, stop=True)
                    last.then_inc(s_g, 1)
                    eng.wait_ge(s_sq, p + 1)
                    eng.wait_ge(s_var, p + 1)
                    for half in range(2):
                        last = eng.matmul(psq[:, half, 0:TH], m.headones[:, :], sq[:, x, half * TH:(half + 1) * TH],
                                          start=True, stop=True)
                    last.then_inc(s_v, 1)

        @block.scalar
        def _(eng):
            with eng.Fori(0, NP // 2) as i:
                for x in range(2):
                    p = i * 2 + x
                    eng.wait_ge(s_yc, p + 2)
                    eng.activation(sq[:, x, :], yc[:, x, :], ACT.Square).then_inc(s_sq, 1)
                    eng.wait_ge(s_var, p + 2)
                    eng.activation(sq[:, x, :], sq[:, x, :], ACT.Ln).then_inc(s_ln, 1)
                    eng.wait_ge(s_ln, p + 1)
                    eng.activation(sq[:, x, :], sq[:, x, :], ACT.Exp, scale=-0.5).then_inc(s_rs, 1)

        @block.vector
        def _(eng):
            for s in (s_yc, s_var, s_yb):
                eng.sem_inc(s, 1)
            with eng.Fori(0, NP // 2) as i:
                body = Steps(eng, s_step, i * 4)
                for x in range(2):
                    p = i * 2 + x
                    y = m.r[:, bass.ds(p, 1), :].rearrange("p a t -> p (a t)")

                    def col(name):
                        return m.vecs[:, bass.ds(p + VEC[name][0], 1)]

                    eng.wait_ge(s_m, p + 1)
                    eng.scalar_tensor_tensor(out=split(yc[:, x, :]), in0=halves(psm), scalar=-1.0 / HD, in1=split(y),
                                             op0=ALU.mult, op1=ALU.add).then_inc(s_yc, 1)
                    eng.wait_ge(s_v, p + 1)
                    eng.tensor_scalar(split(sq[:, x, :]), halves(psq), 1.0 / HD, GN_EPS, ALU.mult, ALU.add).then_inc(s_var, 1)
                    eng.wait_ge(s_rs, p + 1)
                    body.did(eng.tensor_tensor(yc[:, x, :], yc[:, x, :], sq[:, x, :], ALU.mult))
                    body.wait()
                    bonus = m.bonus[:, bass.ds(p, 1), :].rearrange("p a t -> p (a t)")
                    body.did(eng.scalar_tensor_tensor(out=yc[:, x, :], in0=yc[:, x, :], scalar=col("lnx_w"), in1=bonus,
                                                      op0=ALU.mult, op1=ALU.add))
                    body.wait()
                    eng.wait_ge(s_g, p + 1)
                    eng.scalar_tensor_tensor(out=split(m.yb[:, bass.ds(p, 1), :].rearrange("p a t -> p (a t)")),
                                             in0=split(yc[:, x, :]), scalar=col("lnx_b"), in1=halves(psg),
                                             op0=ALU.add, op1=ALU.mult).then_inc(s_yb, 1)


def phase_merge(nc, m, a):
    ctx, sb, ps, sem = open_phase(nc)
    with ctx:
        w = sb("mg_w", [P, 2, 4, NK, P])
        g = sb("mg_g", [P, 2, T])
        t = sb("mg_t", [P, 2, T])
        psn = [ps(f"mg_ps{n}", [P, 2, 512]) for n in range(4)]
        s_w = [sem("m_w0"), sem("m_w1")]
        s_p = [sem(f"m_p{n}") for n in range(4)]
        s_g, s_t, s_mg = (sem("m_" + n) for n in ("g", "t", "mg"))
        block = ctx.enter_context(nc.Block())

        @block.sync
        def _(eng):
            def load(slot, c):
                for n, off in enumerate((OFF_GA, OFF_GB)):
                    eng.dma_start(w[:, slot, n], w_cols(a["w_in"], bass.ds(c * P + off, P))).then_inc(s_w[slot], 16)
                for n, src in ((2, a["proj_a"]), (3, a["proj_b"])):
                    eng.dma_start(w[:, slot, n], w_cols(src, bass.ds(c * P, P))).then_inc(s_w[slot], 16)

            for slot in range(2):
                load(slot, slot)
            with eng.Fori(1, NP // 2) as i:
                for slot in range(2):
                    eng.wait_ge(s_p[3], i * 2 + (slot - 1))
                    load(slot, i * 2 + slot)

        @block.tensor
        def _(eng):
            with eng.Fori(0, NP // 2) as i:
                for x in range(2):
                    c = i * 2 + x
                    eng.wait_ge(s_w[x], i * 64 + 64)
                    for n, src in enumerate((m.xT, m.xT, m.ya, m.yb)):
                        if n < 2:
                            eng.wait_ge(s_g, c * 2 + n + 1)
                        else:
                            eng.wait_ge(s_t, c * 2 + n - 1)
                        project(eng, psn[n], w[:, x, n], src).then_inc(s_p[n], 1)

        @block.scalar
        def _(eng):
            eng.sem_inc(s_g, 2)
            with eng.Fori(0, NP // 2) as i:
                for x in range(2):
                    c = i * 2 + x
                    for n in range(2):
                        eng.wait_ge(s_p[n], c + 1)
                        eng.wait_ge(s_t, c * 2 + n + 1)
                        eng.activation(split(g[:, n, :]), halves(psn[n]), ACT.Sigmoid).then_inc(s_g, 1)

        @block.vector
        def _(eng):
            eng.sem_inc(s_t, 2)
            with eng.Fori(0, NP // 2) as i:
                for x in range(2):
                    c = i * 2 + x
                    for n in range(2):
                        eng.wait_ge(s_g, c * 2 + n + 3)
                        eng.wait_ge(s_p[2 + n], c + 1)
                        eng.tensor_tensor(split(t[:, n, :]), halves(psn[2 + n]), split(g[:, n, :]), ALU.mult).then_inc(s_t, 1)
                    eng.wait_ge(s_t, c * 2 + 4)
                    eng.tensor_tensor(m.mg[:, bass.ds(c, 1), :].rearrange("p a t -> p (a t)"), t[:, 0, :], t[:, 1, :],
                                      ALU.add).then_inc(s_mg, 1)
                    eng.wait_ge(s_mg, c + 1)


def phase_residual(nc, m, a):
    ctx, sb, ps, sem = open_phase(nc)
    with ctx:
        x2 = sb("rs_x2", [P, NT + 1, D])
        w = sb("rs_w", [P, NK, D])
        rt = sb("rs_rt", [P, NK, NG + NE])
        rb = sb("rs_rb", [P, NG + NE])
        gf = sb("rs_gf", [P, D])
        xn = sb("rs_xn", [P, 2, D])
        xnT = sb("rs_xnT", [P, NK, T])
        ms = sb("rs_ms", [P, NT + 1])
        fill = sb("rs_fill", [P, 2 * (ROUNDS + 1) * NE * CAP // P], I32)
        pso = [ps(f"rs_pso{n}", [P, 2, 512]) for n in range(2)]
        pst = ps("rs_pst", [P, 2, 512])
        psr = ps("rs_psr", [P, 512])
        s_x = [sem(f"o_in{j}") for j in range(NT + 1)]
        s_tok = [sem(f"o_tok{n}") for n in range(2)]
        (s_w, s_rt, s_o, s_x2, s_sq, s_ms, s_ln, s_rstd, s_xn, s_t, s_te, s_r, s_lg, s_zero, s_fill, s_tab, s_step) = \
            (sem("o_" + n) for n in ("w", "rt", "o", "x2", "sq", "ms", "ln", "rstd", "xn", "t", "te", "r", "lg",
                                     "zero", "fill", "tab", "step"))
        rows = [P] * NT + [TS]
        block = ctx.enter_context(nc.Block())

        @block.sync
        def _(eng):
            eng.dma_start(w[:, :, :], a["w_out"][0].rearrange("(k p) c -> p k c", p=P)).then_inc(s_w, 16)
            for j in range(NT):
                eng.dma_start(x2[:, j, :], a["x_prompt"][0, j * P:(j + 1) * P, :]).then_inc(s_x[j], 16)
            eng.dma_start(x2[0:TS, NT, :], a["x_sample"][:, 0, :]).then_inc(s_x[NT], 16)
            eng.dma_start(gf[:, :], a["norm_ffn_w"].partition_broadcast(P).rearrange("p l d -> p (l d)")).then_inc(s_rt, 16)
            eng.dma_start(rt[:, :, 0:NG], a["router_group"][0].rearrange("(k p) c -> p k c", p=P)).then_inc(s_rt, 16)
            eng.dma_start(rt[:, :, NG:NG + NE], a["router_expert"][0].rearrange("(k p) c -> p k c", p=P)).then_inc(s_rt, 16)
            eng.dma_start(rb[:, 0:NG], a["router_group_bias"].partition_broadcast(P).rearrange("p l d -> p (l d)")).then_inc(s_rt, 16)
            eng.dma_start(rb[:, NG:NG + NE], a["router_expert_bias"].partition_broadcast(P).rearrange("p l d -> p (l d)"))\
               .then_inc(s_rt, 16)
            eng.wait_ge(s_fill, 1)
            eng.dma_start(m.d_table.rearrange("(p n) c -> p (n c)", p=P), fill[:, :]).then_inc(s_tab, 16)
            for j, n in enumerate(rows):
                eng.wait_ge(s_xn, j + 1)
                eng.dma_start(m.d_tok[j * P:j * P + n, :], xn[0:n, j % 2, :]).then_inc(s_tok[j % 2], 16)
            for j, n in enumerate(rows):
                eng.dma_start(m.d_x2[j * P:j * P + n, :], x2[0:n, j, :]).then_inc(s_tab, 16)
            eng.wait_ge(s_tab, 16 * (NT + 2))
            for n in range(2):
                eng.wait_ge(s_tok[n], 16 * ((NT + 2 - n) // 2))

        @block.gpsimd
        def _(eng):
            eng.memset(fill[:, :], NOBODY).then_inc(s_fill, 1)

        @block.tensor
        def _(eng):
            eng.wait_ge(s_w, 16)
            for j, n in enumerate(rows):
                if j >= 2:
                    eng.wait_ge(s_x2, j - 1)
                for h in range(2):
                    for k in range(NK):
                        last = eng.matmul(pso[j % 2][0:n, h, :], m.mg[:, k, j * P:j * P + n], w[:, k, h * 512:(h + 1) * 512],
                                          start=(k == 0), stop=(k == NK - 1))
                last.then_inc(s_o, 1)
            eng.wait_ge(s_rt, 80)
            for j, n in enumerate(rows):
                eng.wait_ge(s_xn, j + 1)
                for h in range(2):
                    if j:
                        eng.wait_ge(s_te, 2 * (j - 1) + h + 1)
                    for k in range(4):
                        last = eng.transpose(pst[:, h, k * n:(k + 1) * n], xn[0:n, j % 2, (4 * h + k) * P:(4 * h + k + 1) * P],
                                             m.ident[0:n, 0:n])
                    last.then_inc(s_t, 1)
            for j, n in enumerate(rows):
                eng.wait_ge(s_te, 2 * j + 2)
                for k in range(NK):
                    last = eng.matmul(psr[0:n, j * (NG + NE):(j + 1) * (NG + NE)], xnT[:, k, j * P:j * P + n], rt[:, k, :],
                                      start=(k == 0), stop=(k == NK - 1))
            last.then_inc(s_r, 1)

        @block.scalar
        def _(eng):
            eng.wait_ge(s_zero, 1)
            for j, n in enumerate(rows):
                eng.wait_ge(s_x2, j + 1)
                if j >= 2:
                    eng.wait_ge(s_sq, j - 1)
                eng.activation(xn[0:n, j % 2, :], x2[0:n, j, :], ACT.Square, accum_out=ms[0:n, j:j + 1]).then_inc(s_sq, 1)
            eng.wait_ge(s_ms, 1)
            eng.activation(ms[:, :], ms[:, :], ACT.Ln).then_inc(s_ln, 1)
            eng.wait_ge(s_ln, 1)
            eng.activation(ms[:, :], ms[:, :], ACT.Exp, scale=-0.5).then_inc(s_rstd, 1)

        @block.vector
        def _(eng):
            eng.memset(ms[:, :], 1.0)
            eng.memset(m.logits[:, :, :], 0.0).then_inc(s_zero, 1)
            for j, n in enumerate(rows):
                eng.wait_ge(s_x[j], 16)
                eng.wait_ge(s_o, j + 1)
                row = x2[0:n, j, :].rearrange("p (h c) -> p h c", h=2)
                eng.tensor_tensor(row, pso[j % 2][0:n], row, ALU.add).then_inc(s_x2, 1)
            eng.wait_ge(s_sq, NT + 1)
            eng.tensor_scalar(ms[:, :], ms[:, :], 1.0 / D, RMS_EPS, ALU.mult, ALU.add).then_inc(s_ms, 1)
            eng.wait_ge(s_rstd, 1)
            eng.wait_ge(s_rt, 80)
            for j, n in enumerate(rows):
                if j >= 2:
                    eng.wait_ge(s_tok[j % 2], 16 * (j // 2))
                    eng.wait_ge(s_t, 2 * (j - 1))
                eng.scalar_tensor_tensor(out=xn[0:n, j % 2, :], in0=x2[0:n, j, :], scalar=ms[0:n, j:j + 1],
                                         in1=gf[0:n, :], op0=ALU.mult, op1=ALU.mult).then_inc(s_xn, 1)
                for h in range(2):
                    eng.wait_ge(s_t, 2 * j + h + 1)
                    eng.tensor_copy(xnT[:, 4 * h:4 * h + 4, j * P:j * P + n],
                                    pst[:, h, 0:4 * n].rearrange("p (k t) -> p k t", t=n)).then_inc(s_te, 1)
            eng.wait_ge(s_r, 1)
            for j, n in enumerate(rows):
                eng.tensor_tensor(m.logits[0:n, j, :], psr[0:n, j * (NG + NE):(j + 1) * (NG + NE)], rb[0:n, :], ALU.add)\
                   .then_inc(s_lg, 1)


NOBODY = 1 << 20


def phase_route(nc, m, a):
    ctx, sb, ps, sem = open_phase(nc)
    NTT = NT + 1
    with ctx:
        mx = sb("ro_mx", [P, NTT])
        pr = sb("ro_pr", [P, EG])
        g_oh = sb("ro_goh", [P, NTT, NG])
        gx = sb("ro_gx", [P, NTT, NG])
        q = sb("ro_q", [P, NTT, EG])
        q4 = sb("ro_q4", [P, NTT, NG])
        pg = sb("ro_pg", [P, NTT])
        masked = sb("ro_masked", [P, NTT, NG, EG])
        le = sb("ro_le", [P, NTT, EG])
        e_oh = sb("ro_eoh", [P, 2, NTT, EG])
        top = sb("ro_top", [P, 2, NTT])
        oh = sb("ro_oh", [P, 2, NTT, NE])
        member = sb("ro_member", [P, NTT, NE])
        base = sb("ro_base", [P, NE])
        slot = sb("ro_slot", [P, NTT, NE])
        over = sb("ro_over", [P, NTT, NE])
        ssum = sb("ro_ssum", [P, 2, NTT])
        pos = sb("ro_pos", [P, 2, NTT], I32)
        value = sb("ro_value", [P, 2, NTT, 2], I32)
        cnt = sb("ro_cnt", [P, 2])
        psr = ps("ro_ps", [P, 512])
        psc = ps("ro_psc", [P, 512])
        (s_step, s_io, s_d, s_x, s_m, s_pc, s_val, s_pos, s_sc, s_e) = \
            (sem("g_" + n) for n in ("step", "io", "d", "x", "m", "pc", "val", "pos", "sc", "e"))
        rows = [P] * NT + [TS]
        block = ctx.enter_context(nc.Block())

        @block.gpsimd
        def _(eng):
            for n in range(EG):
                eng.memset(pr[:, n:n + 1], float(EG - n))
            eng.iota(base[:, :], [[CAP, NE]], base=0, channel_multiplier=0, allow_small_or_imprecise_dtypes=True).then_inc(s_io, 1)
            for c in range(2):
                for n in range(2):
                    eng.iota(value[:, c, :, n], [[P, NTT]], base=n * c * T, channel_multiplier=1).then_inc(s_val, 1)
            eng.wait_ge(s_pos, 1)
            eng.wait_ge(s_val, 4)
            for j, n in enumerate(rows):
                for c in range(2):
                    eng.indirect_dma_start(out=m.d_table, out_offset=bass.IndirectOffsetOnAxis(ap=pos[0:n, c, j:j + 1], axis=0),
                                           in_=value[0:n, c, j, :], in_offset=None).then_inc(s_sc, 16)
            eng.wait_ge(s_sc, 16 * 2 * NTT)

        @block.tensor
        def _(eng):
            eng.wait_ge(s_m, 1)
            for j, n in enumerate(rows):
                out = psr[0:n, j * NE:(j + 1) * NE]
                for i in range(j):
                    eng.matmul(out, m.ones[:, 0:n], member[:, i, :], start=(i == 0), stop=False)
                eng.matmul(out, m.below[0:n, 0:n], member[0:n, j, :], start=(j == 0), stop=True)
            for j, n in enumerate(rows):
                last = eng.matmul(psc[:, 0:NE], m.ones[0:n, :], member[0:n, j, :], start=(j == 0), stop=(j == NT))
            last.then_inc(s_pc, 1)

        @block.scalar
        def _(eng):
            eng.wait_ge(s_d, 1)
            eng.activation(gx[:, :, :], gx[:, :, :], ACT.Exp).then_inc(s_x, 1)
            eng.wait_ge(s_e, 1)
            eng.activation(top[:, 1, :], top[:, 1, :], ACT.Exp).then_inc(s_x, 1)

        @block.vector
        def _(eng):
            step = Steps(eng, s_step)

            def do(ins):
                step.did(ins)
                step.wait()

            def first_max(src, width, best, out, scratch):
                full = [P, NTT, width]
                do(eng.tensor_reduce(best, src, AX.X, ALU.max))
                do(eng.tensor_tensor(scratch, src, best.unsqueeze(2).to_broadcast(full), ALU.is_ge))
                do(eng.tensor_tensor(scratch, scratch, pr[:, EG - width:EG].unsqueeze(1).to_broadcast(full), ALU.mult))
                do(eng.tensor_reduce(mx[:, :], scratch, AX.X, ALU.max))
                do(eng.tensor_tensor(out, scratch, mx[:, :].unsqueeze(2).to_broadcast(full), ALU.is_equal))

            eng.wait_ge(s_io, 1)
            gl = m.logits[:, :, 0:NG]
            first_max(gl, NG, pg[:, :], g_oh[:, :, :], q4[:, :, :])
            eng.tensor_tensor(gx[:, :, :], gl, pg[:, :].unsqueeze(2).to_broadcast([P, NTT, NG]), ALU.subtract).then_inc(s_d, 1)
            experts = m.logits[:, :, NG:NG + NE].rearrange("p t (g e) -> p t g e", g=NG)
            for j in range(NTT):
                step.did(eng.tensor_tensor(masked[:, j], experts[:, j], g_oh[:, j, :].unsqueeze(2).to_broadcast([P, NG, EG]), ALU.mult))
            step.wait()
            for j in range(NTT):
                step.did(eng.tensor_reduce(le[:, j, :], masked[:, j].rearrange("p g e -> p e g"), AX.X, ALU.add))
            step.wait()
            first_max(le[:, :, :], EG, top[:, 0, :], e_oh[:, 0], q[:, :, :])
            do(eng.scalar_tensor_tensor(out=le[:, :, :], in0=e_oh[:, 0], scalar=-3e38, in1=le[:, :, :], op0=ALU.mult, op1=ALU.add))
            first_max(le[:, :, :], EG, top[:, 1, :], e_oh[:, 1], q[:, :, :])
            do(eng.tensor_tensor(top[:, 1, :], top[:, 1, :], top[:, 0, :], ALU.subtract))
            eng.sem_inc(s_e, 1)
            for c in range(2):
                for j in range(NTT):
                    step.did(eng.tensor_tensor(oh[:, c, j, :].rearrange("p (g e) -> p g e", g=NG),
                                               g_oh[:, j, :].unsqueeze(2).to_broadcast([P, NG, EG]),
                                               e_oh[:, c, j, :].unsqueeze(1).to_broadcast([P, NG, EG]), ALU.mult))
            step.wait()
            do(eng.tensor_tensor(member[:, :, :], oh[:, 0], oh[:, 1], ALU.add))
            eng.sem_inc(s_m, 1)
            eng.wait_ge(s_x, 2)
            do(eng.tensor_reduce(pg[:, :], gx[:, :, :], AX.X, ALU.add))
            do(eng.scalar_tensor_tensor(out=pg[:, :], in0=top[:, 1, :], scalar=1.0, in1=pg[:, :], op0=ALU.add, op1=ALU.mult))
            do(eng.reciprocal(m.weight[:, 0, :], pg[:, :]))
            do(eng.tensor_tensor(m.weight[:, 1, :], m.weight[:, 0, :], top[:, 1, :], ALU.mult))
            eng.wait_ge(s_pc, 1)
            rank = psr[:, 0:NTT * NE].rearrange("p (t e) -> p t e", e=NE)
            do(eng.memset(slot[:, :, :], 0.0))
            do(eng.tensor_copy(slot[:, 0:NT, :], rank[:, 0:NT, :]))
            do(eng.tensor_copy(slot[0:TS, NT, :], rank[0:TS, NT, :]))
            do(eng.tensor_scalar(over[:, :, :], slot[:, :, :], float(CAP), None, ALU.is_ge))
            for n in range(2, ROUNDS):
                do(eng.scalar_tensor_tensor(out=over[:, :, :], in0=slot[:, :, :], scalar=float(n * CAP), in1=over[:, :, :],
                                            op0=ALU.is_ge, op1=ALU.add))
            do(eng.scalar_tensor_tensor(out=slot[:, :, :], in0=over[:, :, :], scalar=float((NE - 1) * CAP), in1=slot[:, :, :],
                                        op0=ALU.mult, op1=ALU.add))
            do(eng.tensor_tensor(slot[:, :, :], slot[:, :, :], base[:, :].unsqueeze(1).to_broadcast([P, NTT, NE]), ALU.add))
            for c in range(2):
                do(eng.tensor_tensor(over[:, :, :], slot[:, :, :], oh[:, c], ALU.mult))
                do(eng.tensor_reduce(ssum[:, c, :], over[:, :, :], AX.X, ALU.add))
            do(eng.tensor_copy(pos[:, :, :], ssum[:, :, :]))
            eng.sem_inc(s_pos, 1)
            do(eng.tensor_reduce(cnt[:, 0:1], psc[:, 0:NE], AX.X, ALU.max))
            do(eng.memset(cnt[:, 1:2], float(NE // XG)))
            for n in range(1, ROUNDS):
                do(eng.tensor_scalar(mx[:, 0:1], cnt[:, 0:1], float(n * CAP), float(NE // XG), ALU.is_gt, ALU.mult))
                do(eng.tensor_tensor(cnt[:, 1:2], cnt[:, 1:2], mx[:, 0:1], ALU.add))
            do(eng.tensor_copy(m.passes[:, 0:1], cnt[:, 1:2]))
            do(eng.tensor_scalar(cnt[:, 1:2], cnt[:, 1:2], float(XG) / NE, None, ALU.mult))
            do(eng.tensor_copy(m.passes[:, 1:2], cnt[:, 1:2]))


XG = 4


def phase_experts(nc, m, a):
    ctx, sb, ps, sem = open_phase(nc)
    with ctx:
        wgu = sb("ex_wgu", [P, XG, NK, 2 * DE])
        wd = sb("ex_wd", [P, XG, DE // P, D])
        idx = sb("ex_idx", [P, 2, XG, 2], I32)
        xg = sb("ex_xg", [P, XG, D])
        xgT = sb("ex_xgT", [P, 2, NK, P])
        sg = sb("ex_sg", [P, 2, DE])
        hT = sb("ex_hT", [P, 2, DE // P, P])
        yo = sb("ex_yo", [P, 2, D])
        pst = ps("ex_pst", [P, 2, 512])
        psg = [ps(f"ex_psg{n}", [P, 512]) for n in range(2)]
        psh = ps("ex_psh", [P, 512])
        psd = ps("ex_psd", [P, 2, 512])
        s_w = [sem(f"e_w{n}") for n in range(XG)]
        s_wd = [sem(f"e_wd{n}") for n in range(XG)]
        s_x = [sem(f"e_x{n}") for n in range(XG)]
        s_y = [sem(f"e_y{n}") for n in range(2)]
        (s_idx, s_t, s_te, s_gu, s_sg, s_h, s_ht, s_hte, s_d, s_ya, s_yb, s_xz, s_gate) = \
            (sem("e_" + n) for n in ("idx", "t", "te", "gu", "sg", "h", "ht", "hte", "d", "ya", "yb", "xz", "gate"))
        block = ctx.enter_context(nc.Block())

        def passes(eng):
            return eng.value_load(m.passes[0:1, 0:1], min_val=NE // XG, max_val=ROUNDS * NE // XG)

        @block.sync
        def _(eng):
            rounds = eng.value_load(m.passes[0:1, 1:2], min_val=1, max_val=ROUNDS)
            with eng.Fori(0, rounds) as r:
                with eng.Fori(0, NE // XG) as g:
                    q = r * (NE // XG) + g
                    for x in range(XG):
                        e = bass.ds(g * XG + x, 1)
                        eng.wait_ge(s_gu, q * XG + (x + 1))
                        for n, src in enumerate((a["moe_w_gate"], a["moe_w_up"])):
                            eng.dma_start(wgu[:, x, :, n * DE:(n + 1) * DE],
                                          src[0, e].rearrange("a (k p) f -> p (a k) f", p=P)).then_inc(s_w[x], 16)
                        eng.wait_ge(s_d, q * XG + (x + 1))
                        eng.dma_start(wd[:, x], a["moe_w_down"][0, e].rearrange("a (k p) c -> p (a k) c", p=P)).then_inc(s_wd[x], 16)

        @block.gpsimd
        def _(eng):
            def list_of(n, buf):
                eng.dma_start(idx[:, buf], m.d_table[bass.ds(n * (XG * CAP), XG * CAP), :].rearrange("(x s) c -> s x c", s=CAP))\
                   .then_inc(s_idx, 16)

            def gather(buf, x):
                eng.indirect_dma_start(out=xg[:, x, :], out_offset=None, in_=m.d_tok,
                                       in_offset=bass.IndirectOffsetOnAxis(ap=idx[:, buf, x, 0:1], axis=0),
                                       bounds_check=T - 1, oob_is_err=False).then_inc(s_x[x], 16)

            n = passes(eng)
            eng.memset(xg[:, :, :], 0.0).then_inc(s_xz, 1)
            list_of(0, 0)
            eng.wait_ge(s_xz, 1)
            for x in range(2):
                eng.dma_start(yo[0:1, x, 0:P], m.ident[0:1, :]).then_inc(s_y[x], 16)
            eng.wait_ge(s_idx, 16)
            for x in range(XG):
                gather(0, x)
            with eng.Fori(0, n, 2) as q:
                for buf in range(2):
                    for x in range(2):
                        eng.wait_ge(s_y[x], q * (8 * XG) + (buf * 8 * XG + 16))
                    list_of(q + (buf + 1), 1 - buf)
                    for x in range(XG):
                        k = q * XG + (buf * XG + x)
                        eng.wait_ge(s_ya, k + 2)
                        eng.wait_ge(s_yb, k + 2)
                        eng.sem_inc(s_gate, 1)
                        eng.indirect_dma_start(out=m.d_y2, out_offset=bass.IndirectOffsetOnAxis(ap=idx[:, buf, x, 1:2], axis=0),
                                               in_=yo[:, x % 2, :], in_offset=None, bounds_check=2 * T - 1, oob_is_err=False)\
                           .then_inc(s_y[x % 2], 16)
                        if x == 0:
                            eng.wait_ge(s_idx, q * 16 + (buf + 2) * 16)
                            eng.sem_inc(s_gate, 1)
                        gather(1 - buf, x)
            for x in range(XG):
                eng.wait_ge(s_x[x], n * 16 + 16)
            for x in range(2):
                eng.wait_ge(s_y[x], n * (8 * XG) + 16)

        @block.tensor
        def _(eng):
            eng.sem_inc(s_gu, XG)
            eng.sem_inc(s_d, XG)
            n = passes(eng)
            with eng.Fori(0, n) as q:
                def turn(x):
                    k = q * XG + x
                    eng.wait_ge(s_x[x], q * 16 + 16)
                    eng.wait_ge(s_te, k * 2 + 2)
                    for kk in range(NK):
                        last = eng.transpose(pst[:, kk // 4, (kk % 4) * P:(kk % 4 + 1) * P], xg[:, x, kk * P:(kk + 1) * P],
                                             m.ident[:, :])
                    last.then_inc(s_t, 1)

                def gate_up(x):
                    k = q * XG + x
                    eng.wait_ge(s_te, k * 2 + 4)
                    eng.wait_ge(s_w[x], q * 32 + 32)
                    eng.wait_ge(s_h, k + 1)
                    for kk in range(NK):
                        last = eng.matmul(psg[x % 2][:, :], xgT[:, x % 2, kk, :], wgu[:, x, kk, :],
                                          start=(kk == 0), stop=(kk == NK - 1))
                    last.then_inc(s_gu, 1)

                def turn_h(x):
                    k = q * XG + x
                    eng.wait_ge(s_h, k + 3)
                    eng.wait_ge(s_hte, k + 1)
                    for kk in range(DE // P):
                        last = eng.transpose(psh[:, kk * P:(kk + 1) * P], sg[:, x % 2, kk * P:(kk + 1) * P], m.ident[:, :])
                    last.then_inc(s_ht, 1)

                def down(x):
                    k = q * XG + x
                    eng.wait_ge(s_hte, k + 2)
                    eng.wait_ge(s_wd[x], q * 16 + 16)
                    eng.wait_ge(s_ya, k + 1)
                    eng.wait_ge(s_yb, k + 1)
                    for h in range(2):
                        for kk in range(DE // P):
                            last = eng.matmul(psd[:, h, :], hT[:, x % 2, kk, :], wd[:, x, kk, h * 512:(h + 1) * 512],
                                              start=(kk == 0), stop=(kk == DE // P - 1))
                    last.then_inc(s_d, 1)

                turn(0)
                for x in range(XG):
                    gate_up(x)
                    if x < XG - 1:
                        turn(x + 1)
                    if x:
                        down(x - 1)
                    turn_h(x)
                down(XG - 1)

        @block.scalar
        def _(eng):
            eng.sem_inc(s_te, 1)
            eng.sem_inc(s_hte, 1)
            eng.sem_inc(s_ya, 1)
            n = passes(eng)
            with eng.Fori(0, n) as q:
                def rows(x):
                    eng.wait_ge(s_t, q * XG + (x + 1))
                    eng.activation(xgT[:, x % 2, 0:4, :], pst[:, 0, :].rearrange("p (k s) -> p k s", s=P), ACT.Copy).then_inc(s_te, 1)

                def out(x):
                    k = q * XG + x
                    eng.wait_ge(s_d, k + (XG + 1))
                    eng.wait_ge(s_y[x % 2], q * (8 * XG) + (x // 2 + 1) * 16)
                    eng.activation(yo[:, x % 2, 0:512], psd[:, 0, :], ACT.Copy).then_inc(s_ya, 1)

                rows(0)
                for x in range(XG):
                    k = q * XG + x
                    eng.wait_ge(s_gu, k + (XG + 1))
                    eng.activation(sg[:, x % 2, :], psg[x % 2][:, 0:DE], ACT.Silu).then_inc(s_sg, 1)
                    if x < XG - 1:
                        rows(x + 1)
                    if x:
                        out(x - 1)
                    eng.wait_ge(s_ht, k + 1)
                    eng.activation(hT[:, x % 2], psh[:, 0:DE].rearrange("p (k s) -> p k s", s=P), ACT.Copy).then_inc(s_hte, 1)
                out(XG - 1)

        @block.vector
        def _(eng):
            eng.sem_inc(s_te, 1)
            eng.sem_inc(s_h, 2)
            eng.sem_inc(s_yb, 1)
            n = passes(eng)
            with eng.Fori(0, n) as q:
                def rows(x):
                    eng.wait_ge(s_t, q * XG + (x + 1))
                    eng.tensor_copy(xgT[:, x % 2, 4:8, :], pst[:, 1, :].rearrange("p (k s) -> p k s", s=P)).then_inc(s_te, 1)

                def out(x):
                    k = q * XG + x
                    eng.wait_ge(s_d, k + (XG + 1))
                    eng.wait_ge(s_y[x % 2], q * (8 * XG) + (x // 2 + 1) * 16)
                    eng.tensor_copy(yo[:, x % 2, 512:D], psd[:, 1, :]).then_inc(s_yb, 1)

                rows(0)
                for x in range(XG):
                    eng.wait_ge(s_sg, q * XG + (x + 1))
                    eng.tensor_tensor(sg[:, x % 2, :], psg[x % 2][:, DE:2 * DE], sg[:, x % 2, :], ALU.mult).then_inc(s_h, 1)
                    if x < XG - 1:
                        rows(x + 1)
                    if x:
                        out(x - 1)
                out(XG - 1)


def phase_final(nc, m, a):
    ctx, sb, ps, sem = open_phase(nc)
    with ctx:
        x2 = sb("fi_x2", [P, NT + 1, D])
        y = sb("fi_y", [P, NT + 1, 2, D])
        gf = sb("fi_gf", [P, D])
        ms = sb("fi_ms", [P, NT + 1])
        sq = sb("fi_sq", [P, 2, D])
        s_y = [sem(f"f_y{j}") for j in range(NT + 1)]
        s_gf, s_x, s_sq, s_ms, s_ln, s_rs, s_o, s_out, s_zero, s_step = \
            (sem("f_" + n) for n in ("gf", "x", "sq", "ms", "ln", "rs", "o", "out", "zero", "step"))
        rows = [P] * NT + [TS]
        block = ctx.enter_context(nc.Block())

        @block.sync
        def _(eng):
            for j, n in enumerate(rows):
                eng.dma_start(x2[0:n, j, :], m.d_x2[j * P:j * P + n, :]).then_inc(s_y[j], 16)
                eng.dma_start(y[0:n, j], m.d_y2.rearrange("(c t) d -> t c d", c=2)[j * P:j * P + n]).then_inc(s_y[j], 16)
            eng.dma_start(gf[:, :], a["norm_final_w"].partition_broadcast(P)).then_inc(s_gf, 16)
            for j, n in enumerate(rows):
                eng.wait_ge(s_o, j + 1)
                dst = a["y_prompt"][0, j * P:(j + 1) * P, :] if j < NT else a["y_sample"][:, 0, :]
                eng.dma_start(dst, x2[0:n, j, :]).then_inc(s_out, 16)
            eng.wait_ge(s_out, 16 * (NT + 1))

        @block.vector
        def _(eng):
            step = Steps(eng, s_step)
            eng.memset(ms[:, :], 1.0).then_inc(s_zero, 1)
            for j, n in enumerate(rows):
                eng.wait_ge(s_y[j], 32)
                step.did(eng.scalar_tensor_tensor(out=x2[0:n, j, :], in0=y[0:n, j, 0, :], scalar=m.weight[0:n, 0, j:j + 1],
                                                  in1=x2[0:n, j, :], op0=ALU.mult, op1=ALU.add))
                step.wait()
                eng.scalar_tensor_tensor(out=x2[0:n, j, :], in0=y[0:n, j, 1, :], scalar=m.weight[0:n, 1, j:j + 1],
                                         in1=x2[0:n, j, :], op0=ALU.mult, op1=ALU.add).then_inc(s_x, 1)
            eng.wait_ge(s_sq, NT + 1)
            eng.tensor_scalar(ms[:, :], ms[:, :], 1.0 / D, RMS_EPS, ALU.mult, ALU.add).then_inc(s_ms, 1)
            eng.wait_ge(s_rs, 1)
            eng.wait_ge(s_gf, 16)
            for j, n in enumerate(rows):
                eng.scalar_tensor_tensor(out=x2[0:n, j, :], in0=x2[0:n, j, :], scalar=ms[0:n, j:j + 1], in1=gf[0:n, :],
                                         op0=ALU.mult, op1=ALU.mult).then_inc(s_o, 1)

        @block.scalar
        def _(eng):
            eng.wait_ge(s_zero, 1)
            for j, n in enumerate(rows):
                eng.wait_ge(s_x, j + 1)
                if j >= 2:
                    eng.wait_ge(s_sq, j - 1)
                eng.activation(sq[0:n, j % 2, :], x2[0:n, j, :], ACT.Square, accum_out=ms[0:n, j:j + 1]).then_inc(s_sq, 1)
            eng.wait_ge(s_ms, 1)
            eng.activation(ms[:, :], ms[:, :], ACT.Ln).then_inc(s_ln, 1)
            eng.wait_ge(s_ln, 1)
            eng.activation(ms[:, :], ms[:, :], ACT.Exp, scale=-0.5).then_inc(s_rs, 1)


INPUTS = ('x_prompt', 'x_sample', 'state_wkv', 'state_shift', 'norm_mix_w', 'w_in', 'sgu_ln_w', 'sgu_ln_b', 'sgu_w_s',
          'sgu_b', 'rwkv_mu', 'w_lora_up', 'w_bias', 'a_lora_up', 'a_bias', 'g_lora_up', 'k_k', 'k_a', 'r_k', 'lnx_w',
          'lnx_b', 'proj_a', 'proj_b', 'w_out', 'norm_ffn_w', 'router_group', 'router_group_bias', 'router_expert',
          'router_expert_bias', 'moe_w_gate', 'moe_w_up', 'moe_w_down', 'norm_final_w')
OUTPUTS = (("y_prompt", (1, TP, D)), ("y_sample", (TS, 1, D)), ("new_wkv_prompt", (1, 1, 2 * NP, HD, HD)),
           ("new_shift_prompt", (1, 1, SHIFT)), ("new_wkv_sample", (1, TS, 2 * NP, HD, HD)),
           ("new_shift_sample", (1, TS, SHIFT)), ("new_chunk_v_sample", (1, TS, 1, NP, P)))


class Memory:
    pass


def build(nc, a):
    m = Memory()
    m.flat = {name: a[name].rearrange("l h d -> (l h d)" if name in ("r_k", "lnx_w", "lnx_b") else "l d -> (l d)")
              for name in VEC_NAMES}
    m.d_sample = nc.dram_tensor("d_sample", (6, TS, D), F32, kind="Internal").ap()
    m.d_y = nc.dram_tensor("d_y", (TS, D), F32, kind="Internal").ap()
    m.d_tok = nc.dram_tensor("d_tok", (T, D), F32, kind="Internal").ap()
    m.d_x2 = nc.dram_tensor("d_x2", (T, D), F32, kind="Internal").ap()
    m.d_table = nc.dram_tensor("d_table", ((ROUNDS + 1) * NE * CAP, 2), I32, kind="Internal").ap()
    m.d_y2 = nc.dram_tensor("d_y2", (2 * T, D), F32, kind="Internal").ap()

    def scope():
        ctx = ExitStack()
        return ctx, lambda name, shape, dt=F32: ctx.enter_context(nc.sbuf_tensor(name, shape, dt))

    whole, sb = scope()
    with whole:
        m.s_sv = whole.enter_context(nc.semaphore("s_sv"))
        m.ident, m.headones, m.causal, m.below, m.ones, m.level1t = \
            (sb(n, [P, P]) for n in ("ident", "headones", "causal", "below", "ones", "level1t"))
        m.levels = sb("levels", [P, 1 + len(LEVELS), P])
        m.vecs = sb("vecs", [P, NVEC])
        m.shift_prev = sb("shift_prev", [P, NSH, TS])
        m.shift_last = sb("shift_last", [P, TS + 1, NSH])
        m.half_bias = sb("half_bias", [P, 2, NP])
        m.lw_sample = sb("lw_sample", [P, NP, TS])
        m.logits = sb("logits", [P, NT + 1, NG + NE])
        m.weight = sb("weight", [P, 2, NT + 1])
        m.passes = sb("passes", [P, 2], I32)
        phase_constants(nc, m)
        mixer, sb = scope()
        with mixer:
            m.lora_in = sb("lora_in", [P, T])
            m.gate_in = sb("gate_in", [P, T])
            m.sv = sb("sv", [P, 6, HD])
            m.xT = sb("xT", [P, NK, T])
            m.r = sb("r_all", [P, NP, T])
            m.bonus = sb("bonus_all", [P, NP, T])
            rwkv, sb = scope()
            with rwkv:
                m.k, m.kk, m.br, m.v = (sb(n + "_all", [P, NP, T]) for n in ("k", "kk", "br", "v"))
                m.cum = sb("cum_all", [P, NP, NC * (CH + 1)])
                phase_tokens(nc, m, a)
                phase_lora_inputs(nc, m, a)
                norm, sb = scope()
                with norm:
                    m.kk_norm = sb("kk_norm", [P, NP, T])
                    phase_rkv(nc, m, a)
                phase_chunks(nc, m, a)
                phase_sample_vectors(nc, m, a)
            late, sb = scope()
            with late:
                m.mg = sb("mg", [P, NP, T])
                m.ya = sb("ya", [P, NP, T])
                state, sb = scope()
                with state:
                    m.wst = sb("wst", [P, NP, P])
                    m.w00 = sb("w00", [P, NP])
                    m.S = sb("S", [P, HD, HD])
                    phase_spatial_weights(nc, m, a)
                    phase_gating(nc, m, a)
                with nc.sbuf_tensor("yb", [P, NP, T], F32) as m.yb:
                    phase_head_norm(nc, m, a)
                    phase_merge(nc, m, a)
                phase_residual(nc, m, a)
        phase_route(nc, m, a)
        phase_experts(nc, m, a)
        phase_final(nc, m, a)


def kernel(**inputs):
    import numpy as _np
    import concourse.bacc as _bacc
    from concourse.bass_utils import run_bass_kernel_spmd as _run

    nc = _bacc.Bacc("TRN2", target_bir_lowering=False, num_devices=1)
    arrays, a = {}, {}
    for name in INPUTS:
        arrays[f"in_{name}"] = _np.ascontiguousarray(inputs[name])
        a[name] = nc.dram_tensor(f"in_{name}", arrays[f"in_{name}"].shape, F32, kind="ExternalInput").ap()
    for name, shape in OUTPUTS:
        a[name] = nc.dram_tensor(f"out_{name}", shape, F32, kind="ExternalOutput").ap()
    build(nc, a)
    r = _run(nc, [arrays], core_ids=[0])
    return tuple(r.results[0][f"out_{name}"] for name, _ in OUTPUTS)
```

```python
import math
from contextlib import ExitStack

import concourse.bass as bass
from concourse import mybir

F32 = mybir.dt.float32
I32 = mybir.dt.int32
ALU = mybir.AluOpType
ACT = mybir.ActivationFunctionType
AX = mybir.AxisListType

P = 128
D = 1024
NK = D // P
TP = 512
TS = 8
T = TP + TS
TH = T // 2
NT = TP // P
HD = 64
NP = D // P
CH = 64
NC = TP // CH
G = 2
GP = NP // G
LEVELS = (2, 4, 8, 16, 32)
OFF_V = D
OFF_SHIFT = 2 * D
SHIFT = 3 * D + 256
NSH = SHIFT // P
OFF_GA = OFF_SHIFT + SHIFT
OFF_GB = OFF_GA + D
NE = 32
NG = 4
EG = NE // NG
DE = 256
CAP = P
ROUNDS = -(-T // CAP)
DECAY = -math.exp(-0.5)
RMS_EPS, LN_EPS, GN_EPS = 1e-6, 1e-5, 64e-5

VEC_NAMES = ("norm_mix_w", "w_bias", "a_bias", "k_k", "k_a", "r_k", "lnx_w", "lnx_b", "norm_ffn_w", "rwkv_mu")
VEC = {name: (n * NP, NSH if name == "rwkv_mu" else NP) for n, name in enumerate(VEC_NAMES)}
NVEC = (len(VEC_NAMES) - 1) * NP + NSH


class Steps:

    def __init__(self, eng, sem, base=0):
        self.eng, self.sem, self.n, self.base = eng, sem, 0, base

    def did(self, ins):
        ins.then_inc(self.sem, 1)
        self.n += 1

    def wait(self):
        self.eng.wait_ge(self.sem, self.base + self.n)


RSQRT_STEPS = 2 + 3 * 3
RKV_STEPS = 2 * (3 * 3 + 2 + 3 + 2)
GATING_STEPS = 2 * ((NT + 1) + (NT + 1) + RSQRT_STEPS + NT + 3 + 2)


def rsqrt(eng, step, y, x, t):
    bits = y.bitcast(I32)
    step.did(eng.tensor_scalar(bits, x.bitcast(I32), 1, None, ALU.logical_shift_right))
    step.wait()
    step.did(eng.tensor_scalar(bits, bits, -1.0, float(0x5f3759df), ALU.mult, ALU.add))
    step.wait()
    for _ in range(3):
        step.did(eng.tensor_tensor(t, y, y, ALU.mult))
        step.wait()
        step.did(eng.scalar_tensor_tensor(out=t, in0=t, scalar=-0.5, in1=x, op0=ALU.mult, op1=ALU.mult))
        step.wait()
        step.did(eng.scalar_tensor_tensor(out=y, in0=t, scalar=1.5, in1=y, op0=ALU.add, op1=ALU.mult))
        step.wait()


def halves(ap):
    return ap[:, :, 0:TH]


def split(ap):
    return ap.rearrange("p (a t) -> p a t", a=2)


def vec(m, name):
    start, rows = VEC[name]
    return m.vecs[:, start:start + rows]


def open_phase(nc):
    ctx, sems = ExitStack(), []

    def sem(name):
        sems.append(nc.alloc_semaphore(name))
        return sems[-1]

    def close():
        nc.clear_and_free_semaphores(sems)
        nc.all_engine_barrier()

    ctx.callback(close)
    return ctx, (lambda n, s, d=F32: ctx.enter_context(nc.sbuf_tensor(n, s, d))), \
        (lambda n, s, d=F32: ctx.enter_context(nc.psum_tensor(n, s, d))), sem


def constants(eng, m, step, s_ident):
    def select(view, op, base, pattern, cm, fill):
        step.wait()
        step.did(eng.affine_select(out=view, in_=view, compare_op=op, fill=fill, base=base,
                                   pattern=pattern, channel_multiplier=cm))

    step.did(eng.memset(m.ident[:, :], 0.0))
    step.did(eng.memset(m.levels[:, :, :], 0.0))
    step.did(eng.memset(m.level1t[:, :], 0.0))
    step.did(eng.memset(m.headones[:, :], 0.0))
    step.did(eng.memset(m.below[:, :], 1.0))
    step.did(eng.memset(m.ones[:, :], 1.0))
    step.did(eng.memset(m.causal[:, :], 1.0))
    select(m.ident[:, :], ALU.not_equal, 0, [[-1, P]], 1, 1.0)
    step.wait()
    eng.sem_inc(s_ident, 1)
    step.wait()
    step.did(eng.memset(m.headones[0:HD, 0:HD], 1.0))
    step.did(eng.memset(m.headones[HD:P, HD:P], 1.0))
    select(m.below[:, :], ALU.is_gt, 0, [[1, P]], -1, 0.0)
    for half in range(2):
        rows = m.causal[HD * half:HD * (half + 1), :]
        select(rows[:, 0:CH], ALU.is_gt, 0, [[1, CH]], -1, 0.0)
        select(rows[:, CH:P], ALU.is_ge, 0, [[1, CH]], -1, 0.0)
    for n, b in enumerate((1,) + LEVELS):
        odd = m.levels[:, n, :].rearrange("p (a two b) -> p a two b", two=2, b=b)[:, :, 1, :]
        step.wait()
        step.did(eng.memset(odd, 1.0))
        select(odd, ALU.is_ge, 0, [[-2 * b, P // (2 * b)], [0, b]], 1, 0.0)
        select(odd, ALU.is_ge, b - 1, [[2 * b, P // (2 * b)], [0, b]], -1, 0.0)
        select(m.levels[:, n, :], ALU.not_equal, 0, [[-1, P]], 1, 1.0)
    even = m.level1t[:, :].rearrange("p (a two) -> p a two", two=2)[:, :, 0]
    select(even, ALU.not_equal, -1, [[-2, P // 2]], 1, 1.0)
    select(m.level1t[:, :], ALU.not_equal, 0, [[-1, P]], 1, 1.0)
    step.wait()


def phase_tokens(nc, m, a):
    ctx, sb, ps, sem = open_phase(nc)
    with ctx:
        x = sb("x_tok", [P, NT + 1, D])
        sq = sb("x_sq", [P, D])
        rows = sb("vec_rows", [P, P])
        shift_rows = sb("shift_rows", [TS, SHIFT])
        ms = sb("x_ms", [P, NT + 1])
        rstd = sb("x_rstd", [P, NT + 1])
        half = sb("x_half", [P, NT + 1])
        psx = ps("ps_x", [P, 4, 512])
        psv = ps("ps_v", [P, 512])
        pss = ps("ps_s", [P, 512])
        s_x = [sem(f"t_x{j}") for j in range(NT + 1)]
        s_vec, s_shift, s_sq, s_ms, s_rstd, s_scaled, s_xt, s_xe, s_zero = \
            (sem("t_" + n) for n in ("vec", "shift", "sq", "ms", "rstd", "scaled", "xt", "xe", "zero"))
        s_vt, s_ve, s_st, s_se = (sem("t_" + n) for n in ("vt", "ve", "st", "se"))
        s_ident, s_const = sem("t_ident"), sem("t_const")
        block = ctx.enter_context(nc.Block())

        @block.gpsimd
        def _(eng):
            constants(eng, m, Steps(eng, s_const), s_ident)

        @block.sync
        def _(eng):
            for j in range(NT):
                eng.dma_start(x[:, j, :], a["x_prompt"][0, j * P:(j + 1) * P, :]).then_inc(s_x[j], 16)
            eng.dma_start(x[0:TS, NT, :], a["x_sample"][:, 0, :]).then_inc(s_x[NT], 16)

        @block.scalar
        def _(eng):
            for name, (start, n) in VEC.items():
                ap = m.flat[name]
                eng.dma_start(rows[start:start + n, :], ap.rearrange("(r c) -> r c", c=P)).then_inc(s_vec, 16)
            eng.dma_start(shift_rows[:, :], a["state_shift"][0]).then_inc(s_shift, 16)
            eng.wait_ge(s_zero, 1)
            for j in range(NT + 1):
                n = P if j < NT else TS
                eng.wait_ge(s_x[j], 16)
                if j:
                    eng.wait_ge(s_sq, j)
                eng.activation(sq[0:n, :], x[0:n, j, :], ACT.Square, accum_out=ms[0:n, j:j + 1]).then_inc(s_sq, 1)

        @block.vector
        def _(eng):
            eng.memset(ms[:, :], 1.0).then_inc(s_zero, 1)
            eng.wait_ge(s_vt, 1)
            eng.tensor_copy(m.vecs[:, :], psv[:, 0:NVEC]).then_inc(s_ve, 1)
            eng.wait_ge(s_st, 1)
            eng.tensor_copy(m.shift_prev[:, :, :], pss[:, 0:NSH * TS].rearrange("p (c t) -> p c t", t=TS)).then_inc(s_se, 1)
            eng.wait_ge(s_sq, NT + 1)
            eng.tensor_scalar(ms[:, :], ms[:, :], 1.0 / D, RMS_EPS, ALU.mult, ALU.add).then_inc(s_ms, 1)
            eng.wait_ge(s_ms, 1)
            rsqrt(eng, Steps(eng, s_rstd), rstd[:, :], ms[:, :], half[:, :])
            for j in range(NT + 1):
                n = P if j < NT else TS
                eng.tensor_scalar(x[0:n, j, :], x[0:n, j, :], rstd[0:n, j:j + 1], None, ALU.mult).then_inc(s_scaled, 1)
            eng.wait_ge(s_ve, 1)
            for j in range(NT + 1):
                n = P if j < NT else TS
                for h in range(2):
                    eng.wait_ge(s_xt, 2 * j + h + 1)
                    w = vec(m, "norm_mix_w")[:, 4 * h:4 * h + 4].unsqueeze(2).to_broadcast([P, 4, n])
                    src = psx[:, 2 * (j % 2) + h, 0:4 * n].rearrange("p (k t) -> p k t", t=n)
                    eng.tensor_tensor(m.xT[:, 4 * h:4 * h + 4, j * P:j * P + n], src, w, ALU.mult).then_inc(s_xe, 1)

        @block.tensor
        def _(eng):
            eng.wait_ge(s_ident, 1)
            eng.wait_ge(s_vec, 16 * len(VEC))
            eng.transpose(psv[:, 0:NVEC], rows[0:NVEC, :], m.ident[0:NVEC, 0:NVEC]).then_inc(s_vt, 1)
            eng.wait_ge(s_shift, 16)
            for c in range(NSH):
                last = eng.transpose(pss[:, c * TS:(c + 1) * TS], shift_rows[:, c * P:(c + 1) * P], m.ident[0:TS, 0:TS])
            last.then_inc(s_st, 1)
            for j in range(NT + 1):
                n = P if j < NT else TS
                eng.wait_ge(s_scaled, j + 1)
                for h in range(2):
                    if j >= 2:
                        eng.wait_ge(s_xe, 2 * (j - 2) + h + 1)
                    for k in range(4):
                        kk = 4 * h + k
                        last = eng.transpose(psx[:, 2 * (j % 2) + h, k * n:(k + 1) * n], x[0:n, j, kk * P:(kk + 1) * P],
                                             m.ident[0:n, 0:n])
                    last.then_inc(s_xt, 1)


def shift_mix(eng, step, m, cols, diff, out, mu, prev):
    step.did(eng.tensor_tensor(diff[:, 0:TP], cols[:, 0:TP], cols[:, 1:TP + 1], ALU.subtract))
    step.did(eng.tensor_tensor(diff[:, TP:T], prev, cols[:, TP + 1:T + 1], ALU.subtract))
    step.wait()
    step.did(eng.scalar_tensor_tensor(out=out, in0=diff[:, :], scalar=mu, in1=cols[:, 1:T + 1],
                                      op0=ALU.mult, op1=ALU.add))
    step.wait()


def project(eng, out, weights, xT):
    for h in range(2):
        for k in range(NK):
            last = eng.matmul(out[:, h, 0:TH], weights[:, k, :], xT[:, k, h * TH:(h + 1) * TH],
                              start=(k == 0), stop=(k == NK - 1))
    return last


def w_cols(w_in, at):
    return w_in[0, :, at].rearrange("(k p) c -> p k c", p=P)


def phase_lora_inputs(nc, m, a):
    ctx, sb, ps, sem = open_phase(nc)
    with ctx:
        w = sb("lw_w", [P, 2, NK, P])
        diff = sb("lw_diff", [P, T])
        xs = sb("lw_xs", [P, 2, T])
        cols = sb("lw_cols", [P, 2, T + 1])
        ws = sb("sw_ws", [P, NP, P])
        psp = ps("lw_ps", [P, 2, 2, 512])
        psw = ps("sw_ps", [P, 2, 512])
        ps0 = ps("sw_ps0", [P, 512])
        s_ws, s_wm, s_wt, s_we = (sem("w_" + n) for n in ("ws", "wm", "t", "e"))
        s_w = [sem("l_w0"), sem("l_w1")]
        s_p, s_e, s_step, s_xs, s_t = (sem("l_" + n) for n in ("p", "e", "step", "xs", "t"))
        block = ctx.enter_context(nc.Block())

        @block.sync
        def _(eng):
            for n in range(2):
                at = OFF_SHIFT + 3 * D + n * P
                eng.dma_start(w[:, n], w_cols(a["w_in"], slice(at, at + P))).then_inc(s_w[n], 16)
            eng.dma_start(ws[:, :, :], a["sgu_w_s"][0].rearrange("h t s -> t h s")).then_inc(s_ws, 16)

        @block.gpsimd
        def _(eng):
            eng.wait_ge(s_ws, 16)
            eng.affine_select(out=ws[:, :, :], in_=ws[:, :, :], compare_op=ALU.is_ge, fill=0.0, base=0,
                              pattern=[[0, NP], [-1, P]], channel_multiplier=1).then_inc(s_wm, 1)

        @block.tensor
        def _(eng):
            for n in range(2):
                eng.wait_ge(s_w[n], 16)
                project(eng, psp[:, n], w[:, n], m.xT).then_inc(s_p, 1)
            eng.wait_ge(s_wm, 1)
            for h in range(NP):
                last = eng.transpose(psw[:, h // 4, (h % 4) * P:(h % 4 + 1) * P], ws[:, h, :], m.ident[:, :])
            last.then_inc(s_wt, 1)
            eng.wait_ge(s_we, 1)
            eng.matmul(ps0[:, 0:NP], m.ones[0:1, :], m.wst[0:1, :, 0], start=True, stop=True).then_inc(s_wt, 1)

        @block.scalar
        def _(eng):
            for n in range(2):
                eng.wait_ge(s_p, n + 1)
                eng.activation(split(cols[:, n, 1:T + 1]), halves(psp[:, n]), ACT.Copy).then_inc(s_e, 1)
            eng.wait_ge(s_xs, 1)
            eng.activation(m.lora_in[0:HD, :], xs[0:HD, 0, :], ACT.Tanh)
            eng.activation(m.lora_in[HD:P, :], xs[HD:P, 0, :], ACT.Copy)
            eng.wait_ge(s_xs, 2)
            eng.activation(m.gate_in[:, :], xs[:, 1, :], ACT.Tanh, scale=0.5).then_inc(s_t, 1)

        @block.vector
        def _(eng):
            step = Steps(eng, s_step)
            step.did(eng.memset(cols[:, :, 0:1], 0.0))
            step.did(eng.tensor_scalar(m.half_bias[:, 0, :], vec(m, "w_bias"), 0.5, None, ALU.mult))
            step.did(eng.tensor_scalar(m.half_bias[:, 1, :], vec(m, "a_bias"), 0.5, None, ALU.mult))
            step.wait()
            for n in range(2):
                eng.wait_ge(s_e, n + 1)
                c = 3 * NP + n
                shift_mix(eng, step, m, cols[:, n], diff, xs[:, n, :], vec(m, "rwkv_mu")[:, c:c + 1], m.shift_prev[:, c, :])
                step.did(eng.tensor_copy(m.shift_last[:, :, c], cols[:, n, TP:T + 1]))
                step.wait()
                eng.sem_inc(s_xs, 1)
            eng.wait_ge(s_t, 1)
            step.did(eng.tensor_scalar(m.gate_in[:, :], m.gate_in[:, :], 0.5, 0.5, ALU.mult, ALU.add))
            eng.wait_ge(s_wt, 1)
            eng.tensor_copy(m.wst[:, :, :].rearrange("p (a h) t -> p a h t", a=2),
                            psw[:, :, :].rearrange("p a (h t) -> p a h t", t=P)).then_inc(s_we, 1)
            eng.wait_ge(s_wt, 2)
            eng.tensor_copy(m.w00[:, :], ps0[:, 0:NP])


def phase_rkv(nc, m, a):
    ctx, sb, ps, sem = open_phase(nc)
    with ctx:
        w = sb("rk_w", [P, 2, 3, NK, P])
        lw = sb("rk_lw", [P, 2, P])
        cols = [sb(f"rk_cols{j}", [P, T + 1]) for j in range(3)]
        diff = sb("rk_diff", [P, T])
        rate = sb("rk_rate", [P, T])
        tw = sb("rk_tw", [P, T])
        ta = sb("rk_ta", [P, T])
        kk2 = sb("rk_kk2", [P, T])
        rkk = sb("rk_rkk", [P, T])
        kx = sb("rk_kx", [P, T])
        norm = sb("rk_norm", [P, T])
        carry = sb("rk_carry", [P, NC, CH + 1])
        psp = [ps(f"rk_ps{n}", [P, 2, 512]) for n in range(2)]
        psz = ps("rk_psz", [P, 2, 512])
        pss = ps("rk_pss", [P, 2, 512])
        s_w = [sem("r_w0"), sem("r_w1")]
        names = ("step", "proj", "cols", "zw", "za", "tw", "ta", "ss", "bo", "ss_read", "bo_read",
                 "kk", "kk2", "rkk", "r_used", "k_used", "v_used", "lw_used", "rate_used", "ln", "rn")
        (s_step, s_proj, s_cols, s_zw, s_za, s_tw, s_ta, s_ss, s_bo, s_ss_read, s_bo_read, s_kk, s_kk2,
         s_rkk, s_r_used, s_k_used, s_v_used, s_lw_used, s_rate_used, s_ln, s_rn) = \
            (sem("r_" + n) for n in names)
        used = [s_r_used, s_k_used, s_v_used]
        block = ctx.enter_context(nc.Block())
        @block.sync
        def _(eng):
            def load(slot, pair):
                for j in range(3):
                    eng.dma_start(w[:, slot, j], w_cols(a["w_in"], bass.ds(pair * P + (OFF_SHIFT + j * D), P)))\
                       .then_inc(s_w[slot], 16)
                eng.dma_start(lw[0:HD, slot, :], a["w_lora_up"][0, :, bass.ds(pair * P, P)]).then_inc(s_w[slot], 16)
                eng.dma_start(lw[HD:P, slot, :], a["a_lora_up"][0, :, bass.ds(pair * P, P)]).then_inc(s_w[slot], 16)

            for slot in range(2):
                load(slot, slot)
            with eng.Fori(1, NP // 2) as i:
                for slot in range(2):
                    eng.wait_ge(s_proj, i * 6 + (3 * slot - 3))
                    load(slot, i * 2 + slot)

        @block.tensor
        def _(eng):
            with eng.Fori(0, NP // 2) as i:
                for h in range(2):
                    def proj(j):
                        n = 3 * h + j
                        eng.wait_ge(s_cols, i * 6 + (n + 1))
                        project(eng, psp[n % 2], w[:, h, j], m.xT).then_inc(s_proj, 1)

                    def z(rows, s_out, s_free, v):
                        eng.wait_ge(s_free, i * 2 + v)
                        for half in range(2):
                            last = eng.matmul(psz[:, half, 0:TH], lw[rows, h, :], m.lora_in[rows, half * TH:(half + 1) * TH],
                                              start=True, stop=True)
                        last.then_inc(s_out, 1)

                    eng.wait_ge(s_w[h], i * 80 + 80)
                    proj(0)
                    z(slice(0, HD), s_zw, s_bo_read, h + 1)
                    proj(1)
                    z(slice(HD, P), s_za, s_tw, h + 1)
                    proj(2)
                    eng.wait_ge(s_kk2, i * 2 + h + 1)
                    eng.wait_ge(s_ss_read, i * 2 + h + 1)
                    for half in range(2):
                        last = eng.matmul(pss[:, half, 0:TH], m.headones[:, :], kk2[:, half * TH:(half + 1) * TH],
                                          start=True, stop=True)
                    last.then_inc(s_ss, 1)
                    eng.wait_ge(s_rkk, i * 2 + h + 1)
                    eng.wait_ge(s_ta, i * 2 + h + 1)
                    for half in range(2):
                        last = eng.matmul(psz[:, half, 0:TH], m.headones[:, :], rkk[:, half * TH:(half + 1) * TH],
                                          start=True, stop=True)
                    last.then_inc(s_bo, 1)

        @block.scalar
        def _(eng):
            eng.sem_inc(s_cols, 2)
            with eng.Fori(0, NP // 2) as i:
                for h in range(2):
                    def copy_cols(j):
                        eng.wait_ge(s_proj, i * 6 + (3 * h + j + 1))
                        eng.wait_ge(used[j], i * 2 + h + 1)
                        eng.activation(split(cols[j][:, 1:T + 1]), halves(psp[(3 * h + j) % 2]), ACT.Copy).then_inc(s_cols, 1)

                    def half_tanh(out, sem_in, free, bias, sem_out):
                        eng.wait_ge(sem_in, i * 2 + h + 1)
                        eng.wait_ge(free, i * 2 + h + 1)
                        eng.activation(split(out[:, :]), halves(psz), ACT.Tanh, scale=0.5,
                                       bias=m.half_bias[:, bias, bass.ds(i * 2 + h, 1)]).then_inc(sem_out, 1)

                    copy_cols(0)
                    half_tanh(tw, s_zw, s_lw_used, 0, s_tw)
                    copy_cols(1)
                    half_tanh(ta, s_za, s_rate_used, 1, s_ta)
                    eng.wait_ge(s_kk, i * 2 + h + 1)
                    eng.activation(kk2[:, :], m.kk[:, bass.ds(i * 2 + h, 1), :].rearrange("p a t -> p (a t)"),
                                   ACT.Square).then_inc(s_kk2, 1)
                    copy_cols(2)
                    eng.wait_ge(s_ss_read, i * 2 + h + 2)
                    eng.activation(norm[:, :], norm[:, :], ACT.Ln).then_inc(s_ln, 1)
                    eng.wait_ge(s_ln, i * 2 + h + 1)
                    eng.activation(norm[:, :], norm[:, :], ACT.Exp, scale=-0.5).then_inc(s_rn, 1)

        @block.vector
        def _(eng):
            step = Steps(eng, s_step)
            for c in cols:
                step.did(eng.memset(c[:, 0:1], 0.0))
            step.did(eng.memset(m.cum[:, :, :].rearrange("p n (c t) -> p n c t", t=CH + 1)[:, :, :, 0:1], 0.0))
            step.did(eng.memset(carry[:, :, :], 1.0))
            step.wait()
            step.did(eng.memset(carry[:, :, 0:1], 0.0))
            step.wait()
            first = step.n
            for s in used + [s_lw_used, s_rate_used, s_ss_read, s_bo_read]:
                eng.sem_inc(s, 1)
            with eng.Fori(0, NP // 2) as i:
                body = Steps(eng, s_step, i * RKV_STEPS + first)
                for h in range(2):
                    pair = i * 2 + h

                    def at(t):
                        return t[:, bass.ds(pair, 1), :].rearrange("p a t -> p (a t)")

                    def col(name, add=0):
                        return m.vecs[:, bass.ds(pair + (VEC[name][0] + add), 1)]

                    def shifted(j, out):
                        eng.wait_ge(s_cols, i * 6 + (3 * h + j + 3))
                        prev = m.shift_prev[:, bass.ds(pair + j * NP, 1), :].rearrange("p a t -> p (a t)")
                        shift_mix(eng, body, m, cols[j], diff, out, col("rwkv_mu", j * NP), prev)
                        last = m.shift_last[:, :, bass.ds(pair + j * NP, 1)].rearrange("p t a -> p (t a)")
                        eng.tensor_copy(last, cols[j][:, TP:T + 1]).then_inc(used[j], 1)

                    shifted(0, at(m.r))
                    eng.wait_ge(s_tw, pair + 1)
                    body.did(eng.tensor_scalar(at(m.cum).rearrange("p (c t) -> p c t", t=CH + 1)[:, :, 1:CH + 1],
                                               tw[:, 0:TP].rearrange("p (c t) -> p c t", t=CH),
                                               DECAY / 2, DECAY / 2, ALU.mult, ALU.add))
                    eng.tensor_scalar(m.lw_sample[:, bass.ds(pair, 1), :].rearrange("p a t -> p (a t)"), tw[:, TP:T],
                                      DECAY / 2, DECAY / 2, ALU.mult, ALU.add).then_inc(s_lw_used, 1)
                    body.wait()
                    body.did(eng.tensor_tensor_scan(at(m.cum), carry[:, :, :].rearrange("p c t -> p (c t)"),
                                                    at(m.cum), 0.0, ALU.mult, ALU.add))
                    shifted(1, kx[:, :])
                    eng.tensor_scalar(at(m.kk), kx[:, :], col("k_k"), None, ALU.mult).then_inc(s_kk, 1)
                    eng.wait_ge(s_ta, pair + 1)
                    eng.tensor_scalar(rate[:, :], ta[:, :], 0.5, 0.5, ALU.mult, ALU.add).then_inc(s_rate_used, 1)
                    eng.wait_ge(s_kk, pair + 1)
                    eng.wait_ge(s_rate_used, pair + 2)
                    body.did(eng.tensor_tensor(at(m.br), at(m.kk), rate[:, :], ALU.mult))
                    body.wait()
                    body.did(eng.tensor_scalar(rate[:, :], rate[:, :], -1.0, col("k_a"), ALU.add, ALU.mult))
                    body.wait()
                    body.did(eng.scalar_tensor_tensor(out=at(m.k), in0=rate[:, :], scalar=1.0, in1=kx[:, :],
                                                      op0=ALU.add, op1=ALU.mult))
                    body.wait()
                    eng.scalar_tensor_tensor(out=rkk[:, :], in0=at(m.r), scalar=col("r_k"), in1=at(m.k),
                                             op0=ALU.mult, op1=ALU.mult).then_inc(s_rkk, 1)
                    shifted(2, at(m.v))
                    eng.wait_ge(s_ss, pair + 1)
                    eng.tensor_scalar(split(norm[:, :]), halves(pss), 1e-24, None, ALU.max).then_inc(s_ss_read, 1)
                    eng.wait_ge(s_bo, pair + 1)
                    eng.tensor_tensor(split(at(m.bonus)), halves(psz), split(at(m.v)), ALU.mult).then_inc(s_bo_read, 1)
                    eng.wait_ge(s_rn, pair + 1)
                    body.did(eng.scalar_tensor_tensor(out=at(m.kk), in0=at(m.kk), scalar=-1.0, in1=norm[:, :],
                                                      op0=ALU.mult, op1=ALU.mult))
                    body.did(eng.tensor_tensor(at(m.br), at(m.br), norm[:, :], ALU.mult))
                assert body.n == RKV_STEPS, body.n


def phase_chunks(nc, m, a):
    ctx, sb, ps, sem = open_phase(nc)
    with ctx:
        pi = sb("ck_pi", [P, NP, CH])
        L = sb("ck_L", [P, NP, 2, P])
        bk = sb("ck_bk", [P, NP, P])
        bkt = sb("ck_bkt", [P, NP, P])
        v2 = sb("ck_v2", [P, NP, 2, CH])
        wv = sb("ck_wv", [P, NP, 2, HD])
        mb = sb("ck_mb", [P, NP, P])
        nb = sb("ck_nb", [P, NP, P])
        a1 = sb("ck_a1", [P, NP, P])
        X = sb("ck_X", [P, NP, P])
        Z = sb("ck_Z", [P, NP, P])
        W = sb("ck_W", [P, NP, P])
        rh = sb("ck_rh", [P, NP, HD])
        st = sb("ck_st", [P, NP, HD])
        bank = [[ps(f"ck_b{g}{n}", [P, 512]) for n in range(4)] for g in range(G)]
        s_step, s_init, s_px, s_pi, s_ar, s_bk, s_v2, s_fin, s_sto, s_out, s_l_free = \
            (sem("k_" + n) for n in ("step", "init", "px", "pi", "ar", "bk", "v2", "fin", "sto", "out", "l_free"))

        def pair_sems(name):
            return [sem(f"k_{name}{g}") for g in range(G)]

        s_eo, s_tb, s_nt, s_w, s_xz, s_rhs, s_u, s_y, s_s = \
            (pair_sems(n) for n in ("eo", "tb", "nt", "w", "xz", "rhs", "u", "y", "s"))
        s_eo_e, s_nb, s_tb_e, s_a1, s_x1, s_w_e, s_xz_e, s_rh_e, s_u_e, s_y_e, s_st, s_s0 = \
            (pair_sems(n) for n in ("eo_e", "nb", "tb_e", "a1", "x1", "w_e", "xz_e", "rh_e", "u_e", "y_e", "st", "s0"))
        NL = len(LEVELS)
        block = ctx.enter_context(nc.Block())

        sto = v2[0:HD].rearrange("p n a t -> p n (a t)")

        def grp(g):
            return slice(g * GP, (g + 1) * GP)

        def b4(ap):
            return ap[:, 0:GP * P].rearrange("p (n c) -> p n c", c=P)

        def b64(ap):
            return ap[:, 0:GP * HD].rearrange("p (n c) -> p n c", c=HD)

        lo, hi = slice(0, HD), slice(HD, P)

        def running(c, first, last):
            return m.cum[:, :, :].rearrange("p n (c t) -> p n c t", t=CH + 1)[:, :, bass.ds(c, 1), first:last]\
                .rearrange("p n a t -> p n (a t)")

        def after(c):
            return (c + 1) % NC

        def a_r_rows(eng, c, rows, which):
            at = bass.ds(c * CH, CH)
            eng.tensor_tensor(L[rows, :, which, 0:CH], m.kk[rows, :, at], running(c, 0, CH)[rows], ALU.mult).then_inc(s_ar, 1)
            eng.tensor_tensor(L[rows, :, which, CH:P], m.r[rows, :, at], running(c, 1, CH + 1)[rows], ALU.mult)\
               .then_inc(s_ar, 1)

        def b_k_rows(eng, c, rows):
            at = bass.ds(c * CH, CH)
            others = hi if rows == lo else lo
            eng.tensor_tensor(bk[rows, :, rows], m.br[rows, :, at], pi[rows, :, :], ALU.mult).then_inc(s_bk, 1)
            eng.tensor_tensor(bk[rows, :, others], m.k[rows, :, at], pi[rows, :, :], ALU.mult).then_inc(s_bk, 1)

        @block.tensor
        def _(eng):
            with eng.Fori(0, NC) as c:
                for g in range(G):
                    b = bank[g]
                    if g == 0:
                        eng.wait_ge(s_ar, c * 4 + 4)
                        eng.wait_ge(s_bk, c * 4 + 4)
                    eng.wait_ge(s_st[g], c + 1)
                    eng.wait_ge(s_u_e[g], c * 2 + 2)
                    for n in range(GP):
                        p = g * GP + n
                        eng.matmul(b4(b[0])[:, n, :], bk[lo, p, :], L[lo, p, 0, :], start=True, stop=True)
                    for n in range(GP):
                        p = g * GP + n
                        last = eng.matmul(b4(b[1])[:, n, :], bk[hi, p, :], L[hi, p, 1, :], start=True, stop=True)
                    last.then_inc(s_eo[g], 1)
                for g in range(G):
                    b = bank[g]
                    if g == 0:
                        eng.wait_ge(s_v2, c + 1)
                    eng.wait_ge(s_y_e[g], c * 2 + 2)
                    for n in range(GP):
                        p = g * GP + n
                        eng.transpose(b4(b[2])[:, n, :], bk[:, p, :], m.ident[:, :])
                    for n in range(GP):
                        p = g * GP + n
                        last = eng.transpose(b4(b[3])[:, n, :], v2[:, p].rearrange("p a t -> p (a t)"), m.ident[:, :])
                    last.then_inc(s_tb[g], 1)
                for g in range(G):
                    b = bank[g]
                    eng.wait_ge(s_nb[g], c * 2 + 2)
                    eng.wait_ge(s_eo_e[g], c * 4 + 4)
                    for n in range(GP):
                        last = eng.transpose(b4(b[0])[:, n, :], nb[:, g * GP + n, :], m.ident[:, :])
                    last.then_inc(s_nt[g], 1)
                for lv in range(NL):
                    for g in range(G):
                        b = bank[g]
                        if lv == 0:
                            eng.wait_ge(s_a1[g], c + 1)
                            eng.wait_ge(s_x1[g], c * 2 + 2)
                            eng.wait_ge(s_tb_e[g], c * 3 + 3)
                        else:
                            eng.wait_ge(s_xz_e[g], c * (2 * NL - 1) + 2 * lv)
                        for n in range(GP):
                            p = g * GP + n
                            last = eng.matmul(b4(b[1])[:, n, :], a1[:, p, :], X[:, p, :], start=True, stop=True)
                        last.then_inc(s_w[g], 1)
                    for g in range(G):
                        b = bank[g]
                        eng.wait_ge(s_w_e[g], c * NL + lv + 1)
                        for n in range(GP):
                            p = g * GP + n
                            last = eng.matmul(b4(b[2])[:, n, :], Z[:, p, :], W[:, p, :], start=True, stop=True)
                        last.then_inc(s_xz[g], 1)
                        if lv < NL - 1:
                            for n in range(GP):
                                p = g * GP + n
                                last = eng.matmul(b4(b[3])[:, n, :], W[:, p, :], Z[:, p, :], start=True, stop=True)
                            last.then_inc(s_xz[g], 1)
                for g in range(G):
                    b = bank[g]
                    eng.wait_ge(s_s0[g], c * 2 + 2)
                    eng.wait_ge(s_xz_e[g], c * (2 * NL - 1) + (2 * NL - 1))
                    for n in range(GP):
                        p = g * GP + n
                        eng.matmul(b64(b[0])[lo, n, :], L[:, p, 0, 0:CH], wv[:, p, 0, :], start=True, stop=True)
                        last = eng.matmul(b64(b[0])[hi, n, :], L[:, p, 1, 0:CH], wv[:, p, 1, :], start=True, stop=True)
                    last.then_inc(s_rhs[g], 1)
                    for n in range(GP):
                        p = g * GP + n
                        eng.matmul(b64(b[2])[lo, n, :], wv[:, p, 0, :], L[:, p, 0, CH:P], start=(n == 0), stop=False,
                                   skip_group_check=True)
                        last = eng.matmul(b64(b[3])[hi, n, :], wv[:, p, 1, :], L[:, p, 1, CH:P], start=(n == 0), stop=False,
                                          skip_group_check=True)
                    if g == G - 1:
                        last.then_inc(s_l_free, 1)
                for g in range(G):
                    b = bank[g]
                    eng.wait_ge(s_rh_e[g], c + 1)
                    for n in range(GP):
                        p = g * GP + n
                        last = eng.matmul(b64(b[1])[:, n, :], X[:, p, :], rh[:, p, :], start=True, stop=True)
                    last.then_inc(s_u[g], 1)
                for g in range(G):
                    b = bank[g]
                    eng.wait_ge(s_u_e[g], c * 2 + 4)
                    for n in range(GP):
                        p = g * GP + n
                        eng.matmul(b64(b[0])[lo, n, :], bkt[:, p, 0:HD], wv[:, p, 0, :], start=True, stop=True)
                        last = eng.matmul(b64(b[0])[hi, n, :], bkt[:, p, HD:P], wv[:, p, 1, :], start=True, stop=True)
                    last.then_inc(s_s[g], 1)
                    for n in range(GP):
                        p = g * GP + n
                        eng.matmul(b64(b[2])[lo, n, :], wv[lo, p, 0, :], mb[lo, p, CH:P], start=False, stop=True,
                                   skip_group_check=True)
                        last = eng.matmul(b64(b[3])[hi, n, :], wv[hi, p, 1, :], mb[hi, p, CH:P], start=False, stop=True,
                                          skip_group_check=True)
                    last.then_inc(s_y[g], 1)
            for g in range(G):
                eng.wait_ge(s_s0[g], NC * 2 + 2)
                eng.wait_ge(s_y_e[g], NC * 2 + 2)
                for n in range(GP):
                    last = eng.transpose(b4(bank[g][2])[0:HD, n, :], st[:, g * GP + n, :], m.ident[:, :])
                last.then_inc(s_fin, 1)

        @block.scalar
        def _(eng):
            for g in range(G):
                eng.sem_inc(s_y_e[g], 2)
            eng.sem_inc(s_u_e[0], 1)
            eng.sem_inc(s_u_e[1], 1)
            def exponentials(c, n):
                eng.activation(pi[:, :, :], running(c, 1, CH + 1), ACT.Exp, scale=-1.0).then_inc(s_pi, 1)
                for half in range(2):
                    ins = eng.activation(v2[:, :, half, :], m.v[:, :, bass.ds(c * CH, CH)], ACT.Copy)
                ins.then_inc(s_v2, 1)
                eng.wait_ge(s_pi, n + 1)
                eng.activation(running(c, 0, CH + 1), running(c, 0, CH + 1), ACT.Exp).then_inc(s_px, 1)

            exponentials(0, 0)
            with eng.Fori(0, NC) as c:
                for g in range(G):
                    b = bank[g]
                    eng.wait_ge(s_tb[g], c + 1)
                    eng.activation(bkt[:, grp(g), :], b4(b[2]), ACT.Copy).then_inc(s_tb_e[g], 1)
                    eng.activation(wv[hi, grp(g), 0, :], b4(b[3])[hi, :, 0:HD], ACT.Copy).then_inc(s_tb_e[g], 1)
                    eng.activation(wv[lo, grp(g), 1, :], b4(b[3])[lo, :, HD:P], ACT.Copy).then_inc(s_tb_e[g], 1)
                for g in range(G):
                    eng.wait_ge(s_nt[g], c + 1)
                    eng.activation(a1[:, grp(g), :], b4(bank[g][0]), ACT.Copy).then_inc(s_a1[g], 1)
                eng.wait_ge(s_bk, c * 4 + 4)
                exponentials(after(c), c + 1)
                for lv in range(NL):
                    for g in range(G):
                        eng.wait_ge(s_xz[g], c * (2 * NL - 1) + 2 * lv + 1)
                        eng.activation(X[:, grp(g), :], b4(bank[g][2]), ACT.Copy).then_inc(s_xz_e[g], 1)
                        if lv < NL - 1:
                            eng.wait_ge(s_xz[g], c * (2 * NL - 1) + 2 * lv + 2)
                            eng.activation(Z[:, grp(g), :], b4(bank[g][3]), ACT.Copy).then_inc(s_xz_e[g], 1)
                for g in range(G):
                    eng.wait_ge(s_rhs[g], c + 1)
                    eng.activation(rh[:, grp(g), :], b64(bank[g][0]), ACT.Copy).then_inc(s_rh_e[g], 1)
                for g in range(G):
                    eng.wait_ge(s_u[g], c + 1)
                    eng.activation(wv[lo, grp(g), 0, :], b64(bank[g][1])[lo], ACT.Copy).then_inc(s_u_e[g], 1)
                for g in range(G):
                    eng.wait_ge(s_y[g], c + 1)
                    y = m.r[:, grp(g), bass.ds(c * CH, CH)]
                    eng.activation(y[lo], b64(bank[g][2])[lo], ACT.Copy).then_inc(s_y_e[g], 1)
                    eng.activation(y[hi], b64(bank[g][3])[hi], ACT.Copy).then_inc(s_y_e[g], 1)
                    eng.wait_ge(s_st[g], c + 2)
                    eng.activation(wv[lo, grp(g), 0, :], st[lo, grp(g), :], ACT.Copy).then_inc(s_s0[g], 1)
            for g in range(G):
                eng.wait_ge(s_fin, g + 1)
                eng.activation(sto[:, grp(g), :], b4(bank[g][2])[0:HD], ACT.Copy).then_inc(s_sto, 1)

        @block.vector
        def _(eng):
            step = Steps(eng, s_step)
            step.did(eng.memset(st[:, :, :], 0.0))
            step.did(eng.memset(wv[:, :, :, :], 0.0))
            step.did(eng.memset(nb[:, :, :], 0.0))
            step.wait()
            first = step.n
            for g in range(G):
                eng.sem_inc(s_st[g], 1)
                eng.sem_inc(s_u_e[g], 1)
                eng.sem_inc(s_s0[g], 2)
            eng.sem_inc(s_init, 1)
            eng.wait_ge(s_pi, 1)
            b_k_rows(eng, 0, lo)
            eng.wait_ge(s_px, 1)
            a_r_rows(eng, 0, lo, 0)
            a_r_rows(eng, 0, hi, 1)
            with eng.Fori(0, NC) as c:
                body = Steps(eng, s_step, c * G + first)
                for g in range(G):
                    b = bank[g]
                    mask = m.causal[:, :].unsqueeze(1).to_broadcast([P, GP, P])
                    eng.wait_ge(s_eo[g], c + 1)
                    eng.tensor_tensor(mb[lo, grp(g), :], b4(b[0])[lo], mask[lo], ALU.mult).then_inc(s_eo_e[g], 1)
                    eng.tensor_tensor(mb[hi, grp(g), :], b4(b[1])[hi], mask[hi], ALU.mult).then_inc(s_eo_e[g], 1)
                    eng.tensor_tensor(L[hi, grp(g), 0, :], b4(b[0])[hi], mask[hi], ALU.mult).then_inc(s_eo_e[g], 1)
                    eng.tensor_tensor(L[lo, grp(g), 1, :], b4(b[1])[lo], mask[lo], ALU.mult).then_inc(s_eo_e[g], 1)
                for g in range(G):
                    eng.wait_ge(s_nb[g], c * 2 + 2)
                    eng.tensor_tensor(X[:, grp(g), :], nb[:, grp(g), :],
                                      m.levels[:, 0, :].unsqueeze(1).to_broadcast([P, GP, P]), ALU.mult).then_inc(s_x1[g], 1)
                for g in range(G):
                    eng.wait_ge(s_a1[g], c + 1)
                    eng.tensor_tensor(Z[:, grp(g), :], a1[:, grp(g), :],
                                      m.level1t[:, :].unsqueeze(1).to_broadcast([P, GP, P]), ALU.mult).then_inc(s_x1[g], 1)
                for lv in range(NL):
                    for g in range(G):
                        eng.wait_ge(s_w[g], c * NL + lv + 1)
                        eng.tensor_tensor(W[:, grp(g), :], b4(bank[g][1]),
                                          m.levels[:, lv + 1, :].unsqueeze(1).to_broadcast([P, GP, P]), ALU.mult)\
                           .then_inc(s_w_e[g], 1)
                for g in range(G):
                    eng.wait_ge(s_u[g], c + 1)
                    eng.tensor_copy(wv[hi, grp(g), 1, :], b64(bank[g][1])[hi]).then_inc(s_u_e[g], 1)
                eng.wait_ge(s_px, c + 2)
                eng.wait_ge(s_l_free, c + 1)
                a_r_rows(eng, after(c), lo, 0)
                for g in range(G):
                    eng.wait_ge(s_s[g], c + 1)
                    eng.wait_ge(s_s0[g], c * 2 + 2)
                    body.did(eng.tensor_tensor(st[:, grp(g), :], b64(bank[g][0]), st[:, grp(g), :], ALU.add))
                    body.wait()
                    eng.tensor_tensor(st[:, grp(g), :], st[:, grp(g), :],
                                      running(c, CH, CH + 1)[:, grp(g), :].to_broadcast([P, GP, HD]), ALU.mult).then_inc(s_st[g], 1)
                    eng.wait_ge(s_st[g], c + 2)
                    eng.wait_ge(s_y[g], c + 1)
                    eng.tensor_copy(wv[hi, grp(g), 1, :], st[hi, grp(g), :]).then_inc(s_s0[g], 1)

        @block.gpsimd
        def _(eng):
            eng.wait_ge(s_init, 1)
            eng.wait_ge(s_pi, 1)
            b_k_rows(eng, 0, hi)
            with eng.Fori(0, NC) as c:
                for g in range(G):
                    eng.wait_ge(s_eo_e[g], c * 4 + 2)
                    eng.tensor_tensor(nb[lo, grp(g), 0:CH], mb[lo, grp(g), 0:CH],
                                      m.ident[lo, 0:CH].unsqueeze(1).to_broadcast([HD, GP, CH]), ALU.add).then_inc(s_nb[g], 1)
                    eng.tensor_tensor(nb[hi, grp(g), CH:P], mb[hi, grp(g), 0:CH],
                                      m.ident[hi, CH:P].unsqueeze(1).to_broadcast([HD, GP, CH]), ALU.add).then_inc(s_nb[g], 1)
                eng.wait_ge(s_pi, c + 2)
                eng.wait_ge(s_tb[G - 1], c + 1)
                for rows in (lo, hi):
                    b_k_rows(eng, after(c), rows)
                eng.wait_ge(s_px, c + 2)
                eng.wait_ge(s_l_free, c + 1)
                a_r_rows(eng, after(c), hi, 1)

        @block.sync
        def _(eng):
            eng.wait_ge(s_sto, G)
            eng.dma_start(a["new_wkv_prompt"][0, 0].rearrange("(n e) i j -> i n e j", e=2),
                          sto[:, :, :].rearrange("i n (e j) -> i n e j", e=2)).then_inc(s_out, 16)
            eng.wait_ge(s_out, 16)


def phase_sample_vectors(nc, m, a):
    ctx, sb, ps, sem = open_phase(nc)
    with ctx:
        tok = sb("sv_tok", [TS, 6, D])
        sh = sb("sv_sh", [3 * NSH, 3, P])
        pst = ps("sv_ps", [P, 6, 512])
        psh = ps("sv_psh", [P, 512])
        s_w, s_t, s_e, s_h, s_he, s_out, s_q = (sem("v_" + n) for n in ("w", "t", "e", "h", "he", "out", "q"))
        block = ctx.enter_context(nc.Block())

        @block.scalar
        def _(eng):
            eng.activation(m.lw_sample[:, :, :], m.lw_sample[:, :, :], ACT.Exp).then_inc(s_w, 1)
            for n in range(6):
                eng.wait_ge(s_t, n + 1)
                eng.activation(tok[:, n, :].rearrange("b (h c) -> b h c", h=2), pst[0:TS, 2 * (n % 3):2 * (n % 3) + 2, :],
                               ACT.Copy).then_inc(s_e, 1)

        @block.tensor
        def _(eng):
            for n in range(3):
                last = eng.transpose(psh[0:3 * NSH, n * P:(n + 1) * P],
                                     m.shift_last[:, 3 * n:3 * n + 3, :].rearrange("p t c -> p (t c)"), m.ident[:, :])
            last.then_inc(s_h, 1)
            eng.wait_ge(s_w, 1)
            for n, t in enumerate((m.r, m.lw_sample, m.k, m.v, m.kk, m.br)):
                if n >= 3:
                    eng.wait_ge(s_e, n - 2)
                for p in range(NP):
                    src = t[:, p, :] if n == 1 else t[:, p, TP:T]
                    last = eng.transpose(pst[0:TS, 2 * (n % 3) + p // 4, (p % 4) * P:(p % 4 + 1) * P], src, m.ident[:, :])
                last.then_inc(s_t, 1)

        @block.vector
        def _(eng):
            eng.wait_ge(s_h, 1)
            eng.tensor_copy(sh[:, :, :], psh[0:3 * NSH, 0:3 * P].rearrange("r (n c) -> r n c", n=3)).then_inc(s_he, 1)

        @block.sync
        def _(eng):
            eng.wait_ge(s_he, 1)
            eng.dma_start(a["new_shift_prompt"][0, 0].rearrange("(c p) -> c p", p=P), sh[0:NSH, 0, :]).then_inc(s_out, 16)
            eng.dma_start(a["new_shift_sample"][0, 0:2].rearrange("t (c p) -> (t c) p", p=P), sh[NSH:3 * NSH, 0, :]).then_inc(s_out, 16)
            for n in range(1, 3):
                eng.dma_start(a["new_shift_sample"][0, 3 * n - 1:3 * n + 2].rearrange("t (c p) -> (t c) p", p=P), sh[:, n, :])\
                   .then_inc(s_out, 16)
            eng.wait_ge(s_e, 6)
            eng.dma_start(m.d_sample.rearrange("n b c -> b n c"), tok[:, :, :]).then_inc(s_q, 16)
            eng.wait_ge(s_q, 16)
            eng.dma_start(m.sv[:, :, :], m.d_sample.rearrange("n b (h j) -> (b h) n j", j=HD)).then_inc(m.s_sv, 16)
            eng.wait_ge(s_out, 64)


def phase_gating(nc, m, a):
    ctx, sb, ps, sem = open_phase(nc)
    with ctx:
        w = sb("uv_w", [P, 2, 2, NK, P])
        lnw = sb("uv_lnw", [P, D])
        lnb = sb("uv_lnb", [P, D])
        sbias = sb("uv_sb", [P, D])
        gv = sb("uv_gv", [P, T])
        gu = sb("uv_gu", [P, T])
        vn = sb("uv_vn", [P, NT + 1, P])
        vns = sb("uv_vns", [TS, D])
        st = sb("uv_st", [P, NT + 1, 6])
        mv = sb("uv_mv", [P, NT + 1, 2])
        rstd = sb("uv_rstd", [P, NT + 1])
        var = sb("uv_var", [P, NT + 1])
        half = sb("uv_half", [P, NT + 1])
        pause = sb("uv_pause", [P, 1])
        gate = sb("uv_gate", [P, T])
        T1 = sb("sw_t", [P, HD, HD])
        sa = sb("sw_sa", [P, HD])
        ys = sb("sw_y", [P, HD])
        yt = sb("sw_yt", [TS, D])
        psv = ps("uv_psv", [P, 2, 512])
        psu = ps("uv_psu", [P, 2, 512])
        pst = ps("uv_pst", [P, 512])
        psx = ps("uv_psx", [P, 512])
        psw = ps("uv_psw", [P, 512])
        pss = ps("uv_pss", [P, 512])
        s_w = [sem("u_w0"), sem("u_w1")]
        s_S = sem("u_S")
        (s_row, s_pv, s_pu, s_gv, s_gu, s_t, s_ve, s_rs, s_vn, s_sp,
         s_ya, s_step, s_zero, s_vns, s_cv, s_pool, s_sdone, s_y, s_yd, s_yl, s_yt, s_rstep) = \
            (sem("u_" + n) for n in ("row", "pv", "pu", "gv", "gu", "t", "ve", "rs",
                                     "vn", "sp", "ya", "step", "zero", "vns", "cv", "pool", "sdone", "y", "yd",
                                     "yl", "yt", "rstep"))
        block = ctx.enter_context(nc.Block())
        row = lambda ap: ap.rearrange("l h d -> l (h d)").partition_broadcast(P).rearrange("p l d -> p (l d)")

        @block.sync
        def _(eng):
            def load(slot, h):
                for n, off in enumerate((OFF_V, 0)):
                    eng.dma_start(w[:, slot, n], w_cols(a["w_in"], bass.ds(h * P + off, P))).then_inc(s_w[slot], 16)

            load(0, 0)
            eng.dma_start(m.S[:, :, :], a["state_wkv"][0].rearrange("b h i j -> (b h) i j")).then_inc(s_S, 16)
            load(1, 1)
            for t, src in ((lnw, a["sgu_ln_w"]), (lnb, a["sgu_ln_b"]), (sbias, a["sgu_b"])):
                eng.dma_start(t[:, :], row(src)).then_inc(s_row, 16)
            with eng.Fori(1, NP // 2) as i:
                for slot in range(2):
                    eng.wait_ge(s_pu, i * 2 + (slot - 1))
                    load(slot, i * 2 + slot)
            eng.wait_ge(s_pu, NP - 1)
            load(0, 0)
            eng.wait_ge(s_sdone, 1)
            eng.dma_start(a["new_wkv_sample"][0].rearrange("b h i j -> (b h) i j"), m.S[:, :, :]).then_inc(s_cv, 16)
            eng.wait_ge(s_y, 1)
            eng.dma_start(m.d_y.rearrange("b (h j) -> (b h) j", j=HD), ys[:, :]).then_inc(s_yd, 16)
            eng.wait_ge(s_yd, 16)
            eng.dma_start(yt[:, :], m.d_y).then_inc(s_yl, 16)
            eng.wait_ge(s_vns, NP)
            eng.dma_start(a["new_chunk_v_sample"].rearrange("l b t h d -> (l b t) (h d)"), vns[:, :]).then_inc(s_cv, 16)
            eng.wait_ge(s_cv, 32)

        @block.tensor
        def _(eng):
            def v_columns(i, x):
                eng.wait_ge(s_w[x], i * 32 + 32)
                eng.wait_ge(s_gv, i * 2 + (x + 1))
                project(eng, psv, w[:, x, 0], m.xT).then_inc(s_pv, 1)

            v_columns(0, 0)
            with eng.Fori(0, NP // 2) as i:
                def turn_v(x):
                    h = i * 2 + x
                    eng.wait_ge(s_gv, h + 2)
                    eng.wait_ge(s_ve, h + 1)
                    for c in range(NT):
                        eng.transpose(pst[:, c * P:(c + 1) * P], gv[:, c * P:(c + 1) * P], m.ident[:, :])
                    eng.transpose(psx[0:TS, 0:P], gv[:, TP:T], m.ident[:, :]).then_inc(s_t, 1)

                def u_columns(x):
                    h = i * 2 + x
                    eng.wait_ge(s_gu, h + 1)
                    project(eng, psu, w[:, x, 1], m.xT).then_inc(s_pu, 1)

                def spatial(x):
                    h = i * 2 + x
                    eng.wait_ge(s_vn, h + 1)
                    eng.wait_ge(s_ya, h + 1)
                    for c in range(NT):
                        eng.matmul(pss[:, c * P:(c + 1) * P], vn[:, c, :],
                                   m.wst[:, bass.ds(h, 1), :].rearrange("p a t -> p (a t)"), start=True, stop=True)
                    eng.transpose(psw[:, 0:TS], vn[0:TS, NT, :], m.ident[0:TS, 0:TS]).then_inc(s_sp, 1)

                turn_v(0)
                u_columns(0)
                v_columns(i, 1)
                spatial(0)
                turn_v(1)
                u_columns(1)
                v_columns(i + 1, 0)
                spatial(1)
            eng.wait_ge(s_yl, 16)
            eng.wait_ge(s_ya, NP + 1)
            for p in range(NP):
                last = eng.transpose(psw[:, p * TS:(p + 1) * TS], yt[:, p * P:(p + 1) * P], m.ident[0:TS, 0:TS])
            last.then_inc(s_yt, 1)

        @block.scalar
        def _(eng):
            eng.sem_inc(s_gv, 1)
            eng.sem_inc(s_gu, 1)

            def gelu_v(h):
                eng.wait_ge(s_pv, h + 1)
                eng.activation(split(gv[:, :]), halves(psv), ACT.Gelu_apprx_tanh).then_inc(s_gv, 1)

            gelu_v(0)
            with eng.Fori(0, NP // 2) as i:
                for x in range(2):
                    h = i * 2 + x
                    eng.wait_ge(s_pu, h + 1)
                    eng.wait_ge(s_ya, h + 1)
                    eng.activation(split(gu[:, :]), halves(psu), ACT.Gelu_apprx_tanh).then_inc(s_gu, 1)
                    gelu_v(h + 1)

        @block.vector
        def _(eng):
            eng.memset(mv[:, :, :], 1.0).then_inc(s_zero, 1)
            eng.wait_ge(s_zero, 1)
            eng.sem_inc(s_ve, 1)
            eng.sem_inc(s_ya, 1)
            eng.wait_ge(s_row, 48)
            with eng.Fori(0, NP // 2) as i:
                body = Steps(eng, s_step, i * GATING_STEPS)
                for x in range(2):
                    h = i * 2 + x
                    hs = bass.ds(h * P, P)
                    eng.wait_ge(s_t, h + 1)
                    for c in range(NT + 1):
                        n = P if c < NT else TS
                        src = pst[:, c * P:(c + 1) * P] if c < NT else psx[0:TS, 0:P]
                        body.did(eng.bn_stats(st[0:n, c, :], src))
                    body.wait()
                    eng.memset(pause[:, :], 0.0)
                    for c in range(NT + 1):
                        n = P if c < NT else TS
                        body.did(eng.bn_aggr(mv[0:n, c, :], st[0:n, c, :]))
                    body.wait()
                    eng.tensor_scalar(var[:, :], mv[:, :, 1], LN_EPS, None, ALU.add).then_inc(s_rs, 1)
                    eng.wait_ge(s_rs, h + 1)
                    rsqrt(eng, body, rstd[:, :], var[:, :], half[:, :])
                    for c in range(NT + 1):
                        n = P if c < NT else TS
                        src = pst[:, c * P:(c + 1) * P] if c < NT else psx[0:TS, 0:P]
                        ins = eng.tensor_scalar(vn[0:n, c, :], src, mv[0:n, c, 0:1], rstd[0:n, c:c + 1],
                                                ALU.subtract, ALU.mult)
                        if c < NT:
                            body.did(ins)
                    ins.then_inc(s_ve, 1)
                    eng.wait_ge(s_ve, h + 2)
                    body.wait()
                    body.did(eng.tensor_tensor(vn[:, 0:NT, :], vn[:, 0:NT, :],
                                               lnw[:, hs].unsqueeze(1).to_broadcast([P, NT, P]), ALU.mult))
                    body.did(eng.tensor_tensor(vn[0:TS, NT, :], vn[0:TS, NT, :], lnw[0:TS, hs], ALU.mult))
                    body.wait()
                    body.did(eng.tensor_tensor(vn[0:TS, NT, :], vn[0:TS, NT, :], lnb[0:TS, hs], ALU.add))
                    eng.tensor_tensor(vn[:, 0:NT, :], vn[:, 0:NT, :],
                                      lnb[:, hs].unsqueeze(1).to_broadcast([P, NT, P]), ALU.add).then_inc(s_vn, 1)
                    body.wait()
                    eng.tensor_copy(vns[:, hs], vn[0:TS, NT, :]).then_inc(s_vns, 1)
                    eng.wait_ge(s_sp, h + 1)
                    body.did(eng.tensor_tensor(gate[:, 0:TP].rearrange("p (c t) -> p c t", t=P),
                                               pss[:, :].rearrange("p (c t) -> p c t", t=P),
                                               sbias[:, hs].unsqueeze(1).to_broadcast([P, NT, P]), ALU.add))
                    body.did(eng.tensor_scalar(gate[:, TP:T], psw[:, 0:TS], m.w00[:, bass.ds(h, 1)],
                                               sbias[:, bass.ds(h * P, 1)], ALU.mult, ALU.add))
                    body.wait()
                    eng.wait_ge(s_gu, h + 2)
                    eng.tensor_tensor(m.ya[:, bass.ds(h, 1), :].rearrange("p a t -> p (a t)"), gate[:, :], gu[:, :],
                                      ALU.mult).then_inc(s_ya, 1)
                assert body.n == GATING_STEPS, body.n
            eng.wait_ge(s_yt, 1)
            eng.tensor_copy(m.r[:, :, TP:T], psw[:, 0:NP * TS].rearrange("p (n t) -> p n t", t=TS)).then_inc(s_rstep, 1)

        @block.gpsimd
        def _(eng):
            eng.wait_ge(m.s_sv, 16)
            eng.wait_ge(s_S, 16)
            step = Steps(eng, s_pool)
            full = [P, HD, HD]
            r, wd, k, v, aa, b = (m.sv[:, n, :] for n in range(6))
            over_i = lambda t: t.unsqueeze(1).to_broadcast(full)
            over_j = lambda t: t.unsqueeze(2).to_broadcast(full)

            def reduce_j(out):
                n = HD // 2
                while n:
                    dst = T1[:, :, 0:n] if n > 1 else out.unsqueeze(2)
                    step.did(eng.tensor_tensor(dst, T1[:, :, 0:n], T1[:, :, n:2 * n], ALU.add))
                    step.wait()
                    n //= 2

            step.did(eng.tensor_tensor(T1[:, :, :], m.S[:, :, :], over_i(aa), ALU.mult))
            step.wait()
            step.did(eng.tensor_tensor(m.S[:, :, :], m.S[:, :, :], over_i(wd), ALU.mult))
            reduce_j(sa[:, :])
            step.did(eng.tensor_tensor(T1[:, :, :], over_j(sa[:, :]), over_i(b), ALU.mult))
            step.wait()
            step.did(eng.tensor_tensor(m.S[:, :, :], m.S[:, :, :], T1[:, :, :], ALU.add))
            step.wait()
            step.did(eng.tensor_tensor(T1[:, :, :], over_j(v), over_i(k), ALU.mult))
            step.wait()
            step.did(eng.tensor_tensor(m.S[:, :, :], m.S[:, :, :], T1[:, :, :], ALU.add))
            step.wait()
            eng.sem_inc(s_sdone, 1)
            step.did(eng.tensor_tensor(T1[:, :, :], m.S[:, :, :], over_i(r), ALU.mult))
            step.wait()
            reduce_j(ys[:, :])
            eng.sem_inc(s_y, 1)


def load_merge(eng, m, a, slot, c):
    for n, src in enumerate((w_cols(a["w_in"], bass.ds(c * P + OFF_GA, P)), w_cols(a["w_in"], bass.ds(c * P + OFF_GB, P)),
                             w_cols(a["proj_a"], bass.ds(c * P, P)), w_cols(a["proj_b"], bass.ds(c * P, P)))):
        eng.dma_start(m.w_merge[:, slot, n], src).then_inc(m.s_merge[slot], 16)


def phase_head_norm(nc, m, a):
    ctx, sb, ps, sem = open_phase(nc)
    with ctx:
        gl = sb("hn_gl", [P, 2, P])
        sq = sb("hn_sq", [P, 2, T])
        psm = ps("hn_psm", [P, 2, 512])
        psq = ps("hn_psq", [P, 2, 512])
        psg = ps("hn_psg", [P, 2, 512])
        s_w = [sem("h_w0"), sem("h_w1")]
        (s_m, s_g, s_v, s_yc, s_sq, s_var, s_gate) = \
            (sem("h_" + n) for n in ("m", "g", "v", "yc", "sq", "var", "gate"))
        block = ctx.enter_context(nc.Block())

        @block.sync
        def _(eng):
            def load(slot, p):
                eng.dma_start(gl[:, slot, :], a["g_lora_up"][0, :, bass.ds(p * P, P)]).then_inc(s_w[slot], 16)

            for slot in range(2):
                load(slot, slot)
            for slot in range(2):
                load_merge(eng, m, a, slot, slot)
            with eng.Fori(1, NP // 2) as i:
                for slot in range(2):
                    eng.wait_ge(s_g, i * 2 + (slot - 1))
                    load(slot, i * 2 + slot)

        @block.tensor
        def _(eng):
            with eng.Fori(0, NP // 2) as i:
                for x in range(2):
                    p = i * 2 + x
                    y = m.r[:, bass.ds(p, 1), :].rearrange("p a t -> p (a t)")
                    eng.wait_ge(s_yc, p + 1)
                    for half in range(2):
                        last = eng.matmul(psm[:, half, 0:TH], m.headones[:, :], split(y)[:, half, :], start=True, stop=True)
                    last.then_inc(s_m, 1)
                for x in range(2):
                    p = i * 2 + x
                    eng.wait_ge(s_w[x], i * 16 + 16)
                    eng.wait_ge(s_gate, p + 1)
                    for half in range(2):
                        last = eng.matmul(psg[:, half, 0:TH], gl[:, x, :], m.gate_in[:, half * TH:(half + 1) * TH],
                                          start=True, stop=True)
                    last.then_inc(s_g, 1)
                    eng.wait_ge(s_sq, p + 1)
                    eng.wait_ge(s_var, p + 1)
                    for half in range(2):
                        last = eng.matmul(psq[:, half, 0:TH], m.headones[:, :], sq[:, x, half * TH:(half + 1) * TH],
                                          start=True, stop=True)
                    last.then_inc(s_v, 1)

        @block.scalar
        def _(eng):
            eng.sem_inc(s_gate, 1)
            with eng.Fori(0, NP // 2) as i:
                for x in range(2):
                    p = i * 2 + x
                    eng.wait_ge(s_yc, p + 2)
                    eng.activation(sq[:, x, :], m.yb[:, bass.ds(p, 1), :].rearrange("p a t -> p (a t)"), ACT.Square)\
                       .then_inc(s_sq, 1)
                    eng.wait_ge(s_g, p + 1)
                    eng.activation(split(m.og[:, bass.ds(p, 1), :].rearrange("p a t -> p (a t)")), halves(psg), ACT.Copy)\
                       .then_inc(s_gate, 1)

        @block.vector
        def _(eng):
            for s in (s_yc, s_var):
                eng.sem_inc(s, 1)
            with eng.Fori(0, NP // 2) as i:
                for x in range(2):
                    p = i * 2 + x
                    y = m.r[:, bass.ds(p, 1), :].rearrange("p a t -> p (a t)")
                    eng.wait_ge(s_m, p + 1)
                    eng.scalar_tensor_tensor(out=split(m.yb[:, bass.ds(p, 1), :].rearrange("p a t -> p (a t)")),
                                             in0=halves(psm), scalar=-1.0 / HD, in1=split(y),
                                             op0=ALU.mult, op1=ALU.add).then_inc(s_yc, 1)
                for x in range(2):
                    p = i * 2 + x
                    eng.wait_ge(s_v, p + 1)
                    eng.tensor_scalar(split(m.mg[:, bass.ds(p, 1), :].rearrange("p a t -> p (a t)")), halves(psq),
                                      HD * GN_EPS, None, ALU.add).then_inc(s_var, 1)


def phase_merge(nc, m, a):
    ctx, sb, ps, sem = open_phase(nc)
    with ctx:
        w = m.w_merge
        g = sb("mg_g", [P, 2, T])
        t = sb("mg_t", [P, 2, T])
        psn = [ps(f"mg_ps{n}", [P, 2, 512]) for n in range(4)]
        s_w = m.s_merge
        s_p = [sem(f"m_p{n}") for n in range(4)]
        s_g, s_t, s_mg, s_yb, s_step, s_ln, s_rs = (sem("m_" + n) for n in ("g", "t", "mg", "yb", "step", "ln", "rs"))
        block = ctx.enter_context(nc.Block())

        @block.sync
        def _(eng):
            eng.dma_start(m.w_out_lo, a["w_out"][0, 0:NK // 2 * P].rearrange("(k p) c -> p k c", p=P)).then_inc(m.s_w_out, 16)
            with eng.Fori(1, NP // 2) as i:
                for slot in range(2):
                    eng.wait_ge(s_p[3], i * 2 + (slot - 1))
                    load_merge(eng, m, a, slot, i * 2 + slot)

        @block.tensor
        def _(eng):
            with eng.Fori(0, NP // 2) as i:
                for x in range(2):
                    c = i * 2 + x
                    eng.wait_ge(s_w[x], i * 64 + 64)
                    for n, src in enumerate((m.xT, m.xT, m.ya, m.yb)):
                        if n < 2:
                            eng.wait_ge(s_g, c * 2 + n + 1)
                        else:
                            eng.wait_ge(s_t, c * 2 + n - 1)
                        if n == 3:
                            eng.wait_ge(s_yb, NP)
                        project(eng, psn[n], w[:, x, n], src).then_inc(s_p[n], 1)

        @block.scalar
        def _(eng):
            eng.sem_inc(s_g, 2)
            for h in range(2):
                pairs = slice(h * NP // 2, (h + 1) * NP // 2)
                eng.activation(m.mg[:, pairs, :], m.mg[:, pairs, :], ACT.Ln).then_inc(s_ln, 1)
            for h in range(2):
                pairs = slice(h * NP // 2, (h + 1) * NP // 2)
                eng.wait_ge(s_ln, h + 1)
                eng.activation(m.mg[:, pairs, :], m.mg[:, pairs, :], ACT.Exp, scale=-0.5).then_inc(s_rs, 1)
            with eng.Fori(0, NP // 2) as i:
                for x in range(2):
                    c = i * 2 + x
                    for n in range(2):
                        eng.wait_ge(s_p[n], c + 1)
                        eng.wait_ge(s_t, c * 2 + n + 1)
                        eng.activation(split(g[:, n, :]), halves(psn[n]), ACT.Sigmoid).then_inc(s_g, 1)

        @block.vector
        def _(eng):
            eng.sem_inc(s_t, 2)
            for h in range(2):
                eng.wait_ge(s_rs, h + 1)
                with eng.Fori(h * NP // 2, (h + 1) * NP // 2) as p:
                    def at(t):
                        return t[:, bass.ds(p, 1), :].rearrange("p a t -> p (a t)")

                    def col(name):
                        return m.vecs[:, bass.ds(p + VEC[name][0], 1)]

                    body = Steps(eng, s_step, p * 2)
                    body.did(eng.scalar_tensor_tensor(out=at(m.yb), in0=at(m.yb), scalar=math.sqrt(HD), in1=at(m.mg),
                                                      op0=ALU.mult, op1=ALU.mult))
                    body.wait()
                    body.did(eng.scalar_tensor_tensor(out=at(m.yb), in0=at(m.yb), scalar=col("lnx_w"), in1=at(m.bonus),
                                                      op0=ALU.mult, op1=ALU.add))
                    body.wait()
                    eng.scalar_tensor_tensor(out=at(m.yb), in0=at(m.yb), scalar=col("lnx_b"), in1=at(m.og),
                                             op0=ALU.add, op1=ALU.mult).then_inc(s_yb, 1)
            with eng.Fori(0, NP // 2) as i:
                for x in range(2):
                    c = i * 2 + x
                    for n in range(2):
                        eng.wait_ge(s_g, c * 2 + n + 3)
                        eng.wait_ge(s_p[2 + n], c + 1)
                        eng.tensor_tensor(split(t[:, n, :]), halves(psn[2 + n]), split(g[:, n, :]), ALU.mult).then_inc(s_t, 1)
                    eng.wait_ge(s_t, c * 2 + 4)
                    eng.tensor_tensor(m.mg[:, bass.ds(c, 1), :].rearrange("p a t -> p (a t)"), t[:, 0, :], t[:, 1, :],
                                      ALU.add).then_inc(s_mg, 1)
                    eng.wait_ge(s_mg, c + 1)


def load_gate_up(eng, m, a, x, expert):
    for n, src in enumerate((a["moe_w_gate"], a["moe_w_up"])):
        eng.dma_start(m.wgu[x][:, :, n * DE:(n + 1) * DE],
                      src[0, bass.ds(expert, 1)].rearrange("a (k p) f -> p (a k) f", p=P)).then_inc(m.s_gate_up[x], 16)


def load_down(eng, m, a, x, expert):
    eng.dma_start(m.wd[:, x], a["moe_w_down"][0, bass.ds(expert, 1)].rearrange("a (k p) c -> p (a k) c", p=P))\
       .then_inc(m.s_down[x], 16)


def phase_residual(nc, m, a):
    ctx, sb, ps, sem = open_phase(nc)
    with ctx:
        x2 = sb("rs_x2", [P, NT + 1, D])
        w_hi = sb("rs_w", [P, NK // 2, D])
        rt = sb("rs_rt", [P, NK, NG + NE])
        rb = sb("rs_rb", [P, NG + NE])
        gf = sb("rs_gf", [P, D])
        xn = sb("rs_xn", [P, 2, D])
        xnT = sb("rs_xnT", [P, NK, T])
        ms = sb("rs_ms", [P, NT + 1])
        rstd = sb("rs_rstd", [P, NT + 1])
        half = sb("rs_half", [P, NT + 1])
        fill = sb("rs_fill", [P, 2 * (ROUNDS + 1) * NE * CAP // P], I32)
        pso = [ps(f"rs_pso{n}", [P, 2, 512]) for n in range(2)]
        pst = ps("rs_pst", [P, 2, 512])
        psr = ps("rs_psr", [P, 512])
        s_x = [sem(f"o_in{j}") for j in range(NT + 1)]
        s_tok = [sem(f"o_tok{n}") for n in range(2)]
        (s_w, s_rt, s_o, s_x2, s_sq, s_ms, s_xn, s_t, s_te, s_r, s_lg, s_zero, s_fill, s_tab, s_step) = \
            (sem("o_" + n) for n in ("w", "rt", "o", "x2", "sq", "ms", "xn", "t", "te", "r", "lg",
                                     "zero", "fill", "tab", "step"))
        rows = [P] * NT + [TS]
        block = ctx.enter_context(nc.Block())

        @block.sync
        def _(eng):
            eng.dma_start(w_hi[:, :, :], a["w_out"][0, NK // 2 * P:D].rearrange("(k p) c -> p k c", p=P)).then_inc(s_w, 16)
            for j in range(NT):
                eng.dma_start(x2[:, j, :], a["x_prompt"][0, j * P:(j + 1) * P, :]).then_inc(s_x[j], 16)
            eng.dma_start(x2[0:TS, NT, :], a["x_sample"][:, 0, :]).then_inc(s_x[NT], 16)
            eng.dma_start(gf[:, :], a["norm_ffn_w"].partition_broadcast(P).rearrange("p l d -> p (l d)")).then_inc(s_rt, 16)
            eng.dma_start(rt[:, :, 0:NG], a["router_group"][0].rearrange("(k p) c -> p k c", p=P)).then_inc(s_rt, 16)
            eng.dma_start(rt[:, :, NG:NG + NE], a["router_expert"][0].rearrange("(k p) c -> p k c", p=P)).then_inc(s_rt, 16)
            eng.dma_start(rb[:, 0:NG], a["router_group_bias"].partition_broadcast(P).rearrange("p l d -> p (l d)"))\
               .then_inc(s_rt, 16)
            eng.dma_start(rb[:, NG:NG + NE], a["router_expert_bias"].partition_broadcast(P).rearrange("p l d -> p (l d)"))\
               .then_inc(s_rt, 16)
            for x in (0, 1, 3):
                load_gate_up(eng, m, a, x, x)
            for x in range(XG):
                load_down(eng, m, a, x, x)
            eng.wait_ge(s_fill, 1)
            eng.dma_start(m.d_table.rearrange("(p n) c -> p (n c)", p=P), fill[:, :]).then_inc(s_tab, 16)
            for j, n in enumerate(rows):
                eng.wait_ge(s_xn, j + 1)
                eng.dma_start(m.d_tok[j * P:j * P + n, :], xn[0:n, j % 2, :]).then_inc(s_tok[j % 2], 16)
            load_gate_up(eng, m, a, 2, 2)
            for j, n in enumerate(rows):
                eng.dma_start(m.d_x2[j * P:j * P + n, :], x2[0:n, j, :]).then_inc(s_tab, 16)
            eng.wait_ge(s_tab, 16 * (NT + 2))
            for n in range(2):
                eng.wait_ge(s_tok[n], 16 * ((NT + 2 - n) // 2))

        @block.gpsimd
        def _(eng):
            eng.memset(fill[:, :], NOBODY).then_inc(s_fill, 1)

        @block.tensor
        def _(eng):
            def out_rows(j, n):
                if j >= 2:
                    eng.wait_ge(s_x2, j - 1)
                for part, w in enumerate((m.w_out_lo, w_hi)):
                    if j == 0 and part == 1:
                        eng.wait_ge(s_w, 16)
                    for h in range(2):
                        for k in range(NK // 2):
                            last = eng.matmul(pso[j % 2][0:n, h, :], m.mg[:, part * NK // 2 + k, j * P:j * P + n],
                                              w[:, k, h * 512:(h + 1) * 512],
                                              start=(part == 0 and k == 0), stop=(part == 1 and k == NK // 2 - 1))
                last.then_inc(s_o, 1)

            def turn(j, n):
                eng.wait_ge(s_xn, j + 1)
                for h in range(2):
                    if j:
                        eng.wait_ge(s_te, 2 * (j - 1) + h + 1)
                    for k in range(4):
                        last = eng.transpose(pst[:, h, k * n:(k + 1) * n], xn[0:n, j % 2, (4 * h + k) * P:(4 * h + k + 1) * P],
                                             m.ident[0:n, 0:n])
                    last.then_inc(s_t, 1)

            eng.wait_ge(m.s_w_out, 16)
            for j, n in enumerate(rows):
                out_rows(j, n)
                if j:
                    turn(j - 1, P)
            turn(NT, TS)
            eng.wait_ge(s_rt, 80)
            for j, n in enumerate(rows):
                eng.wait_ge(s_te, 2 * j + 2)
                for k in range(NK):
                    last = eng.matmul(psr[0:n, j * (NG + NE):(j + 1) * (NG + NE)], xnT[:, k, j * P:j * P + n], rt[:, k, :],
                                      start=(k == 0), stop=(k == NK - 1))
            last.then_inc(s_r, 1)

        @block.scalar
        def _(eng):
            eng.wait_ge(s_zero, 1)
            for j, n in enumerate(rows):
                eng.wait_ge(s_x2, j + 1)
                if j >= 2:
                    eng.wait_ge(s_t, 2 * (j - 1))
                    eng.wait_ge(s_tok[j % 2], 16 * (j // 2))
                eng.activation(xn[0:n, j % 2, :], x2[0:n, j, :], ACT.Square, accum_out=ms[0:n, j:j + 1]).then_inc(s_sq, 1)

        @block.vector
        def _(eng):
            eng.memset(ms[:, :], 1.0)
            eng.memset(m.logits[:, :, :], 0.0).then_inc(s_zero, 1)
            step = Steps(eng, s_step)

            def add(j, n):
                eng.wait_ge(s_x[j], 16)
                eng.wait_ge(s_o, j + 1)
                row = x2[0:n, j, :].rearrange("p (h c) -> p h c", h=2)
                eng.tensor_tensor(row, pso[j % 2][0:n], row, ALU.add).then_inc(s_x2, 1)

            def evacuate(j, n):
                for h in range(2):
                    eng.wait_ge(s_t, 2 * j + h + 1)
                    eng.tensor_copy(xnT[:, 4 * h:4 * h + 4, j * P:j * P + n],
                                    pst[:, h, 0:4 * n].rearrange("p (k t) -> p k t", t=n)).then_inc(s_te, 1)

            eng.wait_ge(s_rt, 80)
            for j, n in enumerate(rows):
                add(j, n)
                eng.wait_ge(s_sq, j + 1)
                col = slice(j, j + 1)
                eng.tensor_scalar(ms[:, col], ms[:, col], 1.0 / D, RMS_EPS, ALU.mult, ALU.add).then_inc(s_ms, 1)
                eng.wait_ge(s_ms, j + 1)
                rsqrt(eng, step, rstd[:, col], ms[:, col], half[:, col])
                eng.scalar_tensor_tensor(out=xn[0:n, j % 2, :], in0=x2[0:n, j, :], scalar=rstd[0:n, j:j + 1],
                                         in1=gf[0:n, :], op0=ALU.mult, op1=ALU.mult).then_inc(s_xn, 1)
                if j:
                    evacuate(j - 1, P)
            evacuate(NT, TS)
            eng.wait_ge(s_r, 1)
            for j, n in enumerate(rows):
                eng.tensor_tensor(m.logits[0:n, j, :], psr[0:n, j * (NG + NE):(j + 1) * (NG + NE)], rb[0:n, :], ALU.add)\
                   .then_inc(s_lg, 1)


NOBODY = 1 << 20


def phase_route(nc, m, a):
    ctx, sb, ps, sem = open_phase(nc)
    NTT = NT + 1
    with ctx:
        mx = sb("ro_mx", [P, NTT])
        pr = sb("ro_pr", [P, EG])
        g_oh = sb("ro_goh", [P, NTT, NG])
        gx = sb("ro_gx", [P, NTT, NG])
        q = sb("ro_q", [P, NTT, EG])
        q4 = sb("ro_q4", [P, NTT, NG])
        pg = sb("ro_pg", [P, NTT])
        masked = sb("ro_masked", [P, NTT, NG, EG])
        le = sb("ro_le", [P, NTT, EG])
        e_oh = sb("ro_eoh", [P, 2, NTT, EG])
        top = sb("ro_top", [P, 2, NTT])
        oh = sb("ro_oh", [P, 2, NTT, NE])
        member = sb("ro_member", [P, NTT, NE])
        base = sb("ro_base", [P, NE])
        slot = sb("ro_slot", [P, NTT, NE])
        over = sb("ro_over", [P, NTT, NE])
        ssum = sb("ro_ssum", [P, 2, NTT])
        pos = sb("ro_pos", [P, 2, NTT], I32)
        value = sb("ro_value", [P, 2, NTT, 2], I32)
        cnt = sb("ro_cnt", [P, 2])
        psr = ps("ro_ps", [P, 512])
        psc = ps("ro_psc", [P, 512])
        (s_step, s_io, s_d, s_x, s_m, s_pc, s_val, s_pos, s_sc, s_e) = \
            (sem("g_" + n) for n in ("step", "io", "d", "x", "m", "pc", "val", "pos", "sc", "e"))
        rows = [P] * NT + [TS]
        block = ctx.enter_context(nc.Block())

        @block.gpsimd
        def _(eng):
            for n in range(EG):
                eng.memset(pr[:, n:n + 1], float(EG - n))
            eng.iota(base[:, :], [[CAP, NE]], base=0, channel_multiplier=0, allow_small_or_imprecise_dtypes=True).then_inc(s_io, 1)
            for c in range(2):
                for n in range(2):
                    eng.iota(value[:, c, :, n], [[P, NTT]], base=n * c * T, channel_multiplier=1).then_inc(s_val, 1)
            eng.wait_ge(s_pos, 1)
            eng.wait_ge(s_val, 4)
            for j, n in enumerate(rows):
                for c in range(2):
                    eng.indirect_dma_start(out=m.d_table, out_offset=bass.IndirectOffsetOnAxis(ap=pos[0:n, c, j:j + 1], axis=0),
                                           in_=value[0:n, c, j, :], in_offset=None).then_inc(s_sc, 16)
            eng.wait_ge(s_sc, 16 * 2 * NTT)

        @block.tensor
        def _(eng):
            eng.wait_ge(s_m, 1)
            for j, n in enumerate(rows):
                out = psr[0:n, j * NE:(j + 1) * NE]
                for i in range(j):
                    eng.matmul(out, m.ones[:, 0:n], member[:, i, :], start=(i == 0), stop=False)
                eng.matmul(out, m.below[0:n, 0:n], member[0:n, j, :], start=(j == 0), stop=True)
            for j, n in enumerate(rows):
                last = eng.matmul(psc[:, 0:NE], m.ones[0:n, :], member[0:n, j, :], start=(j == 0), stop=(j == NT))
            last.then_inc(s_pc, 1)

        @block.scalar
        def _(eng):
            eng.wait_ge(s_d, 1)
            eng.activation(gx[:, :, :], gx[:, :, :], ACT.Exp).then_inc(s_x, 1)
            eng.wait_ge(s_e, 1)
            eng.activation(top[:, 1, :], top[:, 1, :], ACT.Exp).then_inc(s_x, 1)

        @block.vector
        def _(eng):
            step = Steps(eng, s_step)

            def do(ins):
                step.did(ins)
                step.wait()

            def first_max(src, width, best, out, scratch):
                full = [P, NTT, width]
                do(eng.tensor_reduce(best, src, AX.X, ALU.max))
                do(eng.tensor_tensor(scratch, src, best.unsqueeze(2).to_broadcast(full), ALU.is_ge))
                do(eng.tensor_tensor(scratch, scratch, pr[:, EG - width:EG].unsqueeze(1).to_broadcast(full), ALU.mult))
                do(eng.tensor_reduce(mx[:, :], scratch, AX.X, ALU.max))
                do(eng.tensor_tensor(out, scratch, mx[:, :].unsqueeze(2).to_broadcast(full), ALU.is_equal))

            eng.wait_ge(s_io, 1)
            gl = m.logits[:, :, 0:NG]
            first_max(gl, NG, pg[:, :], g_oh[:, :, :], q4[:, :, :])
            eng.tensor_tensor(gx[:, :, :], gl, pg[:, :].unsqueeze(2).to_broadcast([P, NTT, NG]), ALU.subtract).then_inc(s_d, 1)
            experts = m.logits[:, :, NG:NG + NE].rearrange("p t (g e) -> p t g e", g=NG)
            for j in range(NTT):
                step.did(eng.tensor_tensor(masked[:, j], experts[:, j],
                                           g_oh[:, j, :].unsqueeze(2).to_broadcast([P, NG, EG]), ALU.mult))
            step.wait()
            for j in range(NTT):
                step.did(eng.tensor_reduce(le[:, j, :], masked[:, j].rearrange("p g e -> p e g"), AX.X, ALU.add))
            step.wait()
            first_max(le[:, :, :], EG, top[:, 0, :], e_oh[:, 0], q[:, :, :])
            do(eng.scalar_tensor_tensor(out=le[:, :, :], in0=e_oh[:, 0], scalar=-3e38, in1=le[:, :, :], op0=ALU.mult, op1=ALU.add))
            first_max(le[:, :, :], EG, top[:, 1, :], e_oh[:, 1], q[:, :, :])
            do(eng.tensor_tensor(top[:, 1, :], top[:, 1, :], top[:, 0, :], ALU.subtract))
            eng.sem_inc(s_e, 1)
            for c in range(2):
                for j in range(NTT):
                    step.did(eng.tensor_tensor(oh[:, c, j, :].rearrange("p (g e) -> p g e", g=NG),
                                               g_oh[:, j, :].unsqueeze(2).to_broadcast([P, NG, EG]),
                                               e_oh[:, c, j, :].unsqueeze(1).to_broadcast([P, NG, EG]), ALU.mult))
            step.wait()
            do(eng.tensor_tensor(member[:, :, :], oh[:, 0], oh[:, 1], ALU.add))
            eng.sem_inc(s_m, 1)
            eng.wait_ge(s_x, 2)
            do(eng.tensor_reduce(pg[:, :], gx[:, :, :], AX.X, ALU.add))
            do(eng.scalar_tensor_tensor(out=pg[:, :], in0=top[:, 1, :], scalar=1.0, in1=pg[:, :], op0=ALU.add, op1=ALU.mult))
            do(eng.reciprocal(m.weight[:, 0, :], pg[:, :]))
            do(eng.tensor_tensor(m.weight[:, 1, :], m.weight[:, 0, :], top[:, 1, :], ALU.mult))
            eng.wait_ge(s_pc, 1)
            rank = psr[:, 0:NTT * NE].rearrange("p (t e) -> p t e", e=NE)
            do(eng.memset(slot[:, :, :], 0.0))
            do(eng.tensor_copy(slot[:, 0:NT, :], rank[:, 0:NT, :]))
            do(eng.tensor_copy(slot[0:TS, NT, :], rank[0:TS, NT, :]))
            do(eng.tensor_scalar(over[:, :, :], slot[:, :, :], float(CAP), None, ALU.is_ge))
            for n in range(2, ROUNDS):
                do(eng.scalar_tensor_tensor(out=over[:, :, :], in0=slot[:, :, :], scalar=float(n * CAP), in1=over[:, :, :],
                                            op0=ALU.is_ge, op1=ALU.add))
            do(eng.scalar_tensor_tensor(out=slot[:, :, :], in0=over[:, :, :], scalar=float((NE - 1) * CAP), in1=slot[:, :, :],
                                        op0=ALU.mult, op1=ALU.add))
            do(eng.tensor_tensor(slot[:, :, :], slot[:, :, :], base[:, :].unsqueeze(1).to_broadcast([P, NTT, NE]), ALU.add))
            for c in range(2):
                do(eng.tensor_tensor(over[:, :, :], slot[:, :, :], oh[:, c], ALU.mult))
                do(eng.tensor_reduce(ssum[:, c, :], over[:, :, :], AX.X, ALU.add))
            do(eng.tensor_copy(pos[:, :, :], ssum[:, :, :]))
            eng.sem_inc(s_pos, 1)
            do(eng.tensor_reduce(cnt[:, 0:1], psc[:, 0:NE], AX.X, ALU.max))
            do(eng.memset(cnt[:, 1:2], float(NE // XG)))
            for n in range(1, ROUNDS):
                do(eng.tensor_scalar(mx[:, 0:1], cnt[:, 0:1], float(n * CAP), float(NE // XG), ALU.is_gt, ALU.mult))
                do(eng.tensor_tensor(cnt[:, 1:2], cnt[:, 1:2], mx[:, 0:1], ALU.add))
            do(eng.tensor_copy(m.passes[:, 0:1], cnt[:, 1:2]))
            do(eng.tensor_scalar(cnt[:, 1:2], cnt[:, 1:2], float(XG) / NE, None, ALU.mult))
            do(eng.tensor_copy(m.passes[:, 1:2], cnt[:, 1:2]))


XG = 4


def phase_experts(nc, m, a):
    ctx, sb, ps, sem = open_phase(nc)
    with ctx:
        idx = sb("ex_idx", [P, 2, XG, 2], I32)
        xg = sb("ex_xg", [P, XG, D])
        xgT = sb("ex_xgT", [P, 2, NK, P])
        sg = sb("ex_sg", [P, 2, DE])
        hT = sb("ex_hT", [P, 2, DE // P, P])
        yo = sb("ex_yo", [P, 2, D])
        pst = ps("ex_pst", [P, 2, 512])
        psg = [ps(f"ex_psg{n}", [P, 512]) for n in range(2)]
        psh = ps("ex_psh", [P, 512])
        psd = ps("ex_psd", [P, 2, 512])
        s_x = [sem(f"e_x{n}") for n in range(XG)]
        s_y = [sem(f"e_y{n}") for n in range(2)]
        (s_idx, s_t, s_te, s_gu, s_sg, s_h, s_ht, s_hte, s_d, s_ya, s_yb, s_xz, s_gate) = \
            (sem("e_" + n) for n in ("idx", "t", "te", "gu", "sg", "h", "ht", "hte", "d", "ya", "yb", "xz", "gate"))
        block = ctx.enter_context(nc.Block())

        def passes(eng):
            return eng.value_load(m.passes[0:1, 0:1], min_val=NE // XG, max_val=ROUNDS * NE // XG)

        @block.sync
        def _(eng):
            for j in range(NT + 1):
                r = P if j < NT else TS
                eng.dma_start(m.x2[0:r, j, :], m.d_x2[j * P:j * P + r, :]).then_inc(m.s_x2, 16)
            eng.dma_start(m.gain[:, :], a["norm_final_w"].partition_broadcast(P)).then_inc(m.s_x2, 16)
            n = passes(eng)
            with eng.Fori(1, n) as q:
                for x in range(XG):
                    e = (q % (NE // XG)) * XG + x
                    eng.wait_ge(s_gu, q * XG + (x + 1))
                    load_gate_up(eng, m, a, x, e)
                    eng.wait_ge(s_d, q * XG + (x + 1))
                    load_down(eng, m, a, x, e)

        @block.gpsimd
        def _(eng):
            def list_of(n, buf):
                eng.dma_start(idx[:, buf], m.d_table[bass.ds(n * (XG * CAP), XG * CAP), :].rearrange("(x s) c -> s x c", s=CAP))\
                   .then_inc(s_idx, 16)

            def gather(buf, x):
                eng.indirect_dma_start(out=xg[:, x, :], out_offset=None, in_=m.d_tok,
                                       in_offset=bass.IndirectOffsetOnAxis(ap=idx[:, buf, x, 0:1], axis=0),
                                       bounds_check=T - 1, oob_is_err=False).then_inc(s_x[x], 16)

            n = passes(eng)
            list_of(0, 0)
            eng.wait_ge(s_xz, 1)
            for x in range(2):
                eng.dma_start(yo[0:1, x, 0:P], m.ident[0:1, :]).then_inc(s_y[x], 16)
            eng.wait_ge(s_idx, 16)
            for x in range(XG):
                gather(0, x)
            with eng.Fori(0, n, 2) as q:
                for buf in range(2):
                    for x in range(2):
                        eng.wait_ge(s_y[x], q * (8 * XG) + (buf * 8 * XG + 16))
                    list_of(q + (buf + 1), 1 - buf)
                    for x in range(XG):
                        k = q * XG + (buf * XG + x)
                        eng.wait_ge(s_ya, k + 2)
                        eng.wait_ge(s_yb, k + 2)
                        eng.sem_inc(s_gate, 1)
                        eng.indirect_dma_start(out=m.d_y2, out_offset=bass.IndirectOffsetOnAxis(ap=idx[:, buf, x, 1:2], axis=0),
                                               in_=yo[:, x % 2, :], in_offset=None, bounds_check=2 * T - 1, oob_is_err=False)\
                           .then_inc(s_y[x % 2], 16)
                        if x == 0:
                            eng.wait_ge(s_idx, q * 16 + (buf + 2) * 16)
                            eng.sem_inc(s_gate, 1)
                        gather(1 - buf, x)
            for x in range(XG):
                eng.wait_ge(s_x[x], n * 16 + 16)
            for x in range(2):
                eng.wait_ge(s_y[x], n * (8 * XG) + 16)

        @block.tensor
        def _(eng):
            eng.sem_inc(s_gu, XG)
            eng.sem_inc(s_d, XG)
            n = passes(eng)

            def turn(q, x):
                eng.wait_ge(s_x[x], q * 16 + 16)
                eng.wait_ge(s_te, (q * XG + x) * 2 + 2)
                for kk in range(NK):
                    last = eng.transpose(pst[:, kk // 4, (kk % 4) * P:(kk % 4 + 1) * P], xg[:, x, kk * P:(kk + 1) * P],
                                         m.ident[:, :])
                last.then_inc(s_t, 1)

            turn(0, 0)
            with eng.Fori(0, n) as q:
                def gate_up(x):
                    k = q * XG + x
                    eng.wait_ge(s_te, k * 2 + 4)
                    eng.wait_ge(m.s_gate_up[x], q * 32 + 32)
                    eng.wait_ge(s_h, k + 1)
                    for kk in range(NK):
                        last = eng.matmul(psg[x % 2][:, :], xgT[:, x % 2, kk, :], m.wgu[x][:, kk, :],
                                          start=(kk == 0), stop=(kk == NK - 1))
                    last.then_inc(s_gu, 1)

                def turn_h(x):
                    k = q * XG + x
                    eng.wait_ge(s_h, k + 3)
                    eng.wait_ge(s_hte, k + 1)
                    for kk in range(DE // P):
                        last = eng.transpose(psh[:, kk * P:(kk + 1) * P], sg[:, x % 2, kk * P:(kk + 1) * P], m.ident[:, :])
                    last.then_inc(s_ht, 1)

                def down(x):
                    k = q * XG + x
                    eng.wait_ge(s_hte, k + 2)
                    eng.wait_ge(m.s_down[x], q * 16 + 16)
                    eng.wait_ge(s_ya, k + 1)
                    eng.wait_ge(s_yb, k + 1)
                    for h in range(2):
                        for kk in range(DE // P):
                            last = eng.matmul(psd[:, h, :], hT[:, x % 2, kk, :], m.wd[:, x, kk, h * 512:(h + 1) * 512],
                                              start=(kk == 0), stop=(kk == DE // P - 1))
                    last.then_inc(s_d, 1)

                for x in range(XG):
                    gate_up(x)
                    if x < XG - 1:
                        turn(q, x + 1)
                    if x:
                        down(x - 1)
                    turn_h(x)
                turn(q + 1, 0)
                down(XG - 1)

        @block.scalar
        def _(eng):
            eng.sem_inc(s_te, 1)
            eng.sem_inc(s_hte, 1)
            eng.sem_inc(s_ya, 1)
            n = passes(eng)

            def rows(q, x):
                eng.wait_ge(s_t, q * XG + (x + 1))
                eng.activation(xgT[:, x % 2, 0:4, :], pst[:, 0, :].rearrange("p (k s) -> p k s", s=P), ACT.Copy).then_inc(s_te, 1)

            rows(0, 0)
            with eng.Fori(0, n) as q:
                def out(x):
                    k = q * XG + x
                    eng.wait_ge(s_d, k + (XG + 1))
                    eng.wait_ge(s_y[x % 2], q * (8 * XG) + (x // 2 + 1) * 16)
                    eng.activation(yo[:, x % 2, 0:512], psd[:, 0, :], ACT.Copy).then_inc(s_ya, 1)

                for x in range(XG):
                    k = q * XG + x
                    eng.wait_ge(s_gu, k + (XG + 1))
                    eng.activation(sg[:, x % 2, :], psg[x % 2][:, 0:DE], ACT.Silu).then_inc(s_sg, 1)
                    if x < XG - 1:
                        rows(q, x + 1)
                    if x:
                        out(x - 1)
                    eng.wait_ge(s_ht, k + 1)
                    eng.activation(hT[:, x % 2], psh[:, 0:DE].rearrange("p (k s) -> p k s", s=P), ACT.Copy).then_inc(s_hte, 1)
                rows(q + 1, 0)
                out(XG - 1)

        @block.vector
        def _(eng):
            eng.sem_inc(s_te, 1)
            eng.sem_inc(s_h, 2)
            eng.sem_inc(s_yb, 1)
            eng.memset(xg[:, :, :], 0.0).then_inc(s_xz, 1)
            n = passes(eng)

            def rows(q, x):
                eng.wait_ge(s_t, q * XG + (x + 1))
                eng.tensor_copy(xgT[:, x % 2, 4:8, :], pst[:, 1, :].rearrange("p (k s) -> p k s", s=P)).then_inc(s_te, 1)

            rows(0, 0)
            with eng.Fori(0, n) as q:
                def out(x):
                    k = q * XG + x
                    eng.wait_ge(s_d, k + (XG + 1))
                    eng.wait_ge(s_y[x % 2], q * (8 * XG) + (x // 2 + 1) * 16)
                    eng.tensor_copy(yo[:, x % 2, 512:D], psd[:, 1, :]).then_inc(s_yb, 1)

                for x in range(XG):
                    eng.wait_ge(s_sg, q * XG + (x + 1))
                    eng.tensor_tensor(sg[:, x % 2, :], psg[x % 2][:, DE:2 * DE], sg[:, x % 2, :], ALU.mult).then_inc(s_h, 1)
                    if x < XG - 1:
                        rows(q, x + 1)
                    if x:
                        out(x - 1)
                rows(q + 1, 0)
                out(XG - 1)


def phase_final(nc, m, a):
    ctx, sb, ps, sem = open_phase(nc)
    with ctx:
        x2 = m.x2
        y = sb("fi_y", [P, NT + 1, 2, D])
        gf = m.gain
        ms = sb("fi_ms", [P, NT + 1])
        rstd = sb("fi_rstd", [P, NT + 1])
        half = sb("fi_half", [P, NT + 1])
        sq = sb("fi_sq", [P, 2, D])
        s_y = [sem(f"f_y{j}") for j in range(NT + 1)]
        s_x, s_sq, s_ms, s_rs, s_o, s_out, s_zero, s_step = \
            (sem("f_" + n) for n in ("x", "sq", "ms", "rs", "o", "out", "zero", "step"))
        rows = [P] * NT + [TS]
        block = ctx.enter_context(nc.Block())

        @block.sync
        def _(eng):
            for j, n in enumerate(rows):
                eng.dma_start(y[0:n, j], m.d_y2.rearrange("(c t) d -> t c d", c=2)[j * P:j * P + n]).then_inc(s_y[j], 16)
            for j, n in enumerate(rows):
                eng.wait_ge(s_o, j + 1)
                dst = a["y_prompt"][0, j * P:(j + 1) * P, :] if j < NT else a["y_sample"][:, 0, :]
                eng.dma_start(dst, x2[0:n, j, :]).then_inc(s_out, 16)
            eng.wait_ge(s_out, 16 * (NT + 1))

        @block.vector
        def _(eng):
            step = Steps(eng, s_step)
            eng.memset(ms[:, :], 1.0).then_inc(s_zero, 1)
            eng.wait_ge(m.s_x2, 16 * (NT + 2))
            for j, n in enumerate(rows):
                eng.wait_ge(s_y[j], 16)
                step.did(eng.scalar_tensor_tensor(out=x2[0:n, j, :], in0=y[0:n, j, 0, :], scalar=m.weight[0:n, 0, j:j + 1],
                                                  in1=x2[0:n, j, :], op0=ALU.mult, op1=ALU.add))
                step.wait()
                eng.scalar_tensor_tensor(out=x2[0:n, j, :], in0=y[0:n, j, 1, :], scalar=m.weight[0:n, 1, j:j + 1],
                                         in1=x2[0:n, j, :], op0=ALU.mult, op1=ALU.add).then_inc(s_x, 1)
            eng.wait_ge(s_sq, NT + 1)
            eng.tensor_scalar(ms[:, :], ms[:, :], 1.0 / D, RMS_EPS, ALU.mult, ALU.add).then_inc(s_ms, 1)
            eng.wait_ge(s_ms, 1)
            rsqrt(eng, Steps(eng, s_rs), rstd[:, :], ms[:, :], half[:, :])
            for j, n in enumerate(rows):
                eng.scalar_tensor_tensor(out=x2[0:n, j, :], in0=x2[0:n, j, :], scalar=rstd[0:n, j:j + 1], in1=gf[0:n, :],
                                         op0=ALU.mult, op1=ALU.mult).then_inc(s_o, 1)

        @block.scalar
        def _(eng):
            eng.wait_ge(s_zero, 1)
            for j, n in enumerate(rows):
                eng.wait_ge(s_x, j + 1)
                if j >= 2:
                    eng.wait_ge(s_sq, j - 1)
                eng.activation(sq[0:n, j % 2, :], x2[0:n, j, :], ACT.Square, accum_out=ms[0:n, j:j + 1]).then_inc(s_sq, 1)


INPUTS = ('x_prompt', 'x_sample', 'state_wkv', 'state_shift', 'norm_mix_w', 'w_in', 'sgu_ln_w', 'sgu_ln_b', 'sgu_w_s',
          'sgu_b', 'rwkv_mu', 'w_lora_up', 'w_bias', 'a_lora_up', 'a_bias', 'g_lora_up', 'k_k', 'k_a', 'r_k', 'lnx_w',
          'lnx_b', 'proj_a', 'proj_b', 'w_out', 'norm_ffn_w', 'router_group', 'router_group_bias', 'router_expert',
          'router_expert_bias', 'moe_w_gate', 'moe_w_up', 'moe_w_down', 'norm_final_w')
OUTPUTS = (("y_prompt", (1, TP, D)), ("y_sample", (TS, 1, D)), ("new_wkv_prompt", (1, 1, 2 * NP, HD, HD)),
           ("new_shift_prompt", (1, 1, SHIFT)), ("new_wkv_sample", (1, TS, 2 * NP, HD, HD)),
           ("new_shift_sample", (1, TS, SHIFT)), ("new_chunk_v_sample", (1, TS, 1, NP, P)))


class Memory:
    pass


def build(nc, a):
    m = Memory()
    m.flat = {name: a[name].rearrange("l h d -> (l h d)" if name in ("r_k", "lnx_w", "lnx_b") else "l d -> (l d)")
              for name in VEC_NAMES}
    m.d_sample = nc.dram_tensor("d_sample", (6, TS, D), F32, kind="Internal").ap()
    m.d_y = nc.dram_tensor("d_y", (TS, D), F32, kind="Internal").ap()
    m.d_tok = nc.dram_tensor("d_tok", (T, D), F32, kind="Internal").ap()
    m.d_x2 = nc.dram_tensor("d_x2", (T, D), F32, kind="Internal").ap()
    m.d_table = nc.dram_tensor("d_table", ((ROUNDS + 1) * NE * CAP, 2), I32, kind="Internal").ap()
    m.d_y2 = nc.dram_tensor("d_y2", (2 * T, D), F32, kind="Internal").ap()

    def scope():
        ctx = ExitStack()
        return ctx, lambda name, shape, dt=F32: ctx.enter_context(nc.sbuf_tensor(name, shape, dt))

    whole, sb = scope()
    with whole:
        m.s_sv = whole.enter_context(nc.semaphore("s_sv"))
        m.s_merge = [whole.enter_context(nc.semaphore(f"s_merge{x}")) for x in range(2)]
        m.s_x2 = whole.enter_context(nc.semaphore("s_x2"))
        m.s_w_out = whole.enter_context(nc.semaphore("s_w_out"))
        m.s_gate_up = [whole.enter_context(nc.semaphore(f"s_gate_up{x}")) for x in range(XG)]
        m.s_down = [whole.enter_context(nc.semaphore(f"s_down{x}")) for x in range(XG)]
        m.ident, m.headones, m.causal, m.below, m.ones, m.level1t = \
            (sb(n, [P, P]) for n in ("ident", "headones", "causal", "below", "ones", "level1t"))
        m.levels = sb("levels", [P, 1 + len(LEVELS), P])
        m.vecs = sb("vecs", [P, NVEC])
        m.shift_prev = sb("shift_prev", [P, NSH, TS])
        m.shift_last = sb("shift_last", [P, TS + 1, NSH])
        m.half_bias = sb("half_bias", [P, 2, NP])
        m.lw_sample = sb("lw_sample", [P, NP, TS])
        m.logits = sb("logits", [P, NT + 1, NG + NE])
        m.weight = sb("weight", [P, 2, NT + 1])
        m.passes = sb("passes", [P, 2], I32)
        mixer, sb = scope()
        with mixer:
            m.lora_in = sb("lora_in", [P, T])
            m.gate_in = sb("gate_in", [P, T])
            m.sv = sb("sv", [P, 6, HD])
            m.wst = sb("wst", [P, NP, P])
            m.w00 = sb("w00", [P, NP])
            wide = [sb(n, [P, NK * T]) for n in ("xT", "bonus_all", "r_all")]
            m.xT, m.bonus, m.r = (t.rearrange("p (k t) -> p k t", t=T) for t in wide)
            m.w_out_lo = wide[2][:, 0:NK // 2 * D].rearrange("p (k c) -> p k c", c=D)
            m.wgu = [t[:, 0:NK * 2 * DE].rearrange("p (k f) -> p k f", f=2 * DE) for t in wide]
            rwkv, sb = scope()
            with rwkv:
                m.k, m.kk, m.br, m.v = (sb(n + "_all", [P, NP, T]) for n in ("k", "kk", "br", "v"))
                m.cum = sb("cum_all", [P, NP, NC * (CH + 1)])
                phase_tokens(nc, m, a)
                phase_lora_inputs(nc, m, a)
                phase_rkv(nc, m, a)
                phase_chunks(nc, m, a)
                phase_sample_vectors(nc, m, a)
            late, sb = scope()
            with late:
                m.mg = sb("mg", [P, NP, T])
                branches, sb = scope()
                m.ya = sb("ya", [P, NP, T])
                state, sb = scope()
                with state:
                    m.S = sb("S", [P, HD, HD])
                    phase_gating(nc, m, a)
                m.yb, m.og = (branches.enter_context(nc.sbuf_tensor(n, [P, NP, T], F32)) for n in ("yb", "og"))
                m.w_merge = branches.enter_context(nc.sbuf_tensor("w_merge", [P, 2, 4, NK, P], F32))
                phase_head_norm(nc, m, a)
                phase_merge(nc, m, a)
                branches.close()
                m.wd = late.enter_context(nc.sbuf_tensor("wd", [P, XG, DE // P, D], F32))
                m.wgu.append(late.enter_context(nc.sbuf_tensor("wgu_last", [P, NK, 2 * DE], F32)))
                phase_residual(nc, m, a)
                phase_route(nc, m, a)
                m.x2 = late.enter_context(nc.sbuf_tensor("x2", [P, NT + 1, D], F32))
                m.gain = late.enter_context(nc.sbuf_tensor("gain", [P, D], F32))
                phase_experts(nc, m, a)
                phase_final(nc, m, a)


def kernel(**inputs):
    import numpy as _np
    import concourse.bacc as _bacc
    from concourse.bass_utils import run_bass_kernel_spmd as _run

    nc = _bacc.Bacc("TRN2", target_bir_lowering=False, num_devices=1)
    arrays, a = {}, {}
    for name in INPUTS:
        arrays[f"in_{name}"] = _np.ascontiguousarray(inputs[name])
        a[name] = nc.dram_tensor(f"in_{name}", arrays[f"in_{name}"].shape, F32, kind="ExternalInput").ap()
    for name, shape in OUTPUTS:
        a[name] = nc.dram_tensor(f"out_{name}", shape, F32, kind="ExternalOutput").ap()
    build(nc, a)
    r = _run(nc, [arrays], core_ids=[0])
    return tuple(r.results[0][f"out_{name}"] for name, _ in OUTPUTS)
```
